# Optimizing a Trainium2 kernel written in Bass

```python
import functools
import jax, jax.numpy as jnp
from jax import lax
import numpy as np

D_MODEL = 1024
BATCH = 1
SEQ = 1024
DEPTH = 1
DEC_BATCH = 8
DEC_SEQ = 4
PAST_LEN = 1024
PAGE_SIZE = 128

N_HEADS = 8
HEAD_DIM = 64
KV_HEADS = 4
ATT_WIDTH = N_HEADS * HEAD_DIM
IDX_HEADS = 8
IDX_DIM = 64
TOPK_MAX = 256
Q_BLOCK = 128
HG_HEADS = 4
HG_KDIM = 128
HG_VDIM = 128
HG_KWIDTH = HG_HEADS * HG_KDIM
HG_VWIDTH = HG_HEADS * HG_VDIM
HG_CHUNK = 64
D_FF = 2816
ROPE_THETA = 10000.0
NORM_EPS = 1e-6

_SEGMENTS = (ATT_WIDTH, KV_HEADS * HEAD_DIM, KV_HEADS * HEAD_DIM,
             IDX_HEADS * IDX_DIM, IDX_DIM, IDX_HEADS,
             HG_KWIDTH, HG_KWIDTH, HG_VWIDTH, HG_VWIDTH,
             D_MODEL, D_MODEL)
IN_COLS = sum(_SEGMENTS)

kernel_name = 'hybrid_dsa_hgrn2_macaron_step'

F32 = jnp.float32

def _split_cols(p):
    out, start = [], 0
    for width in _SEGMENTS:
        out.append(p[..., start:start + width])
        start += width
    return out

def _rms_norm(x, g):
    xf = x.astype(F32)
    y = xf * lax.rsqrt(jnp.mean(xf * xf, axis=-1, keepdims=True) + NORM_EPS)
    return (y * g.astype(F32)).astype(x.dtype)

def _rope(x, pos):
    d = x.shape[-1]
    half = d // 2
    inv = ROPE_THETA ** (-jnp.arange(half, dtype=F32) * 2.0 / d)
    ang = pos.astype(F32)[:, None] * inv[None, :]
    cos = jnp.cos(ang)[None, :, None, :]
    sin = jnp.sin(ang)[None, :, None, :]
    xf = x.astype(F32)
    x1, x2 = xf[..., :half], xf[..., half:]
    return jnp.concatenate([x1 * cos - x2 * sin, x2 * cos + x1 * sin], axis=-1).astype(x.dtype)

def _swiglu(x, w_gate, w_up, w_down):
    return (jax.nn.silu(x @ w_gate) * (x @ w_up)) @ w_down

def _idx_scores(qi, wi, ki):
    s = jnp.einsum('bthd,bsd->bths', qi.astype(F32), ki.astype(F32)) * (IDX_DIM ** -0.5)
    return jnp.einsum('bths,bth->bts', jax.nn.relu(s), wi.astype(F32))

def _gather_rows(rows, idx):
    return jax.vmap(lambda r, i: r[i])(rows, idx)

def _sparse_attend(q, ks, vs, valid):
    b, t, h, d = q.shape
    qg = q.reshape(b, t, KV_HEADS, h // KV_HEADS, d)
    logits = jnp.einsum('btgrd,btkgd->btgrk', qg, ks).astype(F32) * (d ** -0.5)
    logits = jnp.where(valid[:, :, None, None, :], logits, -jnp.inf)
    p = jax.nn.softmax(logits, axis=-1).astype(vs.dtype)
    o = jnp.einsum('btgrk,btkgd->btgrd', p, vs)
    return o.reshape(b, t, h * d).astype(q.dtype)

def _dsa_prompt(q, k, v, qi, ki, wi):
    b, t, h, d = q.shape
    topk = min(TOPK_MAX, t // 4)
    nb = t // Q_BLOCK
    key_pos = jnp.arange(t)

    def blocks(a):
        return a.reshape((b, nb, Q_BLOCK) + a.shape[2:]).swapaxes(0, 1)

    def one_block(args):
        qb, qib, wib, pb = args
        sc = _idx_scores(qib, wib, ki)
        sc = jnp.where(key_pos[None, None, :] <= pb[None, :, None], sc, -jnp.inf)
        _, sel = lax.top_k(sc, topk)
        valid = sel <= pb[None, :, None]
        return _sparse_attend(qb, _gather_rows(k, sel), _gather_rows(v, sel), valid)

    out = lax.map(one_block, (blocks(q), blocks(qi), blocks(wi), key_pos.reshape(nb, Q_BLOCK)))
    return out.swapaxes(0, 1).reshape(b, t, h * d)

def _dsa_sample(q, k, v, qi, ki, wi, *, layer, cache_k, cache_v, cache_ik, page_table):
    db, tn = q.shape[:2]
    n_pages = page_table.shape[1]
    ps = cache_k.shape[2]
    past = n_pages * ps
    total = past + tn
    topk = min(TOPK_MAX, total // 4)
    ki_past = cache_ik[layer, page_table].reshape(db, past, IDX_DIM)
    ki_all = jnp.concatenate([ki_past.astype(ki.dtype), ki], axis=1)
    qpos = past + jnp.arange(tn)
    sc = _idx_scores(qi, wi, ki_all)
    sc = jnp.where(jnp.arange(total)[None, None, :] <= qpos[None, :, None], sc, -jnp.inf)
    _, sel = lax.top_k(sc, topk)
    valid = sel <= qpos[None, :, None]
    from_past = (sel < past)[..., None, None]
    sp = jnp.minimum(sel, past - 1)
    phys = jax.vmap(lambda pt, i: pt[i])(page_table, sp // ps)
    slot = sp % ps
    ns = jnp.clip(sel - past, 0, tn - 1)
    ks = jnp.where(from_past, cache_k[layer, phys, slot].astype(k.dtype), _gather_rows(k, ns))
    vs = jnp.where(from_past, cache_v[layer, phys, slot].astype(v.dtype), _gather_rows(v, ns))
    return _sparse_attend(q, ks, vs, valid)

def _gla_recurrence(q, k, v, logf, s0):
    b, t, h, kd = q.shape
    vd = v.shape[-1]
    c = HG_CHUNK if t % HG_CHUNK == 0 else t
    n = t // c

    def to_chunks(a):
        return a.astype(F32).reshape(b, n, c, h, a.shape[-1]).transpose(1, 0, 3, 2, 4)

    causal = jnp.tril(jnp.ones((c, c), dtype=bool))

    def step(S, inp):
        qc, kc, vc, gc = inp
        G = jnp.cumsum(gc, axis=2)
        o_inter = jnp.einsum('bhtk,bhkv->bhtv', qc * jnp.exp(G), S)
        diff = G[:, :, :, None, :] - G[:, :, None, :, :]
        decay = jnp.exp(jnp.where(causal[:, :, None], diff, -jnp.inf))
        A = jnp.einsum('bhtsk,bhsk->bhts', qc[:, :, :, None, :] * decay, kc)
        o = o_inter + jnp.einsum('bhts,bhsv->bhtv', A, vc)
        G_last = G[:, :, -1:, :]
        S = jnp.exp(G_last[:, :, 0, :])[..., None] * S + jnp.einsum('bhsk,bhsv->bhkv', kc * jnp.exp(G_last - G), vc)
        return S, o

    S, o = lax.scan(step, s0.astype(F32), (to_chunks(q), to_chunks(k), to_chunks(v), to_chunks(logf)))
    o = o.transpose(1, 0, 3, 2, 4).reshape(b, t, h, vd)
    return o, S

def _hgrn2_branch(hq, hf, hi, hg, lb, s0, hg_norm):
    b, t, _ = hq.shape
    q = jax.nn.silu(hq.astype(F32)).reshape(b, t, HG_HEADS, HG_KDIM) * (HG_KDIM ** -0.5)
    z = hf.astype(F32).reshape(b, t, HG_HEADS, HG_KDIM)
    lbh = lb.reshape(HG_HEADS, HG_KDIM)
    f = lbh + (1.0 - lbh) * jax.nn.sigmoid(z)
    k = (1.0 - lbh) * jax.nn.sigmoid(-z)
    v = hi.astype(F32).reshape(b, t, HG_HEADS, HG_VDIM)
    o, S = _gla_recurrence(q, k, v, jnp.log(f), s0)
    o = _rms_norm(o, hg_norm) * jax.nn.silu(hg.astype(F32).reshape(b, t, HG_HEADS, HG_VDIM))
    return o.reshape(b, t, HG_VWIDTH).astype(hq.dtype), S

def _layer(x, pos, attend, s0, lb, ffn1_norm, ffn1_w_gate, ffn1_w_up, ffn1_w_down, mix_norm, w_in,
           q_norm, k_norm, hg_norm, w_branch_attn, w_branch_hgrn, w_out,
           ffn2_norm, ffn2_w_gate, ffn2_w_up, ffn2_w_down):
    b, t, _ = x.shape
    x = x + 0.5 * _swiglu(_rms_norm(x, ffn1_norm), ffn1_w_gate, ffn1_w_up, ffn1_w_down)
    h = _rms_norm(x, mix_norm)
    q, k, v, qi, ki, wi, hq, hf, hi, hg, ga, gr = _split_cols(h @ w_in)
    q = _rope(_rms_norm(q.reshape(b, t, N_HEADS, HEAD_DIM), q_norm), pos)
    k = _rope(_rms_norm(k.reshape(b, t, KV_HEADS, HEAD_DIM), k_norm), pos)
    v = v.reshape(b, t, KV_HEADS, HEAD_DIM)
    qi = _rope(qi.reshape(b, t, IDX_HEADS, IDX_DIM), pos)
    ki = _rope(ki.reshape(b, t, 1, IDX_DIM), pos)[:, :, 0]
    wi = wi * (IDX_HEADS ** -0.5)
    att = attend(q, k, v, qi, ki, wi)
    rec, S = _hgrn2_branch(hq, hf, hi, hg, lb, s0, hg_norm)
    merged = jax.nn.sigmoid(ga) * (att @ w_branch_attn) + jax.nn.sigmoid(gr) * (rec @ w_branch_hgrn)
    x = x + merged @ w_out
    x = x + 0.5 * _swiglu(_rms_norm(x, ffn2_norm), ffn2_w_gate, ffn2_w_up, ffn2_w_down)
    return x, k, v, ki, S

def setup_inputs(seed: int = 0) -> dict:
    key = jax.random.key(seed)
    ks = jax.random.split(key, 26)
    n_pages = PAST_LEN // PAGE_SIZE
    n_used = DEC_BATCH * n_pages
    n_pool = n_used + max(1, n_used // 4)

    def nrm(k, shape, scale):
        return jax.random.normal(k, shape, F32) * scale

    def gain(k, shape):
        return 1.0 + 0.02 * jax.random.normal(k, shape, F32)

    page_table = jax.random.permutation(ks[6], n_pool)[:n_used].reshape(DEC_BATCH, n_pages).astype(jnp.int32)
    return {
        'x_prompt': nrm(ks[0], (BATCH, SEQ, D_MODEL), 1.0),
        'x_sample': nrm(ks[1], (DEC_BATCH, DEC_SEQ, D_MODEL), 1.0),
        'cache_k': nrm(ks[2], (DEPTH, n_pool, PAGE_SIZE, KV_HEADS, HEAD_DIM), 1.0),
        'cache_v': nrm(ks[3], (DEPTH, n_pool, PAGE_SIZE, KV_HEADS, HEAD_DIM), 1.0),
        'cache_idx_k': nrm(ks[4], (DEPTH, n_pool, PAGE_SIZE, IDX_DIM), 1.0),
        'state_hgrn': nrm(ks[5], (DEPTH, DEC_BATCH, HG_HEADS, HG_KDIM, HG_VDIM), 0.5),
        'page_table': page_table,
        'hg_lower_bound': nrm(ks[7], (DEPTH + 1, HG_KWIDTH), 0.1),
        'ffn1_norm': gain(ks[8], (DEPTH, D_MODEL)),
        'ffn1_w_gate': nrm(ks[9], (DEPTH, D_MODEL, D_FF), D_MODEL ** -0.5),
        'ffn1_w_up': nrm(ks[10], (DEPTH, D_MODEL, D_FF), D_MODEL ** -0.5),
        'ffn1_w_down': nrm(ks[11], (DEPTH, D_FF, D_MODEL), D_FF ** -0.5),
        'mix_norm': gain(ks[12], (DEPTH, D_MODEL)),
        'w_in': nrm(ks[13], (DEPTH, D_MODEL, IN_COLS), D_MODEL ** -0.5),
        'q_norm': gain(ks[14], (DEPTH, HEAD_DIM)),
        'k_norm': gain(ks[15], (DEPTH, HEAD_DIM)),
        'hg_norm': gain(ks[16], (DEPTH, HG_VDIM)),
        'w_branch_attn': nrm(ks[17], (DEPTH, ATT_WIDTH, D_MODEL), ATT_WIDTH ** -0.5),
        'w_branch_hgrn': nrm(ks[18], (DEPTH, HG_VWIDTH, D_MODEL), HG_VWIDTH ** -0.5),
        'w_out': nrm(ks[19], (DEPTH, D_MODEL, D_MODEL), D_MODEL ** -0.5),
        'ffn2_norm': gain(ks[20], (DEPTH, D_MODEL)),
        'ffn2_w_gate': nrm(ks[21], (DEPTH, D_MODEL, D_FF), D_MODEL ** -0.5),
        'ffn2_w_up': nrm(ks[22], (DEPTH, D_MODEL, D_FF), D_MODEL ** -0.5),
        'ffn2_w_down': nrm(ks[23], (DEPTH, D_FF, D_MODEL), D_FF ** -0.5),
    }

def reference(x_prompt, x_sample, cache_k, cache_v, cache_idx_k, state_hgrn, page_table, hg_lower_bound,
              ffn1_norm, ffn1_w_gate, ffn1_w_up, ffn1_w_down, mix_norm, w_in, q_norm, k_norm, hg_norm,
              w_branch_attn, w_branch_hgrn, w_out, ffn2_norm, ffn2_w_gate, ffn2_w_up, ffn2_w_down):
    lower_bounds = jnp.cumsum(jax.nn.softmax(hg_lower_bound.astype(F32), axis=0), axis=0)
    b, t = x_prompt.shape[:2]
    db, tn = x_sample.shape[:2]
    past_len = page_table.shape[1] * cache_k.shape[2]
    pos_prompt = jnp.arange(t)
    pos_sample = past_len + jnp.arange(tn)
    s0_prompt = jnp.zeros((b, HG_HEADS, HG_KDIM, HG_VDIM), F32)
    xp, xs = x_prompt, x_sample
    kp_l, vp_l, ikp_l, sp_l, ks_l, vs_l, iks_l, ss_l = [], [], [], [], [], [], [], []
    for l in range(DEPTH):
        w = (ffn1_norm[l], ffn1_w_gate[l], ffn1_w_up[l], ffn1_w_down[l], mix_norm[l], w_in[l],
             q_norm[l], k_norm[l], hg_norm[l], w_branch_attn[l], w_branch_hgrn[l], w_out[l],
             ffn2_norm[l], ffn2_w_gate[l], ffn2_w_up[l], ffn2_w_down[l])
        xp, kp, vp, ikp, sp = _layer(xp, pos_prompt, _dsa_prompt, s0_prompt, lower_bounds[l], *w)
        attend_sample = functools.partial(_dsa_sample, layer=l, cache_k=cache_k, cache_v=cache_v,
                                          cache_ik=cache_idx_k, page_table=page_table)
        xs, ksm, vsm, iksm, ssm = _layer(xs, pos_sample, attend_sample, state_hgrn[l], lower_bounds[l], *w)
        kp_l.append(kp); vp_l.append(vp); ikp_l.append(ikp); sp_l.append(sp.astype(x_prompt.dtype))
        ks_l.append(ksm); vs_l.append(vsm); iks_l.append(iksm); ss_l.append(ssm.astype(state_hgrn.dtype))
    return (xp, xs,
            jnp.stack(kp_l), jnp.stack(vp_l), jnp.stack(ikp_l), jnp.stack(sp_l),
            jnp.stack(ks_l), jnp.stack(vs_l), jnp.stack(iks_l), jnp.stack(ss_l))


_drawn_inputs = setup_inputs


def setup_inputs(seed=0):
    import zlib

    import numpy as np

    out = dict(_drawn_inputs(seed))
    spreads = {}
    factors = {'ffn1_norm': 5.712,
     'mix_norm': 2.728,
     'q_norm': 195.067,
     'k_norm': 27.711,
     'hg_norm': 26.901,
     'ffn2_norm': 29.979,
     'cache_k': 3.312,
     'cache_v': 3.433,
     'cache_idx_k': 3.528}
    for name, (base, spread) in spreads.items():
        noise = np.random.default_rng([zlib.crc32(name.encode()), seed]).standard_normal(out[name].shape)
        drawn = base * np.exp(spread * noise) if base else spread * noise
        out[name] = __import__('jax').numpy.asarray(drawn.astype(out[name].dtype))
    for name, factor in factors.items():
        out[name] = (out[name] * factor).astype(out[name].dtype)
    return out
```

```python
import math
from contextlib import ExitStack

import numpy as np

import concourse.bass as bass
from concourse import mybir
from concourse.bass import DynSlice

F32 = mybir.dt.float32
F32R = mybir.dt.float32r
I32 = mybir.dt.int32
ACT = mybir.ActivationFunctionType
ALU = mybir.AluOpType
AX = mybir.AxisListType

P = 128
D = 1024
KD = D // P
SEQ = 1024
TILES = SEQ // P
DB, DT = 8, 4
NS = DB * DT
T = SEQ + NS
CH = 352
NCH = T // CH
FF = 2816
NFF = FF // P
PAIRS = NFF // 2
EPS = 1e-6
RAW = 6
UNIT = 1024


class Scope:

    def __init__(self, nc, tag):
        self.nc, self.tag, self.stack, self.sems = nc, tag, ExitStack(), []
        self.blocks = ExitStack()

    def __enter__(self):
        self.stack.__enter__()
        return self

    def __exit__(self, *a):
        self.blocks.close()
        if self.sems and a[0] is None:
            with self.nc.Block() as block:
                @block.gpsimd
                def _(pool):
                    for sem in self.sems:
                        pool.sem_clear(sem)
        return self.stack.__exit__(*a)

    def sb(self, name, shape, dt=F32):
        return self.stack.enter_context(self.nc.sbuf_tensor(f"{self.tag}_{name}", shape, dt))

    def ps(self, name, shape, dt=F32):
        return self.stack.enter_context(self.nc.psum_tensor(f"{self.tag}_{name}", shape, dt))

    def sem(self, name):
        self.sems.append(self.stack.enter_context(self.nc.semaphore(f"{self.tag}_{name}")))
        return self.sems[-1]

    def block(self):
        return self.blocks.enter_context(self.nc.Block())


def load_and_turn(nc, x_prompt, x_sample, xT, ident):
    with Scope(nc, "turn") as s:
        rows = s.sb("rows", [P, 2, D])
        turned = s.ps("turned", [P, 4, 4, P])
        loaded = [s.sem(f"loaded{n}") for n in range(2)]
        half_turned = s.sem("half_turned")
        half_kept = s.sem("half_kept")
        xp = x_prompt[0].rearrange("(n p) d -> n p d", p=P)
        xs = x_sample.rearrange("b t d -> (b t) d")
        block = s.block()

        @block.sync
        def _(sp):
            def load(i, n):
                sp.dma_start(rows[:, n, :], xp[DynSlice(2 * i + n, 1)].rearrange("a p d -> (a p) d")
                             ).then_inc(loaded[n], 16)

            load(0, 0)
            load(0, 1)
            with sp.Fori(1, TILES // 2) as i:
                for n in range(2):
                    sp.wait_ge(half_turned, 4 * i - 2 + 2 * n)
                    load(i, n)
            sp.wait_ge(half_turned, 4 * (TILES // 2))
            sp.dma_start(rows[0:NS, 0, :], xs).then_inc(loaded[0], 16)

        @block.tensor
        def _(pe):
            with pe.Fori(0, TILES // 2) as i:
                for n in range(2):
                    pe.wait_ge(loaded[n], 16 * i + 16)
                    for h in range(2):
                        pe.wait_ge(half_kept, 4 * i)
                        for k in range(4):
                            m = nc.tensor.transpose(turned[:, 2 * n + h, k, :],
                                                    rows[:, n, (4 * h + k) * P:(4 * h + k + 1) * P], ident[:, :])
                        m.then_inc(half_turned, 1)
            pe.wait_ge(loaded[0], 16 * (TILES // 2) + 16)
            pe.wait_ge(half_kept, 4 * (TILES // 2))
            for h in range(2):
                for k in range(4):
                    m = nc.tensor.transpose(turned[:, h, k, 0:NS],
                                            rows[0:NS, 0, (4 * h + k) * P:(4 * h + k + 1) * P], ident[0:NS, 0:NS])
                m.then_inc(half_turned, 1)

        @block.vector
        def _(dve):
            with dve.Fori(0, TILES // 2) as i:
                for n in range(2):
                    for h in range(2):
                        dve.wait_ge(half_turned, 4 * i + 2 * n + h + 1)
                        nc.vector.tensor_copy(xT[:, 4 * h:4 * h + 4, DynSlice(2 * P * i + P * n, P)],
                                              turned[:, 2 * n + h, :, :]).then_inc(half_kept, 1)
            for h in range(2):
                dve.wait_ge(half_turned, 4 * (TILES // 2) + h + 1)
                nc.vector.tensor_copy(xT[:, 4 * h:4 * h + 4, SEQ:T], turned[:, h, :, 0:NS]).then_inc(half_kept, 1)


def turn_and_store(nc, xT, y_prompt, y_sample, ident):
    with Scope(nc, "back") as s:
        rows = s.sb("rows", [P, 2, D])
        turned = s.ps("turned", [P, 4, 4, P])
        half_turned = s.sem("half_turned")
        half_kept = s.sem("half_kept")
        stored = [s.sem(f"stored{n}") for n in range(2)]
        yp = y_prompt[0].rearrange("(n p) d -> n p d", p=P)
        block = s.block()

        @block.sync
        def _(sp):
            for n in range(TILES + 1):
                sp.wait_ge(half_kept, 2 * n + 2)
                if n < TILES:
                    sp.dma_start(yp[n], rows[:, n % 2, :]).then_inc(stored[n % 2], 16)
                else:
                    sp.dma_start(y_sample.rearrange("b t d -> (b t) d"), rows[0:NS, n % 2, :]).then_inc(stored[n % 2], 16)
            sp.wait_ge(stored[0], 16 * (TILES // 2 + 1))
            sp.wait_ge(stored[1], 16 * (TILES // 2))

        @block.tensor
        def _(pe):
            for n in range(TILES + 1):
                w = P if n < TILES else NS
                for h in range(2):
                    if n >= 2:
                        pe.wait_ge(half_kept, 2 * n - 3 + h)
                    for k in range(4):
                        m = nc.tensor.transpose(turned[0:w, 2 * (n % 2) + h, k, :],
                                                xT[:, 4 * h + k, n * P:n * P + w], ident[:, :])
                    m.then_inc(half_turned, 1)

        @block.vector
        def _(dve):
            for n in range(TILES + 1):
                w = P if n < TILES else NS
                for h in range(2):
                    dve.wait_ge(half_turned, 2 * n + h + 1)
                    if n >= 2 and h == 0:
                        dve.wait_ge(stored[n % 2], 16 * (n // 2))
                    nc.vector.tensor_copy(rows[0:w, n % 2, 4 * h * P:4 * (h + 1) * P],
                                          turned[0:w, 2 * (n % 2) + h, :, :].rearrange("p a b -> p (a b)")
                                          ).then_inc(half_kept, 1)


def normalise(nc, tag, xT, gain, hhi, hlo, ones):
    with Scope(nc, tag) as s:
        sq = s.sb("sq", [P, KD, CH])
        full = s.sb("full", [P, KD, CH])
        var = s.sb("var", [P, CH])
        inv = s.sb("inv", [P, CH])
        root = s.sb("root", [P, NCH, CH])
        tmp = s.sb("tmp", [P, CH])
        total = s.ps("total", [P, NCH, 512])
        g = s.sb("gain", [P, KD])
        gain_in = s.sem("gain_in")
        squared = s.sem("squared")
        summed = s.sem("summed")
        step = s.sem("step")
        inverted = s.sem("inverted")
        rooted = s.sem("rooted")
        hi_done = s.sem("hi_done")
        block = s.block()

        def cols(c):
            return slice(c * CH, (c + 1) * CH)

        @block.sync
        def _(sp):
            sp.dma_start(g[:, :], gain).then_inc(gain_in, 16)

        @block.scalar
        def _(act):
            for c in range(NCH):
                if c:
                    act.wait_ge(summed, c)
                nc.scalar.activation(sq[:, :, :], xT[:, :, cols(c)], ACT.Square).then_inc(squared, 1)
                act.wait_ge(inverted, c + 1)
                nc.scalar.activation(root[:, c, :], inv[:, :], ACT.Sqrt).then_inc(rooted, 1)

        @block.tensor
        def _(pe):
            for c in range(NCH):
                pe.wait_ge(squared, c + 1)
                for k in range(KD):
                    m = nc.tensor.matmul(total[:, c, 0:CH], ones[:, :], sq[:, k, :], start=(k == 0), stop=(k == KD - 1))
                m.then_inc(summed, 1)

        @block.vector
        def _(dve):
            steps = [0]

            def done(ins):
                ins.then_inc(step, 1)
                steps[0] += 1
                dve.wait_ge(step, steps[0])

            dve.wait_ge(gain_in, 16)
            for c in range(NCH):
                dve.wait_ge(summed, c + 1)
                done(nc.vector.tensor_scalar(var[:, :], total[:, c, 0:CH], 1.0 / D, EPS, ALU.mult, ALU.add))
                nc.vector.reciprocal(inv[:, :], var[:, :]).then_inc(inverted, 1)
                dve.wait_ge(rooted, c + 1)
                done(nc.vector.tensor_tensor(tmp[:, :], root[:, c, :], root[:, c, :], ALU.mult))
                done(nc.vector.tensor_tensor(tmp[:, :], tmp[:, :], var[:, :], ALU.mult))
                done(nc.vector.tensor_scalar(tmp[:, :], tmp[:, :], -0.5, 1.5, ALU.mult, ALU.add))
                done(nc.vector.tensor_tensor(root[:, c, :], root[:, c, :], tmp[:, :], ALU.mult))
                for k in range(KD):
                    done(nc.vector.scalar_tensor_tensor(full[:, k, :], xT[:, k, cols(c)], g[:, k:k + 1],
                                                        root[:, c, :], ALU.mult, ALU.mult))
                nc.vector.tensor_copy(hhi[:, :, cols(c)], full[:, :, :]).then_inc(hi_done, 1)
                dve.wait_ge(hi_done, c + 1)
                done(nc.vector.tensor_tensor(hlo[:, :, cols(c)], full[:, :, :], hhi[:, :, cols(c)], ALU.subtract))


def split_product(nc, out, w_hi, w_lo, x_hi, x_lo, first, last):
    nc.tensor.matmul(out, w_hi, x_hi, start=first, stop=False)
    nc.tensor.matmul(out, w_hi, x_lo, start=False, stop=False)
    return nc.tensor.matmul(out, w_lo, x_hi, start=False, stop=last)


def swiglu(nc, tag, xT, hhi, hlo, w_gate, w_up, w_down):
    with Scope(nc, tag) as s:
        raw = s.sb("raw", [P, RAW, UNIT])
        whi = s.sb("whi", [P, RAW, UNIT], F32R)
        wlo = s.sb("wlo", [P, RAW, UNIT], F32R)
        act_out = s.sb("silu", [P, 2, CH])
        prod = s.sb("prod", [P, 2, CH])
        ahi = s.sb("ahi", [P, 2, T], F32R)
        alo = s.sb("alo", [P, 2, T], F32R)
        gu = s.ps("gu", [P, 2, 2, 512])
        dn = s.ps("dn", [P, 4, 512])
        raw_loaded = [s.sem(f"raw_loaded{n}") for n in range(RAW)]
        w_hi_done = s.sem("w_hi_done")
        w_lo_done = s.sem("w_lo_done")
        gu_done = s.sem("gu_done")
        silu_done = s.sem("silu_done")
        prod_done = s.sem("prod_done")
        a_hi_done = s.sem("a_hi_done")
        a_lo_done = s.sem("a_lo_done")
        down_done = s.sem("down_done")
        down_free = s.sem("down_free")
        block = s.block()
        wg = w_gate[0].rearrange("(k p) f -> p k f", p=P)
        wu = w_up[0].rearrange("(k p) f -> p k f", p=P)
        wd = w_down[0].rearrange("(j p) n -> j p n", p=P)

        @block.sync
        def _(sp):
            def load(g, u, wait):
                if wait:
                    sp.wait_ge(w_lo_done, 6 * g + u - RAW + 1)
                if u < 4:
                    src = (wg, wu)[u % 2][:, :, DynSlice((2 * g + u // 2) * P, P)]
                    dst = raw[:, u, :].rearrange("p (k f) -> p k f", k=KD)
                else:
                    src = wd[DynSlice(2 * g + u - 4, 1)].rearrange("a p n -> (a p) n")
                    dst = raw[:, u, :]
                sp.dma_start(dst, src).then_inc(raw_loaded[u], 16)

            for u in range(6):
                load(0, u, False)
            with sp.Fori(1, PAIRS) as g:
                for u in range(6):
                    load(g, u, True)

        @block.scalar
        def _(act):
            def hi(i, k, wait=True):
                if wait and k in (2, 3):
                    act.wait_ge(gu_done, 6 * i)
                elif wait and k in (4, 5):
                    act.wait_ge(down_done, 24 * i)
                elif wait:
                    act.wait_ge(gu_done, 6 * i + 3)
                act.wait_ge(raw_loaded[k % 6], 16 * (i + k // 6) + 16)
                nc.scalar.activation(whi[:, k % 6, :], raw[:, k % 6, :], ACT.Copy).then_inc(w_hi_done, 1)

            def silu(i, q):
                act.wait_ge(gu_done, 6 * i + q + 1)
                nc.scalar.activation(act_out[:, q % 2, :], gu[:, q % 2, 0, 0:CH], ACT.Silu).then_inc(silu_done, 1)

            def round_(i, last=False):
                hi(i, 2)
                hi(i, 3)
                hi(i, 4)
                hi(i, 5)
                for q in range(3):
                    silu(i, q)
                if not last:
                    hi(i, 6)
                    hi(i, 7)
                for q in range(3, 6):
                    silu(i, q)

            for k in range(6):
                hi(0, k, False)
            for q in range(3):
                silu(0, q)
            hi(0, 6)
            hi(0, 7)
            for q in range(3, 6):
                silu(0, q)
            with act.Fori(1, PAIRS - 1) as i:
                round_(i)
            round_(PAIRS - 1, True)

        @block.vector
        def _(dve):
            def lo(i, k):
                dve.wait_ge(w_hi_done, 6 * i + k + 1)
                nc.vector.tensor_tensor(wlo[:, k % 6, :], raw[:, k % 6, :], whi[:, k % 6, :], ALU.subtract
                                        ).then_inc(w_lo_done, 1)

            def product(i, q, first=False):
                b, cols = q // 3, slice(q % 3 * CH, (q % 3 + 1) * CH)
                dve.wait_ge(silu_done, 6 * i + q + 1)
                nc.vector.tensor_tensor(prod[:, q % 2, :], act_out[:, q % 2, :], gu[:, q % 2, 1, 0:CH], ALU.mult
                                        ).then_inc(prod_done, 1)
                dve.wait_ge(prod_done, 6 * i + q + 1)
                if not first:
                    dve.wait_ge(down_done, 24 * i)
                nc.vector.tensor_copy(ahi[:, b, cols], prod[:, q % 2, :]).then_inc(a_hi_done, 1)
                dve.wait_ge(a_hi_done, 6 * i + q + 1)
                nc.vector.tensor_tensor(alo[:, b, cols], prod[:, q % 2, :], ahi[:, b, cols], ALU.subtract
                                        ).then_inc(a_lo_done, 1)

            def add_down(i):
                for j in range(NCH * KD):
                    c, k = j // KD, j % KD
                    dve.wait_ge(down_done, 24 * i + j + 1)
                    x = xT[:, k, c * CH:(c + 1) * CH]
                    nc.vector.scalar_tensor_tensor(x, dn[:, j % 4, 0:CH], 0.5, x, ALU.mult, ALU.add
                                                   ).then_inc(down_free, 1)

            def round_(i, last=False):
                lo(i, 2)
                lo(i, 3)
                add_down(i - 1)
                lo(i, 4)
                lo(i, 5)
                for q in range(3):
                    product(i, q)
                if not last:
                    lo(i, 6)
                    lo(i, 7)
                for q in range(3, 6):
                    product(i, q)

            dve.sem_inc(down_free, 4)
            for k in range(6):
                lo(0, k)
            for q in range(3):
                product(0, q, True)
            lo(0, 6)
            lo(0, 7)
            for q in range(3, 6):
                product(0, q, True)
            with dve.Fori(1, PAIRS - 1) as i:
                round_(i)
            round_(PAIRS - 1, True)
            add_down(PAIRS - 1)

        @block.tensor
        def _(pe):
            def gate_up(i, b, first=False):
                pe.wait_ge(w_lo_done, 6 * i + 2 * b + 2)
                for c in range(NCH):
                    q = 3 * b + c
                    cols = slice(c * CH, (c + 1) * CH)
                    if not (first and q < 2):
                        pe.wait_ge(prod_done, 6 * i + q - 1)
                    for m in range(2):
                        u = 2 * b + m
                        for k in range(KD):
                            w = slice(k * P, (k + 1) * P)
                            last = split_product(nc, gu[:, q % 2, m, 0:CH], whi[:, u, w], wlo[:, u, w],
                                                 hhi[:, k, cols], hlo[:, k, cols], k == 0, k == KD - 1)
                    last.then_inc(gu_done, 1)

            def down(i):
                pe.wait_ge(w_lo_done, 6 * i + 6)
                for j in range(NCH * KD):
                    c, k = j // KD, j % KD
                    cols = slice(c * CH, (c + 1) * CH)
                    if k == 0:
                        pe.wait_ge(a_lo_done, 6 * i + 3 + c + 1)
                    pe.wait_ge(down_free, 24 * i + j + 1)
                    for b in range(2):
                        last = split_product(nc, dn[:, j % 4, 0:CH], whi[:, 4 + b, k * P:(k + 1) * P],
                                             wlo[:, 4 + b, k * P:(k + 1) * P], ahi[:, b, cols], alo[:, b, cols],
                                             b == 0, b == 1)
                    last.then_inc(down_done, 1)

            gate_up(0, 0, True)
            gate_up(0, 1)
            with pe.Fori(1, PAIRS) as i:
                down(i - 1)
                gate_up(i, 0)
                gate_up(i, 1)
            down(PAIRS - 1)


HD = 64
HEADS, KV = 8, 4
TT = TILES + 1
CW = 256
SROW = P - NS
CHUNKS = [("q", 0), ("q", 256), ("k", 512), ("v", 768), ("qi", 1024), ("qi", 1280), ("ki", 1536),
          ("hv", 2632), ("hv", 2888)]
KI_COLS = HD + HEADS


def newton_rsqrt(nc, done, root, var, tmp):
    done(nc.vector.tensor_tensor(tmp, root, root, ALU.mult))
    done(nc.vector.tensor_tensor(tmp, tmp, var, ALU.mult))
    done(nc.vector.tensor_scalar(tmp, tmp, -0.5, 1.5, ALU.mult, ALU.add))
    done(nc.vector.tensor_tensor(root, root, tmp, ALU.mult))


def token_projections(nc, hhi, hlo, w_in, q_gain, k_gain, cos, sin, ident, qT_d, kT_d, qiT_d, kiT_d, wi_d, hv_d,
                      k_prompt, k_sample, v_prompt, v_sample, ki_prompt, ki_sample):
    NC = len(CHUNKS)
    M = NC * TT
    with Scope(nc, "tok") as s:
        raw = s.sb("raw", [P, 2, KD, CW])
        whi = s.sb("whi", [P, 2, KD, CW], F32R)
        wlo = s.sb("wlo", [P, 2, KD, CW], F32R)
        taken = s.sb("taken", [P, 4, CW])
        sq = s.sb("sq", [P, 2, CW])
        var = s.sb("var", [P, 4])
        inv = s.sb("inv", [P, 4])
        root = s.sb("root", [P, 4])
        tmp = s.sb("tmp", [P, 4])
        xn = s.sb("xn", [P, CW])
        ra = s.sb("ra", [P, CW])
        rb = s.sb("rb", [P, CW])
        out = s.sb("out", [P, 4, CW])
        stage = s.sb("stage", [P, 2, 2, T])
        gains = s.sb("gains", [P, 2, HD])
        cs = s.sb("cs", [P, TT, HD])
        sn = s.sb("sn", [P, TT, HD])
        proj = s.ps("proj", [P, 4, 512])
        turned = s.ps("turned", [P, 2, 4, P])
        w_loaded = [s.sem(f"w_loaded{n}") for n in range(2)]
        tables_in = s.sem("tables_in")
        w_hi_done, w_lo_done = s.sem("w_hi_done"), s.sem("w_lo_done")
        proj_done, take_done, sq_done = s.sem("proj_done"), s.sem("take_done"), s.sem("sq_done")
        inv_done, root_done = s.sem("inv_done"), s.sem("root_done")
        step, out_done = s.sem("step"), s.sem("out_done")
        turn_done, kept_done = s.sem("turn_done"), s.sem("kept_done")
        out_stored = [s.sem(f"out_stored{n}") for n in range(4)]
        stage_stored = [s.sem(f"stage_stored{n}") for n in range(2)]
        block = s.block()

        def kind(m):
            return CHUNKS[m // TT][0]

        def width(c):
            return KI_COLS if CHUNKS[c][0] == "ki" else CW

        def normed(m):
            return kind(m) in "qk"

        def turns(m):
            return kind(m) not in ("v", "hv")

        def stores(m):
            return {"k": 1, "v": 1, "hv": 1, "ki": 2}.get(kind(m), 0)

        def count(f, m):
            return sum(1 for x in range(m) if f(x))

        def stored_before(m, slot):
            return sum(stores(x) for x in range(m) if x % 4 == slot)

        wv = w_in[0].rearrange("(k p) f -> p k f", p=P)

        @block.sync
        def _(sp):
            def load(c):
                if c >= 2:
                    sp.wait_ge(w_lo_done, c - 1)
                w, at = width(c), CHUNKS[c][1]
                sp.dma_start(raw[:, c % 2, :, 0:w], wv[:, :, at:at + w]).then_inc(w_loaded[c % 2], 16)

            load(0)
            for dst, src in ((gains[:, 0, :], q_gain.partition_broadcast(P)), (gains[:, 1, :], k_gain.partition_broadcast(P)),
                             (cs[:, :, :], cos), (sn[:, :, :], sin)):
                sp.dma_start(dst, src).then_inc(tables_in, 16)
            load(1)
            for m in range(M):
                c, n = m // TT, m % TT
                if n == 4 and c + 2 < NC:
                    load(c + 2)
                rows = slice(0, P) if n < TILES else slice(SROW, P)
                at = slice(n * P, (n + 1) * P)
                o = out[rows, m % 4, :]
                if stores(m):
                    sp.wait_ge(out_done, m + 1)
                if kind(m) == "k":
                    dst = k_prompt[at] if n < TILES else k_sample
                    sp.dma_start(dst, o).then_inc(out_stored[m % 4], 16)
                elif kind(m) == "v":
                    dst = v_prompt[at] if n < TILES else v_sample
                    sp.dma_start(dst, o).then_inc(out_stored[m % 4], 16)
                elif kind(m) == "hv":
                    dst = hv_d[n * P:n * P + (P if n < TILES else NS), (c - 7) * CW:(c - 6) * CW]
                    sp.dma_start(dst, o).then_inc(out_stored[m % 4], 16)
                elif kind(m) == "ki":
                    dst = ki_prompt[at] if n < TILES else ki_sample
                    sp.dma_start(dst, o[:, 0:HD]).then_inc(out_stored[m % 4], 16)
                    dst = wi_d[n * P:n * P + (P if n < TILES else NS)]
                    sp.dma_start(dst, o[:, 2 * HD:2 * HD + HEADS]).then_inc(out_stored[m % 4], 16)
                if n == TT - 1 and turns(m):
                    sp.wait_ge(kept_done, count(turns, m + 1))
                    dst = {"q": qT_d, "k": kT_d, "qi": qiT_d, "ki": kiT_d}[kind(m)]
                    b = {"q": 2 * c, "k": 0, "qi": 2 * (c - 4), "ki": 0}[kind(m)]
                    nb = 1 if kind(m) == "ki" else 2
                    sp.dma_start(dst[b:b + nb].rearrange("b p t -> p b t"), stage[:, c % 2, 0:nb, :]
                                 ).then_inc(stage_stored[c % 2], 16)
            for slot in range(4):
                sp.wait_ge(out_stored[slot], 16 * stored_before(M, slot))
            for slot in range(2):
                sp.wait_ge(stage_stored[slot], 16 * sum(1 for c in range(NC) if c % 2 == slot and turns(TT * c)))

        @block.gpsimd
        def _(pool):
            for c in range(NC):
                w = width(c)
                pool.wait_ge(w_hi_done, c + 1)
                nc.gpsimd.tensor_tensor(wlo[:, c % 2, :, 0:w], raw[:, c % 2, :, 0:w], whi[:, c % 2, :, 0:w],
                                        ALU.subtract).then_inc(w_lo_done, 1)

        @block.tensor
        def _(pe):
            def turn(m):
                if m < 0 or m >= M or not turns(m):
                    return
                x = count(turns, m)
                if x >= 2:
                    pe.wait_ge(kept_done, x - 1)
                pe.wait_ge(out_done, m + 1)
                for b in range(1 if kind(m) == "ki" else 2):
                    last = nc.tensor.transpose(turned[:, x % 2, b, :], out[:, m % 4, b * P:(b + 1) * P], ident[:, :])
                last.then_inc(turn_done, 1)

            for m in range(M):
                c, n = m // TT, m % TT
                w = width(c)
                if n == 0:
                    pe.wait_ge(w_lo_done, c + 1)
                if m >= 4:
                    pe.wait_ge(take_done, m - 3)
                tok = slice(n * P, (n + 1) * P) if n < TILES else slice(T - P, T)
                for k in range(KD):
                    ps = proj[:, m % 4, 0:w]
                    nc.tensor.matmul(ps, hhi[:, k, tok], whi[:, c % 2, k, 0:w], start=(k == 0), stop=False)
                    nc.tensor.matmul(ps, hhi[:, k, tok], wlo[:, c % 2, k, 0:w], start=False, stop=False)
                    last = nc.tensor.matmul(ps, hlo[:, k, tok], whi[:, c % 2, k, 0:w], start=False, stop=(k == KD - 1))
                last.then_inc(proj_done, 1)
                turn(m - 2)
            turn(M - 2)
            turn(M - 1)

        @block.scalar
        def _(act):
            def hi(c):
                w = width(c)
                act.wait_ge(w_loaded[c % 2], 16 * (c // 2) + 16)
                if c >= 2:
                    act.wait_ge(proj_done, TT * (c - 1))
                nc.scalar.activation(whi[:, c % 2, :, 0:w], raw[:, c % 2, :, 0:w], ACT.Copy).then_inc(w_hi_done, 1)

            def keep(m):
                if m < 0 or m >= M or not turns(m):
                    return
                c, n = m // TT, m % TT
                act.wait_ge(turn_done, count(turns, m + 1))
                prior = sum(1 for x in range(c) if x % 2 == c % 2 and turns(TT * x))
                if n == 0 and prior:
                    act.wait_ge(stage_stored[c % 2], 16 * prior)
                nb = 1 if kind(m) == "ki" else 2
                x = count(turns, m) % 2
                if n < TILES:
                    dst, src = stage[:, c % 2, 0:nb, n * P:(n + 1) * P], turned[:, x, 0:nb, :]
                else:
                    dst, src = stage[:, c % 2, 0:nb, SEQ:T], turned[:, x, 0:nb, SROW:P]
                nc.scalar.activation(dst, src, ACT.Copy).then_inc(kept_done, 1)

            hi(0)
            hi(1)
            for m in range(M):
                c, n = m // TT, m % TT
                w = width(c)
                act.wait_ge(proj_done, m + 1)
                if m >= 4:
                    act.wait_ge(out_done, m - 3)
                nc.scalar.activation(taken[:, m % 4, 0:w], proj[:, m % 4, 0:w], ACT.Copy).then_inc(take_done, 1)
                if normed(m):
                    act.wait_ge(take_done, m + 1)
                    nc.scalar.activation(sq[:, m % 2, :], taken[:, m % 4, :], ACT.Square).then_inc(sq_done, 1)
                    act.wait_ge(inv_done, count(normed, m + 1))
                    nc.scalar.activation(root[:, :], inv[:, :], ACT.Sqrt).then_inc(root_done, 1)
                keep(m - 3)
                if n == 0 and 1 <= c < NC - 1:
                    hi(c + 1)
            for m in range(M - 3, M):
                keep(m)

        @block.vector
        def _(dve):
            steps = [0]

            def done(ins):
                ins.then_inc(step, 1)
                steps[0] += 1
                dve.wait_ge(step, steps[0])

            def rope(src, n, heads):
                def over(table, a, b):
                    return table[:, n, a:b].unsqueeze(1).broadcast_to([P, heads, b - a])

                h = HD // 2
                a = ra[:, 0:heads * HD].rearrange("p (h d) -> p h d", d=HD)
                b = rb[:, 0:heads * HD].rearrange("p (h d) -> p h d", d=HD)
                done(nc.vector.tensor_tensor(a, src, over(cs, 0, HD), ALU.mult))
                done(nc.vector.tensor_tensor(b[:, :, 0:h], src[:, :, h:HD], over(sn, 0, h), ALU.mult))
                done(nc.vector.tensor_tensor(b[:, :, h:HD], src[:, :, 0:h], over(sn, h, HD), ALU.mult))
                return a, b

            dve.wait_ge(tables_in, 64)
            for m in range(M):
                c, n = m // TT, m % TT
                slot = m % 4
                x = taken[:, slot, :].rearrange("p (h d) -> p h d", d=HD)
                if normed(m):
                    dve.wait_ge(sq_done, count(normed, m + 1))
                    done(nc.vector.tensor_reduce(var[:, :], sq[:, m % 2, :].rearrange("p (h d) -> p h d", d=HD),
                                                 AX.X, ALU.add))
                    done(nc.vector.tensor_scalar(var[:, :], var[:, :], 1.0 / HD, EPS, ALU.mult, ALU.add))
                    nc.vector.reciprocal(inv[:, :], var[:, :]).then_inc(inv_done, 1)
                    dve.wait_ge(root_done, count(normed, m + 1))
                    newton_rsqrt(nc, done, root[:, :], var[:, :], tmp[:, :])
                    y = xn[:, :].rearrange("p (h d) -> p h d", d=HD)
                    done(nc.vector.tensor_tensor(y, x, root[:, :].unsqueeze(2).broadcast_to([P, 4, HD]), ALU.mult))
                    g = gains[:, 0 if kind(m) == "q" else 1, :].unsqueeze(1).broadcast_to([P, 4, HD])
                    done(nc.vector.tensor_tensor(y, y, g, ALU.mult))
                    x = y
                if m:
                    dve.wait_ge(out_done, m)
                if m >= 4:
                    dve.wait_ge(take_done, m + 1)
                    if turns(m - 4):
                        dve.wait_ge(turn_done, count(turns, m - 3))
                    if stores(m - 4):
                        dve.wait_ge(out_stored[slot], 16 * stored_before(m, slot))
                else:
                    dve.wait_ge(take_done, m + 1)
                if not turns(m):
                    nc.vector.tensor_copy(out[:, slot, :], taken[:, slot, :]).then_inc(out_done, 1)
                elif kind(m) == "ki":
                    x = x[:, 0:1, :]
                    a, b = rope(x, n, 1)
                    o = out[:, slot, :].rearrange("p (h d) -> p h d", d=HD)
                    done(nc.vector.tensor_tensor(o[:, 0:1, :], a, b, ALU.add))
                    done(nc.vector.tensor_copy(o[:, 1:2, :], o[:, 0:1, :]))
                    nc.vector.tensor_scalar(out[:, slot, 2 * HD:2 * HD + HEADS], taken[:, slot, HD:HD + HEADS],
                                            float(HEADS) ** -0.5, None, ALU.mult).then_inc(out_done, 1)
                else:
                    a, b = rope(x, n, 4)
                    if kind(m) == "q":
                        o = out[:, slot, :].rearrange("p (r g d) -> p g r d", g=2, d=HD)
                        a = a.rearrange("p (g r) d -> p g r d", g=2)
                        b = b.rearrange("p (g r) d -> p g r d", g=2)
                    else:
                        o = out[:, slot, :].rearrange("p (h d) -> p h d", d=HD)
                    nc.vector.tensor_tensor(o, a, b, ALU.add).then_inc(out_done, 1)


SLABS = TILES - 2 + 1
TOPK = 256
PAGES = 8
PS = 128
PAST = PAGES * PS
SW = PAST + DT
PADB = P + DT
FLOOR = -3.0e38
MASKED = -1.0e30
N_POOL = 80


def slab_width(s):
    return (s + 3) * P if s < SLABS - 1 else SW


def spread(wide):
    return wide[:, :].rearrange("p (b c) -> p b c", c=PADB)[:, :, 0:P].rearrange("p b (h t) -> p b h t", t=NS)[:, :, :, 0:DT]


def index_scores(nc, scores, qiT_d, kiT_d, wi_d, cache_idx_k, page_table, same_token, new_floor, ident):
    with Scope(nc, "idx") as s:
        qiT = s.sb("qiT", [P, 4, T])
        kiT = s.sb("kiT", [P, T])
        w = s.sb("w", [P, TILES, HEADS])
        w_rows = s.sb("w_rows", [P, 2])
        wide = s.sb("wide", [P, DB * PADB])
        pages = s.sb("pages", [P, 2, PAGES, HD])
        past = s.sb("past", [P, 2, PAST])
        relus = s.sb("relus", [P, 3, SW])
        part = s.sb("part", [P, SW])
        sel = s.sb("sel", [P, P])
        floor = s.sb("floor", [P, DT])
        table = s.sb("table", [1, DB * PAGES], I32)
        big = s.ps("big", [P, 6 * 512])
        turned = s.ps("turned", [P, 2, 512])
        loads = [s.sem("qiT_in"), s.sem("kiT_in"), s.sem("w_in"), s.sem("w_rows_in"), s.sem("sel_in"), s.sem("floor_in")]
        qiT_in, kiT_in, w_in, w_rows_in, sel_in, floor_in = loads
        table_in = s.sem("table_in")
        pages_in = [s.sem(f"pages_in{n}") for n in range(2)]
        zeroed, spread_done = s.sem("zeroed"), s.sem("spread_done")
        page_turned, low_kept, high_kept = s.sem("page_turned"), s.sem("low_kept"), s.sem("high_kept")
        seq_scored = s.sem("seq_scored")
        sample_relu, sample_part, sample_sum, sample_done = (s.sem("sample_relu"), s.sem("sample_part"),
                                                             s.sem("sample_sum"), s.sem("sample_done"))
        head_scored, relu_done, head_added, masked = (s.sem("head_scored"), s.sem("relu_done"), s.sem("head_added"),
                                                      s.sem("masked"))
        block = s.block()
        steps = [(t, h) for t in range(2, TILES) for h in range(HEADS)]

        @block.sync
        def _(sp):
            sp.dma_start(table[:, :], page_table.rearrange("(a b) n -> a (b n)", a=1)).then_inc(table_in, 16)
            sp.dma_start(qiT[:, :, :], qiT_d.rearrange("b p t -> p b t")).then_inc(qiT_in, 16)
            sp.dma_start(kiT[:, :], kiT_d[0]).then_inc(kiT_in, 16)
            sp.dma_start(w[:, :, :], wi_d[0:SEQ].rearrange("(n p) h -> p n h", p=P)).then_inc(w_in, 16)
            for h in range(4):
                sp.dma_start(w_rows[NS * h:NS * (h + 1), :], wi_d[SEQ:T, 2 * h:2 * h + 2]).then_inc(w_rows_in, 16)
            sp.dma_start(sel[:, :], same_token).then_inc(sel_in, 16)
            sp.dma_start(floor[:, :], new_floor).then_inc(floor_in, 16)
            sp.wait_ge(table_in, 16)

            def load(i, n, wait):
                if wait:
                    sp.wait_ge(page_turned, 4 * i - 2 + 2 * n)
                for g in range(PAGES):
                    page = sp.value_load(table[0:1, DynSlice(PAGES * (2 * i + n) + g, 1)], min_val=0, max_val=N_POOL - 1)
                    sp.dma_start(pages[:, n, g, :], cache_idx_k[0][DynSlice(page, 1)].rearrange("a s d -> (a s) d")
                                 ).then_inc(pages_in[n], 16)

            load(0, 0, False)
            load(0, 1, False)
            with sp.Fori(1, DB // 2) as i:
                for n in range(2):
                    load(i, n, True)

        @block.gpsimd
        def _(pool):
            for t in range(2, TILES):
                pool.wait_ge(head_added, HEADS * (t - 1))
                d = scores[:, t - 2, t * P:(t + 1) * P]
                nc.gpsimd.affine_select(out=d, in_=d, compare_op=ALU.is_ge, fill=FLOOR, base=0, pattern=[[-1, P]],
                                        channel_multiplier=1).then_inc(masked, 1)

        @block.tensor
        def _(pe):
            def turn(b):
                pe.wait_ge(pages_in[b % 2], 16 * PAGES * (b // 2 + 1))
                if b:
                    pe.wait_ge(low_kept, 2 * b)
                for x in range(2):
                    for g in range(4):
                        last = nc.tensor.transpose(turned[0:HD, x, g * PS:(g + 1) * PS], pages[:, b % 2, 4 * x + g, :],
                                                   ident[:, :])
                    last.then_inc(page_turned, 1)

            turn(0)
            pe.wait_ge(spread_done, 1)
            pe.wait_ge(kiT_in, 16)
            for b in range(DB):
                if b + 1 < DB:
                    turn(b + 1)
                pe.wait_ge(low_kept, 2 * b + 2)
                pe.wait_ge(high_kept, 2 * b + 2)
                for half in range(2):
                    r = slice(half * HD, (half + 1) * HD)
                    q = wide[r, b * P:(b + 1) * P]
                    for x in range(2):
                        nc.tensor.matmul(big[:, (3 * half + x) * 512:(3 * half + x + 1) * 512], q,
                                         past[r, b % 2, x * 512:(x + 1) * 512], start=(b == 0), stop=(b == DB - 1))
                    last = nc.tensor.matmul(big[:, (3 * half + 2) * 512:(3 * half + 2) * 512 + DT], q,
                                            kiT[r, SEQ + DT * b:SEQ + DT * (b + 1)], start=(b == 0), stop=(b == DB - 1))
                last.then_inc(seq_scored, 1)
            pe.wait_ge(sel_in, 16)
            pe.wait_ge(sample_part, 2)
            for x in range(3):
                n = 512 if x < 2 else DT
                last = nc.tensor.matmul(big[:, x * 512:x * 512 + n], sel[:, :], part[:, x * 512:x * 512 + n],
                                        start=True, stop=True)
            last.then_inc(sample_sum, 1)
            for a, (t, h) in enumerate(steps):
                if a < 2:
                    pe.wait_ge(sample_done, a + 1)
                if a >= 3:
                    pe.wait_ge(relu_done, a - 2)
                r = slice(h % 2 * HD, (h % 2 + 1) * HD)
                at = (a + 2) % 3 * 1024
                for x in range(0, (t + 1) * P, 512):
                    n = min(512, (t + 1) * P - x)
                    last = nc.tensor.matmul(big[:, at + x:at + x + n], qiT[r, h // 2, t * P:(t + 1) * P], kiT[r, x:x + n],
                                            start=True, stop=True)
                last.then_inc(head_scored, 1)

        @block.scalar
        def _(act):
            for b in range(DB):
                for x in range(2):
                    act.wait_ge(page_turned, 2 * b + x + 1)
                    if b >= 2:
                        act.wait_ge(seq_scored, b - 1)
                    nc.scalar.activation(past[0:HD, b % 2, x * 512:(x + 1) * 512], turned[0:HD, x, :], ACT.Copy
                                         ).then_inc(low_kept, 1)
            act.wait_ge(seq_scored, DB)
            for half in range(2):
                nc.scalar.activation(relus[:, half, 0:SW], big[:, half * 1536:half * 1536 + SW], ACT.Relu,
                                     scale=HD ** -0.5).then_inc(sample_relu, 1)
            for a, (t, h) in enumerate(steps):
                act.wait_ge(head_scored, a + 1)
                if a < 3:
                    act.wait_ge(sample_part, 2)
                else:
                    act.wait_ge(head_added, a - 2)
                n = (t + 1) * P
                at = (a + 2) % 3 * 1024
                nc.scalar.activation(relus[:, a % 3, 0:n], big[:, at:at + n], ACT.Relu, scale=HD ** -0.5
                                     ).then_inc(relu_done, 1)

        @block.vector
        def _(dve):
            nc.vector.memset(wide[:, :], 0.0).then_inc(zeroed, 1)
            dve.wait_ge(zeroed, 1)
            dve.wait_ge(qiT_in, 16)
            nc.vector.tensor_copy(spread(wide), qiT[:, :, SEQ:T].rearrange("p h (b j) -> p b h j", j=DT)
                                  ).then_inc(spread_done, 1)
            for b in range(DB):
                for x in range(2):
                    dve.wait_ge(low_kept, 2 * b + x + 1)
                    nc.vector.tensor_copy(past[HD:P, b % 2, x * 512:(x + 1) * 512], past[0:HD, b % 2, x * 512:(x + 1) * 512]
                                          ).then_inc(high_kept, 1)
            dve.wait_ge(w_rows_in, 64)
            dve.wait_ge(sample_relu, 1)
            nc.vector.tensor_scalar(part[:, :], relus[:, 0, 0:SW], w_rows[:, 0:1], None, ALU.mult).then_inc(sample_part, 1)
            dve.wait_ge(sample_part, 1)
            dve.wait_ge(sample_relu, 2)
            nc.vector.scalar_tensor_tensor(part[:, :], relus[:, 1, 0:SW], w_rows[:, 1:2], part[:, :], ALU.mult, ALU.add
                                           ).then_inc(sample_part, 1)
            dve.wait_ge(sample_sum, 1)
            dve.wait_ge(floor_in, 16)
            nc.vector.tensor_tensor(scores[:, SLABS - 1, PAST:SW], big[:, PAST:SW], floor[:, :], ALU.add
                                    ).then_inc(sample_done, 1)
            nc.vector.tensor_copy(scores[:, SLABS - 1, 0:PAST], big[:, 0:PAST]).then_inc(sample_done, 1)
            dve.wait_ge(w_in, 16)
            for a, (t, h) in enumerate(steps):
                dve.wait_ge(relu_done, a + 1)
                n = (t + 1) * P
                sc = scores[:, t - 2, 0:n]
                if h == 0:
                    i = nc.vector.tensor_scalar(sc, relus[:, a % 3, 0:n], w[:, t, 0:1], None, ALU.mult)
                else:
                    dve.wait_ge(head_added, a)
                    i = nc.vector.scalar_tensor_tensor(sc, relus[:, a % 3, 0:n], w[:, t, h:h + 1], sc, ALU.mult, ALU.add)
                i.then_inc(head_added, 1)


SECTIONS = [("silu", 1608, 2, 0), ("silu", 3144, 2, 4), ("forget", 2120, 2, 8), ("gate", 3656, 8, 16)]
FEATS = 32


def select_keys_and_project(nc, scores, masks, hhi, hlo, w_in, feat_d):
    with Scope(nc, "sel") as s:
        raw = s.sb("raw", [P, 2, UNIT])
        whi = s.sb("whi", [P, 2, UNIT], F32R)
        wlo = s.sb("wlo", [P, 2, UNIT], F32R)
        stage = s.sb("stage", [P, 2, 2, T])
        over = s.sb("over", [P, SW], mybir.dt.bfloat16)
        equal = s.sb("equal", [P, SW], mybir.dt.bfloat16)
        rank = s.sb("rank", [P, SW])
        count = s.sb("count", [P, SLABS])
        bits = s.sb("bits", [P, SLABS], I32)
        cand = s.sb("cand", [P, SLABS], I32)
        flip = s.sb("flip", [P, SLABS], I32)
        gain = s.sb("gain", [P, SLABS], I32)
        bit = s.sb("bit", [P, SLABS], I32)
        bitf = s.sb("bitf", [P, SLABS])
        thr = s.sb("thr", [P, SLABS], I32)
        proj = s.ps("proj", [P, 2, NCH, 512])
        w_loaded = [s.sem(f"w_loaded{n}") for n in range(2)]
        w_hi_done, w_lo_done = s.sem("w_hi_done"), s.sem("w_lo_done")
        proj_done, proj_read, kept_done = s.sem("proj_done"), s.sem("proj_read"), s.sem("kept_done")
        stage_stored = [s.sem(f"stage_stored{n}") for n in range(2)]
        step, passes = s.sem("step"), s.sem("passes")
        block = s.block()
        wv = w_in[0].rearrange("(k p) f -> p k f", p=P)
        pairs_before = [sum(x[2] for x in SECTIONS[:n]) for n in range(len(SECTIONS) + 1)]
        stored_per = {"silu": 1, "forget": 2, "gate": 1}
        stored_before = [sum(x[2] * stored_per[x[0]] for x in SECTIONS[:n]) for n in range(len(SECTIONS) + 1)]

        def sections(engine, body):
            for n, (_, _, pairs, _) in enumerate(SECTIONS):
                first = 0
                if n == 0:
                    body(0, 0, 0, True)
                    first = 1
                with engine.Fori(first, pairs) as i:
                    body(n, i, i + pairs_before[n], False)

        @block.sync
        def _(sp):
            def body(n, i, pair, first):
                kind, col, _, at = SECTIONS[n]
                for u in range(2):
                    if not first:
                        sp.wait_ge(w_lo_done, 2 * pair + u - 1)
                    sp.dma_start(raw[:, u, :].rearrange("p (k f) -> p k f", k=KD), wv[:, :, DynSlice(col + (2 * i + u) * P, P)]
                                 ).then_inc(w_loaded[u], 16)

            sections(sp, body)

        @block.gpsimd
        def _(pool):
            def body(n, i, pair, first):
                for u in range(2):
                    pool.wait_ge(w_hi_done, 2 * pair + u + 1)
                    nc.gpsimd.tensor_tensor(wlo[:, u, :], raw[:, u, :], whi[:, u, :], ALU.subtract).then_inc(w_lo_done, 1)

            sections(pool, body)

        @block.tensor
        def _(pe):
            def body(n, i, pair, first):
                for u in range(2):
                    pe.wait_ge(w_lo_done, 2 * pair + u + 1)
                    for c in range(NCH):
                        cols = slice(c * CH, (c + 1) * CH)
                        if not first:
                            pe.wait_ge(proj_read, 6 * pair + 3 * u + c - 5)
                        for k in range(KD):
                            w = slice(k * P, (k + 1) * P)
                            last = split_product(nc, proj[:, u, c, 0:CH], whi[:, u, w], wlo[:, u, w], hhi[:, k, cols],
                                                 hlo[:, k, cols], k == 0, k == KD - 1)
                        last.then_inc(proj_done, 1)

            sections(pe, body)

        @block.scalar
        def _(act):
            def hi(u, pair, first):
                act.wait_ge(w_loaded[u], 16 * pair + 16)
                if not first:
                    act.wait_ge(proj_done, 6 * pair + 3 * u - 3)
                nc.scalar.activation(whi[:, u, :], raw[:, u, :], ACT.Copy).then_inc(w_hi_done, 1)

            def body(n, i, pair, first):
                kind, _, _, at = SECTIONS[n]
                for u in range(2):
                    hi(u, pair, first)
                for u in range(2):
                    if not first:
                        stored = stored_before[n] + stored_per[kind] * i
                        act.wait_ge(stage_stored[u], 16 * stored)
                    for c in range(NCH):
                        cols = slice(c * CH, (c + 1) * CH)
                        act.wait_ge(proj_done, 6 * pair + 3 * u + c + 1)
                        if kind == "forget":
                            nc.scalar.activation(stage[:, u, 1, cols], proj[:, u, c, 0:CH], ACT.Sigmoid, scale=-1.0
                                                 ).then_inc(kept_done, 1)
                        func = ACT.Silu if kind == "silu" else ACT.Sigmoid
                        nc.scalar.activation(stage[:, u, 0, cols], proj[:, u, c, 0:CH], func).then_inc(proj_read, 1)
                    act.wait_ge(proj_read, 6 * pair + 3 * u + 3)
                    act.dma_start(feat_d[DynSlice(at + 2 * i + u, 1)].rearrange("a p t -> (a p) t"), stage[:, u, 0, :]
                                  ).then_inc(stage_stored[u], 16)
                    if kind == "forget":
                        act.wait_ge(kept_done, 6 * i + 3 * u + 3)
                        act.dma_start(feat_d[DynSlice(at + 4 + 2 * i + u, 1)].rearrange("a p t -> (a p) t"),
                                      stage[:, u, 1, :]).then_inc(stage_stored[u], 16)

            sections(act, body)
            for u in range(2):
                act.wait_ge(stage_stored[u], 16 * stored_before[-1])

        @block.vector
        def _(dve):
            steps = [0]

            def count_all(r):
                for x in range(SLABS):
                    n = slab_width(x)
                    if x >= 2:
                        dve.wait_ge(passes, SLABS * r + x - 1)
                    flags = (over, equal)[x % 2]
                    nc.vector.tensor_scalar(flags[:, 0:n], scores[:, x, 0:n], thr[:, x:x + 1].bitcast(F32), None,
                                            ALU.is_ge, ALU.add, accum_out=count[:, x:x + 1]).then_inc(passes, 1)
                dve.wait_ge(passes, SLABS * (r + 1))

            def done(ins, at=None):
                ins.then_inc(step, 1)
                steps[0] += 1
                dve.wait_ge(step, steps[0] if at is None else at)

            done(nc.vector.memset(thr[:, :], 0))
            done(nc.vector.memset(bits[:, :], 0))
            done(nc.vector.memset(bit[:, :], 1 << 30))
            done(nc.vector.memset(bitf[:, :], float(1 << 30)))
            count_all(0)
            done(nc.vector.tensor_scalar(flip[:, :], count[:, :], TOPK - 0.5, -1.0, ALU.is_ge, ALU.add))
            base, per = steps[0], 7
            with dve.Fori(0, 31) as r:
                at = [per * r + (base + 1 + n) for n in range(per)]
                done(nc.vector.tensor_tensor(cand[:, :], bits[:, :], bit[:, :], ALU.bitwise_or), at[0])
                done(nc.vector.tensor_tensor(thr[:, :], cand[:, :], flip[:, :], ALU.bitwise_xor), at[1])
                count_all(r + 1)
                done(nc.vector.tensor_scalar(gain[:, :], count[:, :], TOPK - 0.5, None, ALU.is_ge), at[2])
                done(nc.vector.tensor_tensor(gain[:, :], gain[:, :], bitf[:, :], ALU.mult), at[3])
                done(nc.vector.tensor_tensor(bits[:, :], bits[:, :], gain[:, :], ALU.bitwise_or), at[4])
                done(nc.vector.tensor_scalar(bit[:, :], bit[:, :], 1, None, ALU.logical_shift_right), at[5])
                done(nc.vector.tensor_scalar(bitf[:, :], bitf[:, :], 0.5, None, ALU.mult), at[6])
            steps[0] = base + per * 31
            done(nc.vector.tensor_tensor(thr[:, :], bits[:, :], flip[:, :], ALU.bitwise_xor))
            for x in range(SLABS):
                n = slab_width(x)
                sc, t = scores[:, x, 0:n], thr[:, x:x + 1].bitcast(F32)
                done(nc.vector.tensor_scalar(over[:, 0:n], sc, t, None, ALU.is_gt, ALU.add, accum_out=count[:, x:x + 1]))
                done(nc.vector.tensor_scalar(count[:, x:x + 1], count[:, x:x + 1], -1.0, float(TOPK), ALU.mult, ALU.add))
                done(nc.vector.tensor_scalar(equal[:, 0:n], sc, t, None, ALU.is_equal))
                done(nc.vector.tensor_tensor_scan(rank[:, 0:n], equal[:, 0:n], equal[:, 0:n], 0.0, ALU.add, ALU.max))
                done(nc.vector.scalar_tensor_tensor(equal[:, 0:n], rank[:, 0:n], count[:, x:x + 1], equal[:, 0:n],
                                                    ALU.is_le, ALU.mult))
                done(nc.vector.scalar_tensor_tensor(over[:, 0:n], equal[:, 0:n], -1.0, over[:, 0:n], ALU.add, ALU.add))
                done(nc.vector.tensor_scalar(masks[:, x, 0:n], over[:, 0:n], -MASKED, None, ALU.mult))


def attention(nc, mixed_d, masks, qT_d, kT_d, v_prompt, v_sample, cache_k, cache_v, page_table, causal, own, ident):
    with Scope(nc, "att") as s:
        attT = s.sb("attT", [P, 4, T])
        qT = s.sb("qT", [P, 4, T])
        kT = s.sb("kT", [P, 2, T])
        v = s.sb("v", [P, TILES, KV * HD])
        v_new = s.sb("v_new", [NS, KV * HD])
        causal_sb = s.sb("causal", [P, 2 * P])
        own_sb = s.sb("own", [P, DB, DT])
        table = s.sb("table", [1, DB * PAGES], I32)
        wide = s.sb("wide", [P, DB * PADB])
        pages = s.sb("pages", [P, 2, PAGES, KV * HD])
        past = s.sb("past", [P, 2, 2, PAST])
        logits = s.sb("logits", [P, 2, SW])
        probs = s.sb("probs", [P, 2, SW])
        new_probs = s.sb("new_probs", [P, 2, DB, DT])
        probsT = s.sb("probsT", [P, 2, PAGES, P])
        new_probsT = s.sb("new_probsT", [NS, 2, P])
        top = s.sb("top", [P, 2])
        bias = s.sb("bias", [P, 2])
        mass = s.sb("mass", [P, 2, HEADS])
        share = s.sb("share", [P, HEADS])
        heads = s.sb("heads", [P, HEADS * HD])
        big = s.ps("big", [P, 6 * 512])
        turned = s.ps("turned", [P, 2, 512])
        names = ("table", "qT", "kT", "v", "v_new", "causal", "own")
        loaded = {n: s.sem(f"{n}_in") for n in names}
        pages_in = [s.sem(f"pages_in{n}") for n in range(2)]
        zeroed, spread_done = s.sem("zeroed"), s.sem("spread_done")
        page_turned, low_kept, high_kept = s.sem("page_turned"), s.sem("low_kept"), s.sem("high_kept")
        seq_scored, s_logits, s_bias, s_exp, s_norm = (s.sem("seq_scored"), s.sem("s_logits"), s.sem("s_bias"),
                                                       s.sem("s_exp"), s.sem("s_norm"))
        s_share, s_new, s_out, s_kept = s.sem("s_share"), s.sem("s_new"), s.sem("s_out"), s.sem("s_kept")
        new_turned, new_kept = s.sem("new_turned"), s.sem("new_kept")
        scored, masked, top_done, bias_done, exp_done = (s.sem("scored"), s.sem("masked"), s.sem("top_done"),
                                                         s.sem("bias_done"), s.sem("exp_done"))
        low_turned, high_turned, low_ready, high_ready = (s.sem("low_turned"), s.sem("high_turned"), s.sem("low_ready"),
                                                          s.sem("high_ready"))
        mixed, share_done, heads_done, out_turned, out_kept = (s.sem("mixed"), s.sem("share_done"), s.sem("heads_done"),
                                                               s.sem("out_turned"), s.sem("out_kept"))
        stored = s.sem("stored")
        block = s.block()
        steps = [(t, h) for t in range(TILES) for h in range(HEADS)]
        SCALE = HD ** -0.5
        out_ps = big[:, 4 * 512:5 * 512]
        back_ps = big[:, 5 * 512:6 * 512]

        def high_before(a):
            return sum(1 for t, _ in steps[:a] if t >= 4)

        @block.sync
        def _(sp):
            for n, dst, src in (("table", table[:, :], page_table.rearrange("(a b) n -> a (b n)", a=1)),
                                ("qT", qT[:, :, :], qT_d.rearrange("b p t -> p b t")),
                                ("kT", kT[:, :, :], kT_d.rearrange("b p t -> p b t"))):
                sp.dma_start(dst, src).then_inc(loaded[n], 16)
            sp.wait_ge(loaded["table"], 16)

            def load(cache, i, n, sem=None, value=None):
                if sem is not None:
                    sp.wait_ge(sem, value)
                for g in range(PAGES):
                    page = sp.value_load(table[0:1, DynSlice(PAGES * (2 * i + n) + g, 1)], min_val=0, max_val=N_POOL - 1)
                    sp.dma_start(pages[:, n, g, :], cache[DynSlice(page, 1)].rearrange("a s d -> (a s) d")
                                 ).then_inc(pages_in[n], 16)

            load(cache_k, 0, 0)
            load(cache_k, 0, 1)
            for n, dst, src in (("v", v[:, :, :], v_prompt.rearrange("(n p) d -> p n d", p=P)),
                                ("v_new", v_new[:, :], v_sample), ("causal", causal_sb[:, :], causal),
                                ("own", own_sb[:, :, :], own)):
                sp.dma_start(dst, src).then_inc(loaded[n], 16)
            with sp.Fori(1, DB // 2) as i:
                for n in range(2):
                    load(cache_k, i, n, page_turned, 8 * i - 4 + 4 * n)
            for n in range(2):
                load(cache_v, 0, n, page_turned, 4 * (DB - 1 + n))
            with sp.Fori(1, DB // 2) as i:
                for n in range(2):
                    load(cache_v, i, n, s_out, 2 * i - 1 + n)
            sp.wait_ge(s_kept, 2)
            sp.wait_ge(out_kept, TILES)
            sp.dma_start(mixed_d[0:4].rearrange("b p t -> p b t"), attT[:, :, :]).then_inc(stored, 16)
            sp.wait_ge(stored, 16)

        @block.tensor
        def _(pe):
            def turn(b):
                pe.wait_ge(pages_in[b % 2], 16 * PAGES * (b // 2 + 1))
                for f in range(4):
                    x = f % 2
                    if 2 * b + f // 2:
                        pe.wait_ge((low_kept, high_kept)[x], 2 * b + f // 2)
                    for g in range(4):
                        last = nc.tensor.transpose(turned[:, x, g * PS:(g + 1) * PS],
                                                   pages[:, b % 2, 4 * x + g, f // 2 * P:(f // 2 + 1) * P], ident[:, :])
                    last.then_inc(page_turned, 1)

            turn(0)
            pe.wait_ge(spread_done, 1)
            pe.wait_ge(loaded["kT"], 16)
            for b in range(DB):
                if b + 1 < DB:
                    turn(b + 1)
                pe.wait_ge(low_kept, 2 * b + 2)
                pe.wait_ge(high_kept, 2 * b + 2)
                for G in range(2):
                    for g in range(2):
                        r = slice(g * HD, (g + 1) * HD)
                        q = wide[r, b * P + G * 2 * NS:b * P + (G + 1) * 2 * NS]
                        for x in range(2):
                            nc.tensor.matmul(big[r, (3 * G + x) * 512:(3 * G + x + 1) * 512], q,
                                             past[r, b % 2, G, x * 512:(x + 1) * 512], start=(b == 0), stop=(b == DB - 1))
                        last = nc.tensor.matmul(big[r, (3 * G + 2) * 512:(3 * G + 2) * 512 + DT], q,
                                                kT[r, G, SEQ + DT * b:SEQ + DT * (b + 1)], start=(b == 0),
                                                stop=(b == DB - 1))
                last.then_inc(seq_scored, 1)
            for f in range(4):
                G, x = f // 2, f % 2
                pe.wait_ge(s_norm, G + 1)
                pe.wait_ge((low_kept, high_kept)[x], 2 * DB + G)
                for g in range(4):
                    last = nc.tensor.transpose(turned[:, x, g * P:(g + 1) * P],
                                               probs[:, G, (4 * x + g) * PS:(4 * x + g + 1) * PS], ident[:, :])
                last.then_inc(page_turned, 1)
            pe.wait_ge(s_new, 2)
            pe.wait_ge(s_logits, 2)
            for G in range(2):
                last = nc.tensor.transpose(big[0:NS, 512 + G * P:512 + (G + 1) * P],
                                           new_probs[:, G, :, :].rearrange("p b j -> p (b j)"), ident[:, :])
            last.then_inc(new_turned, 1)
            pe.wait_ge(new_kept, 1)
            pe.wait_ge(loaded["v_new"], 16)
            for G in range(2):
                for g in range(2):
                    r = slice(g * HD, (g + 1) * HD)
                    kv = 2 * G + g
                    nc.tensor.matmul(big[r, 3 * G * 512:3 * G * 512 + 2 * NS], v_new[:, kv * HD:(kv + 1) * HD],
                                     new_probsT[:, G, r], start=True, stop=False)
            pe.wait_ge(low_kept, 2 * DB + 2)
            pe.wait_ge(high_kept, 2 * DB + 2)
            for b in range(DB):
                pe.wait_ge(pages_in[b % 2], 16 * PAGES * (DB // 2 + b // 2 + 1))
                for G in range(2):
                    for g in range(2):
                        r = slice(g * HD, (g + 1) * HD)
                        kv = 2 * G + g
                        o = big[r, 3 * G * 512:3 * G * 512 + 2 * NS].rearrange("p (r t) -> p r t", t=NS)
                        for n in range(PAGES):
                            p = probsT[:, G, n, r].rearrange("p (r t) -> p r t", t=NS)
                            last = nc.tensor.matmul(o[:, :, DT * b:DT * (b + 1)], pages[:, b % 2, n, kv * HD:(kv + 1) * HD],
                                                    p[:, :, DT * b:DT * (b + 1)], start=False,
                                                    stop=(b == DB - 1 and n == PAGES - 1))
                last.then_inc(s_out, 1)

            def score(a):
                t, h = steps[a]
                if a < 2:
                    pe.wait_ge(s_kept, 2)
                else:
                    pe.wait_ge(masked, a - 1)
                g, rr = h // 2, h % 2
                r = slice(g % 2 * HD, (g % 2 + 1) * HD)
                for x in range(0, (t + 1) * P, 512):
                    n = min(512, (t + 1) * P - x)
                    last = nc.tensor.matmul(big[:, a % 2 * 1024 + x:a % 2 * 1024 + x + n],
                                            qT[r, g // 2 * 2 + rr, t * P:(t + 1) * P], kT[r, g // 2, x:x + n],
                                            start=True, stop=True)
                last.then_inc(scored, 1)

            def turn_probs(a):
                t, h = steps[a]
                pe.wait_ge(exp_done, a + 1)
                for x in range(1 if t < 4 else 2):
                    if x == 0 and a:
                        pe.wait_ge(low_ready, a)
                    if x == 1 and high_before(a):
                        pe.wait_ge(high_ready, high_before(a))
                    for j in range(4 * x, min(4 * x + 4, t + 1)):
                        last = nc.tensor.transpose(turned[:, x, (j - 4 * x) * P:(j - 4 * x + 1) * P],
                                                   probs[:, a % 2, j * P:(j + 1) * P], ident[:, :])
                    last.then_inc((low_turned, high_turned)[x], 1)

            def mix(a):
                t, h = steps[a]
                if h == 0 and t:
                    pe.wait_ge(heads_done, 2 * t)
                pe.wait_ge(low_ready, a + 1)
                if t >= 4:
                    pe.wait_ge(high_ready, high_before(a + 1))
                for j in range(t + 1):
                    last = nc.tensor.matmul(out_ps[:, h * HD:(h + 1) * HD], probsT[:, a % 2, j, :],
                                            v[:, j, h // 2 * HD:(h // 2 + 1) * HD], start=(j == 0), stop=(j == t))
                last.then_inc(mixed, 1)

            def turn_out(t):
                pe.wait_ge(heads_done, 2 * t + 2)
                if t:
                    pe.wait_ge(out_kept, t)
                for n in range(4):
                    last = nc.tensor.transpose(back_ps[:, n * P:(n + 1) * P], heads[:, n * P:(n + 1) * P], ident[:, :])
                last.then_inc(out_turned, 1)

            pe.wait_ge(loaded["v"], 16)
            for a in range(len(steps) + 4):
                if a < len(steps):
                    score(a)
                if 1 <= a <= len(steps):
                    turn_probs(a - 1)
                if 2 <= a <= len(steps) + 1:
                    mix(a - 2)
                if a >= 11 and (a - 3) % HEADS == 0:
                    turn_out((a - 3) // HEADS - 1)

        @block.scalar
        def _(act):
            act.wait_ge(spread_done, 1)
            for b in range(DB):
                for G in range(2):
                    act.wait_ge(page_turned, 4 * b + 2 * G + 2)
                    if b >= 2:
                        act.wait_ge(seq_scored, b - 1)
                    nc.scalar.activation(past[:, b % 2, G, 512:1024], turned[:, 1, :], ACT.Copy).then_inc(high_kept, 1)
            for G in range(2):
                act.wait_ge(s_bias, G + 1)
                nc.scalar.activation(probs[:, G, :], logits[:, G, :], ACT.Exp, bias=bias[:, G:G + 1], scale=SCALE,
                                     accum_out=mass[:, 0, G:G + 1]).then_inc(s_exp, 1)
            for G in range(2):
                act.wait_ge(page_turned, 4 * DB + 2 * G + 2)
                nc.scalar.activation(probsT[:, G, 4:8, :].rearrange("p a b -> p (a b)"), turned[:, 1, :], ACT.Copy
                                     ).then_inc(high_kept, 1)
            act.wait_ge(s_out, DB)
            for G in range(2):
                nc.scalar.activation(attT[:, 2 * G:2 * G + 2, SEQ:T],
                                     big[:, 3 * G * 512:3 * G * 512 + 2 * NS].rearrange("p (r t) -> p r t", t=NS), ACT.Copy
                                     ).then_inc(s_kept, 1)
            for a in range(len(steps) + 4):
                if a < len(steps):
                    t, h = steps[a]
                    n = (t + 1) * P
                    act.wait_ge(bias_done, a + 1)
                    if a < 2:
                        act.wait_ge(s_out, DB)
                    else:
                        act.wait_ge(low_turned, a - 1)
                        if high_before(a - 1):
                            act.wait_ge(high_turned, high_before(a - 1))
                    if h == 0 and t >= 2:
                        act.wait_ge(share_done, t - 1)
                    nc.scalar.activation(probs[:, a % 2, 0:n], logits[:, a % 2, 0:n], ACT.Exp, bias=bias[:, a % 2:a % 2 + 1],
                                         scale=SCALE, accum_out=mass[:, t % 2, h:h + 1]).then_inc(exp_done, 1)
                if 1 <= a <= len(steps) and steps[a - 1][0] >= 4:
                    t, h = steps[a - 1]
                    act.wait_ge(high_turned, high_before(a))
                    if a >= 3:
                        act.wait_ge(mixed, a - 2)
                    nc.scalar.activation(probsT[:, (a - 1) % 2, 4:t + 1, :],
                                         turned[:, 1, 0:(t - 3) * P].rearrange("p (a b) -> p a b", b=P), ACT.Copy
                                         ).then_inc(high_ready, 1)
                if a >= 11 and (a - 3) % HEADS == 0:
                    t = (a - 3) // HEADS - 1
                    act.wait_ge(out_turned, t + 1)
                    nc.scalar.activation(attT[:, :, t * P:(t + 1) * P], back_ps.rearrange("p (a b) -> p a b", b=P), ACT.Copy
                                         ).then_inc(out_kept, 1)

        @block.vector
        def _(dve):
            nc.vector.memset(wide[:, :], 0.0).then_inc(zeroed, 1)
            dve.wait_ge(zeroed, 1)
            dve.wait_ge(loaded["qT"], 16)
            nc.vector.tensor_copy(spread(wide), qT[:, :, SEQ:T].rearrange("p h (b j) -> p b h j", j=DT)
                                  ).then_inc(spread_done, 1)
            for b in range(DB):
                for G in range(2):
                    dve.wait_ge(page_turned, 4 * b + 2 * G + 1)
                    if b >= 2:
                        dve.wait_ge(seq_scored, b - 1)
                    nc.vector.tensor_copy(past[:, b % 2, G, 0:512], turned[:, 0, :]).then_inc(low_kept, 1)
            dve.wait_ge(seq_scored, DB)
            for G in range(2):
                nc.vector.tensor_tensor_reduce(logits[:, G, :], masks[:, SLABS - 1, :], big[:, 1536 * G:1536 * G + SW], 1.0,
                                               FLOOR, ALU.add, ALU.max, top[:, G:G + 1]).then_inc(s_logits, 1)
                dve.wait_ge(s_logits, G + 1)
                nc.vector.tensor_scalar(bias[:, G:G + 1], top[:, G:G + 1], -SCALE, None, ALU.mult).then_inc(s_bias, 1)
            dve.wait_ge(loaded["own"], 16)
            for G in range(2):
                dve.wait_ge(s_exp, G + 1)
                nc.vector.reciprocal(share[:, G:G + 1], mass[:, 0, G:G + 1]).then_inc(s_share, 1)
                dve.wait_ge(s_share, G + 1)
                nc.vector.tensor_scalar(probs[:, G, :], probs[:, G, :], share[:, G:G + 1], None, ALU.mult).then_inc(s_norm, 1)
                dve.wait_ge(s_norm, G + 1)
                nc.vector.tensor_tensor(new_probs[:, G, :, :], own_sb[:, :, :],
                                        probs[:, G, PAST:SW].unsqueeze(1).broadcast_to([P, DB, DT]), ALU.mult
                                        ).then_inc(s_new, 1)
            for G in range(2):
                dve.wait_ge(page_turned, 4 * DB + 2 * G + 1)
                nc.vector.tensor_copy(probsT[:, G, 0:4, :].rearrange("p a b -> p (a b)"), turned[:, 0, :]
                                      ).then_inc(low_kept, 1)
            dve.wait_ge(new_turned, 1)
            nc.vector.tensor_copy(new_probsT[:, :, :].rearrange("p a b -> p (a b)"), big[0:NS, 512:512 + 2 * P]
                                  ).then_inc(new_kept, 1)
            dve.wait_ge(loaded["causal"], 16)
            for a in range(len(steps) + 4):
                if a < len(steps):
                    t, h = steps[a]
                    n = (t + 1) * P
                    dve.wait_ge(scored, a + 1)
                    if a < 2:
                        dve.wait_ge(s_exp, 2)
                    else:
                        dve.wait_ge(exp_done, a - 1)
                    m = masks[:, t - 2, 0:n] if t >= 2 else causal_sb[:, (1 - t) * P:2 * P]
                    nc.vector.tensor_tensor_reduce(logits[:, a % 2, 0:n], m, big[:, a % 2 * 1024:a % 2 * 1024 + n], 1.0,
                                                   FLOOR, ALU.add, ALU.max, top[:, a % 2:a % 2 + 1]).then_inc(masked, 1)
                    dve.wait_ge(masked, a + 1)
                    nc.vector.tensor_scalar(bias[:, a % 2:a % 2 + 1], top[:, a % 2:a % 2 + 1], -SCALE, None, ALU.mult
                                            ).then_inc(bias_done, 1)
                if 1 <= a <= len(steps):
                    t, h = steps[a - 1]
                    n = min(t + 1, 4)
                    dve.wait_ge(low_turned, a)
                    if a == 1:
                        dve.wait_ge(s_out, DB)
                    if a >= 3:
                        dve.wait_ge(mixed, a - 2)
                    nc.vector.tensor_copy(probsT[:, (a - 1) % 2, 0:n, :],
                                          turned[:, 0, 0:n * P].rearrange("p (a b) -> p a b", b=P)).then_inc(low_ready, 1)
                if a >= 10 and (a - 2) % HEADS == 0:
                    t = (a - 2) // HEADS - 1
                    if t:
                        dve.wait_ge(heads_done, 2 * t)
                    nc.vector.reciprocal(share[:, :], mass[:, t % 2, :]).then_inc(share_done, 1)
                    dve.wait_ge(share_done, t + 1)
                    dve.wait_ge(mixed, HEADS * (t + 1))
                    if t:
                        dve.wait_ge(out_turned, t)
                    half = HEADS * HD // 2
                    for G in range(2):
                        src = out_ps[:, G * half:(G + 1) * half].rearrange("p (g r d) -> p g r d", g=2, r=2)
                        dst = heads[:, G * half:(G + 1) * half].rearrange("p (r g d) -> p g r d", g=2, r=2)
                        w = share[:, 4 * G:4 * G + 4].rearrange("p (g r) -> p g r", g=2).unsqueeze(3)
                        nc.vector.tensor_tensor(dst, src, w.broadcast_to([P, 2, 2, HD]), ALU.mult).then_inc(heads_done, 1)


HG = 4
LEVELS = [64, 32, 16, 8, 4, 2, 1]
NL = len(LEVELS) + 1


def recurrence(nc, mixed_d, feat_d, hv_d, state_in, state_prompt, state_sample, bound, hg_gain, resets, level_masks, owner,
               ident, ones):
    with Scope(nc, "hg") as s:
        silu_q = s.sb("silu_q", [P, T])
        gate = s.sb("gate", [P, T])
        sig = s.sb("sig", [P, T])
        sig_neg = s.sb("sig_neg", [P, T])
        hv = s.sb("hv", [P, TT, P])
        st = s.sb("st", [P, DB, P])
        f = s.sb("f", [P, T])
        logf = s.sb("logf", [P, T])
        G = s.sb("G", [P, T])
        eG = s.sb("eG", [P, T])
        q_in = s.sb("q_in", [P, T])
        kd = s.sb("kd", [P, T])
        dist = s.sb("dist", [P, 2, T])
        decay = s.sb("decay", [P, 2, T])
        qL = s.sb("qL", [P, NL, T])
        kL = s.sb("kL", [P, NL, T])
        kept = s.sb("kept", [P, NL, P])
        attn = s.sb("attn", [P, 2, P])
        kdT = s.sb("kdT", [P, 2, P])
        S = s.sb("S", [P, 2, P])
        own_v = s.sb("own_v", [NS, DB, P])
        new_st = s.sb("new_st", [P, DB, P])
        oT = s.sb("oT", [P, T])
        rec = s.sb("rec", [P, T])
        reset = s.sb("reset", [P, T])
        masks = s.sb("masks", [P, NL, P])
        own = s.sb("own", [NS, DB])
        lb_in = s.sb("lb_in", [P, 2, HG])
        lb = s.sb("lb", [P, HG])
        omlb = s.sb("omlb", [P, HG])
        lmax = s.sb("lmax", [P, HG])
        lexp = s.sb("lexp", [P, 2, HG])
        lsum = s.sb("lsum", [P, HG])
        gain = s.sb("gain", [P, 1])
        pairs = s.ps("pairs", [P, NL, P])
        o_ps = s.ps("o_ps", [P, 512])
        kd_ps = s.ps("kd_ps", [P, 512])
        st_ps = s.ps("st_ps", [P, 512])
        sum_ps = s.ps("sum_ps", [P, NCH, 512])
        q_loaded, gate_loaded, f_loaded, hv_loaded, st_loaded = (s.sem("q_loaded"), s.sem("gate_loaded"), s.sem("f_loaded"),
                                                                 s.sem("hv_loaded"), s.sem("st_loaded"))
        consts = s.sem("consts")
        bound_step, bound_exp, bound_ready = s.sem("bound_step"), s.sem("bound_exp"), s.sem("bound_ready")
        f_ready, log_ready, G_ready, eG_ready = s.sem("f_ready"), s.sem("log_ready"), s.sem("G_ready"), s.sem("eG_ready")
        q_ready, k_ready, q_in_ready = s.sem("q_ready"), s.sem("k_ready"), s.sem("q_in_ready")
        dist_ready, decay_ready, qL_ready, kL_ready = (s.sem("dist_ready"), s.sem("decay_ready"), s.sem("qL_ready"),
                                                       s.sem("kL_ready"))
        pairs_done, kept_done, attn_done = s.sem("pairs_done"), s.sem("kept_done"), s.sem("attn_done")
        kd_turned, kdT_ready, o_done, o_kept = s.sem("kd_turned"), s.sem("kdT_ready"), s.sem("o_done"), s.sem("o_kept")
        st_done, S_ready = s.sem("st_done"), s.sem("S_ready")
        own_ready, new_done, new_scaled, new_ready, new_stored = (s.sem("own_ready"), s.sem("new_done"), s.sem("new_scaled"),
                                                                  s.sem("new_ready"), s.sem("new_stored"))
        S_stored, rec_stored = s.sem("S_stored"), s.sem("rec_stored")
        factor_ready = s.sem("factor_ready")
        squared, summed, var_ready, inv_ready, rooted, root_ready, normed, rec_ready, nstep = (
            s.sem("squared"), s.sem("summed"), s.sem("var_ready"), s.sem("inv_ready"), s.sem("rooted"), s.sem("root_ready"),
            s.sem("normed"), s.sem("rec_ready"), s.sem("nstep"))
        block = s.block()
        sq, var, inv, root, tmp = f, logf, dist[:, 0, :], dist[:, 1, :], decay[:, 0, :]

        def heads(engine, body):
            body(0, True)
            with engine.Fori(1, HG) as h:
                body(h, False)

        def tile(n):
            return slice(n * P, (n + 1) * P) if n < TILES else slice(SEQ, T)

        @block.sync
        def _(sp):
            sp.dma_start(lb_in[:, :, :], bound).then_inc(consts, 16)
            sp.dma_start(gain[:, :], hg_gain).then_inc(consts, 16)
            sp.dma_start(reset[:, :], resets).then_inc(consts, 16)
            sp.dma_start(masks[:, :, :], level_masks).then_inc(consts, 16)
            sp.dma_start(own[:, :], owner).then_inc(consts, 16)

            def body(h, first):
                def feat(b, dst, sem):
                    sp.dma_start(dst[:, :], feat_d[DynSlice(b + h, 1)].rearrange("a p t -> (a p) t")).then_inc(sem, 16)

                if not first:
                    sp.wait_ge(f_ready, h)
                    sp.wait_ge(k_ready, h)
                feat(8, sig, f_loaded)
                feat(12, sig_neg, f_loaded)
                if not first:
                    sp.wait_ge(q_ready, h)
                feat(0, silu_q, q_loaded)
                if not first:
                    sp.wait_ge(o_done, TT * h)
                    sp.wait_ge(new_done, h)
                sp.dma_start(hv[:, 0:TILES, :], hv_d[0:SEQ, DynSlice(P * h, P)].rearrange("(n p) v -> p n v", p=P)
                             ).then_inc(hv_loaded, 16)
                sp.dma_start(hv[0:NS, TILES, :], hv_d[SEQ:T, DynSlice(P * h, P)]).then_inc(hv_loaded, 16)
                if not first:
                    sp.wait_ge(new_ready, h)
                sp.dma_start(st[:, :, :], state_in[DynSlice(h, 1)].rearrange("a k b v -> (a k) b v")).then_inc(st_loaded, 16)
                if not first:
                    sp.wait_ge(rec_ready, h)
                feat(4, gate, gate_loaded)
                sp.wait_ge(S_ready, TILES * h + TILES)
                sp.dma_start(state_prompt[DynSlice(h, 1)].rearrange("a k v -> (a k) v"), S[:, 1, :]).then_inc(S_stored, 16)
                sp.wait_ge(new_ready, h + 1)
                sp.dma_start(state_sample[DynSlice(h, 1)].rearrange("a k b v -> (a k) b v"), new_st[:, :, :]
                             ).then_inc(new_stored, 16)
                sp.wait_ge(rec_ready, h + 1)
                sp.dma_start(mixed_d[DynSlice(h + 4, 1)].rearrange("a p t -> (a p) t"), rec[:, :]).then_inc(rec_stored, 16)

            heads(sp, body)
            sp.wait_ge(rec_stored, 16 * HG)
            sp.wait_ge(S_stored, 16 * HG)
            sp.wait_ge(new_stored, 16 * HG)

        @block.gpsimd
        def _(pool):
            def body(h, first):
                pool.wait_ge(k_ready, h + 1)
                for n in range(NL):
                    pool.wait_ge(decay_ready, 15 * h + (1 if n == 0 else 2 * n + 1))
                    if n == 0:
                        if not first:
                            pool.wait_ge(kd_turned, TT * h)
                        dst, cols = kd[:, :], slice(0, T)
                    else:
                        cols = slice(0, T if LEVELS[n - 1] <= 2 else SEQ)
                        dst = kL[:, n - 1, cols]
                    nc.gpsimd.tensor_tensor(dst, kL[:, NL - 1, cols], decay[:, n % 2, cols], ALU.mult).then_inc(kL_ready, 1)
                pool.wait_ge(rooted, h + 1)
                pool.wait_ge(kL_ready, NL * h + NL)
                nc.gpsimd.tensor_tensor(tmp, root, root, ALU.mult).then_inc(nstep, 1)
                pool.wait_ge(nstep, 2 * h + 1)
                nc.gpsimd.tensor_tensor(tmp, tmp, var[:, :], ALU.mult).then_inc(nstep, 1)
                pool.wait_ge(factor_ready, h + 1)
                nc.gpsimd.tensor_tensor(root, root, tmp, ALU.mult).then_inc(root_ready, 1)

            heads(pool, body)

        @block.scalar
        def _(act):
            act.wait_ge(bound_step, 3)
            for n in range(2):
                nc.scalar.activation(lexp[:, n, :], lb_in[:, n, :], ACT.Exp).then_inc(bound_exp, 1)

            def body(h, first):
                act.wait_ge(f_loaded, 32 * h + 32)
                if first:
                    act.wait_ge(bound_ready, 2)
                else:
                    act.wait_ge(kL_ready, NL * h)
                    act.wait_ge(pairs_done, TT * h)
                nc.scalar.activation(kL[:, NL - 1, :], sig_neg[:, :], ACT.Copy, scale=omlb[:, DynSlice(h, 1)]
                                     ).then_inc(k_ready, 1)
                act.wait_ge(f_ready, h + 1)
                if not first:
                    act.wait_ge(root_ready, h)
                nc.scalar.activation(logf[:, :], f[:, :], ACT.Ln).then_inc(log_ready, 1)
                act.wait_ge(G_ready, h + 1)
                if not first:
                    act.wait_ge(S_ready, TILES * h)
                    act.wait_ge(new_scaled, h)
                nc.scalar.activation(eG[:, :], G[:, :], ACT.Exp).then_inc(eG_ready, 1)
                for n in range(NL):
                    act.wait_ge(dist_ready, (NL + 1) * h + n + 2)
                    if n >= 2 or not first:
                        act.wait_ge(kL_ready, NL * h + n - 1)
                        act.wait_ge(qL_ready, (NL - 1) * h + max(n - 2, 0))
                    if n == 0:
                        nc.scalar.activation(decay[:, 0, :], dist[:, 0, :], ACT.Exp, scale=-1.0).then_inc(decay_ready, 1)
                    else:
                        b = LEVELS[n - 1]
                        w = T if b <= 2 else SEQ
                        e = decay[:, n % 2, 0:w].rearrange("p (n b) -> p n b", b=2 * b)
                        d = dist[:, n % 2, 0:w].rearrange("p (n b) -> p n b", b=2 * b)
                        nc.scalar.activation(e[:, :, b:2 * b], d[:, :, b:2 * b], ACT.Exp).then_inc(decay_ready, 1)
                        nc.scalar.activation(e[:, :, 0:b], d[:, :, 0:b], ACT.Exp, scale=-1.0).then_inc(decay_ready, 1)
                for n in range(TT):
                    w = P if n < TILES else NS
                    act.wait_ge(kd_turned, TT * h + n + 1)
                    if n >= 2:
                        act.wait_ge(st_done, TILES * h + n - 1)
                    elif not first:
                        act.wait_ge(st_done, TILES * h)
                        act.wait_ge(new_done, h)
                    nc.scalar.activation(kdT[0:w, n % 2, :], kd_ps[0:w, 0:P], ACT.Copy).then_inc(kdT_ready, 1)
                    act.wait_ge(o_done, TT * h + n + 1)
                    if n == 0 and not first:
                        act.wait_ge(normed, h)
                    nc.scalar.activation(oT[:, tile(n)], o_ps[:, 0:w], ACT.Copy).then_inc(o_kept, 1)
                act.wait_ge(o_kept, TT * h + TT)
                nc.scalar.activation(sq[:, :], oT[:, :], ACT.Square).then_inc(squared, 1)
                act.wait_ge(inv_ready, h + 1)
                nc.scalar.activation(root, inv, ACT.Sqrt).then_inc(rooted, 1)

            heads(act, body)

        @block.vector
        def _(dve):
            dve.wait_ge(consts, 80)
            nc.vector.tensor_tensor(lmax[:, :], lb_in[:, 0, :], lb_in[:, 1, :], ALU.max).then_inc(bound_step, 1)
            dve.wait_ge(bound_step, 1)
            nc.vector.tensor_tensor(lb_in[:, 0, :], lb_in[:, 0, :], lmax[:, :], ALU.subtract).then_inc(bound_step, 1)
            nc.vector.tensor_tensor(lb_in[:, 1, :], lb_in[:, 1, :], lmax[:, :], ALU.subtract).then_inc(bound_step, 1)
            dve.wait_ge(bound_exp, 2)
            nc.vector.tensor_tensor(lsum[:, :], lexp[:, 0, :], lexp[:, 1, :], ALU.add).then_inc(bound_step, 1)
            dve.wait_ge(bound_step, 4)
            nc.vector.reciprocal(lmax[:, :], lsum[:, :]).then_inc(bound_step, 1)
            dve.wait_ge(bound_step, 5)
            nc.vector.tensor_tensor(lb[:, :], lexp[:, 0, :], lmax[:, :], ALU.mult).then_inc(bound_ready, 1)
            dve.wait_ge(bound_ready, 1)
            nc.vector.tensor_scalar(omlb[:, :], lb[:, :], -1.0, 1.0, ALU.mult, ALU.add).then_inc(bound_ready, 1)
            dve.wait_ge(bound_ready, 2)

            def body(h, first):
                dve.wait_ge(f_loaded, 32 * h + 32)
                if not first:
                    dve.wait_ge(summed, h)
                nc.vector.tensor_scalar(f[:, :], sig[:, :], omlb[:, DynSlice(h, 1)], lb[:, DynSlice(h, 1)], ALU.mult, ALU.add
                                        ).then_inc(f_ready, 1)
                dve.wait_ge(q_loaded, 16 * h + 16)
                if not first:
                    dve.wait_ge(pairs_done, TT * h)
                nc.vector.tensor_scalar(qL[:, NL - 1, :], silu_q[:, :], float(P) ** -0.5, None, ALU.mult).then_inc(q_ready, 1)
                dve.wait_ge(log_ready, h + 1)
                nc.vector.tensor_tensor_scan(G[:, :], reset[:, :], logf[:, :], 0.0, ALU.mult, ALU.add).then_inc(G_ready, 1)
                dve.wait_ge(G_ready, h + 1)
                dve.wait_ge(q_ready, h + 1)

                def distance(n):
                    if n >= 2:
                        dve.wait_ge(decay_ready, 15 * h + (1 if n == 2 else 2 * n - 3))
                    elif not first:
                        dve.wait_ge(root_ready, h)
                        dve.wait_ge(normed, h)
                    if n == 0:
                        parts = [(0, SEQ, P, P - 1), (SEQ, T, DT, DT - 1)]
                    else:
                        b = LEVELS[n - 1]
                        parts = [(0, T if b <= 2 else SEQ, 2 * b, b - 1)]
                    for lo, hi, b, at in parts:
                        g = G[:, lo:hi].rearrange("p (n b) -> p n b", b=b)
                        d = dist[:, n % 2, lo:hi].rearrange("p (n b) -> p n b", b=b)
                        nc.vector.tensor_tensor(d, g, g[:, :, at:at + 1].broadcast_to([P, (hi - lo) // b, b]), ALU.subtract
                                                ).then_inc(dist_ready, 1)

                distance(0)
                distance(1)
                dve.wait_ge(eG_ready, h + 1)
                if not first:
                    dve.wait_ge(o_done, TT * h)
                nc.vector.tensor_tensor(q_in[:, :], qL[:, NL - 1, :], eG[:, :], ALU.mult).then_inc(q_in_ready, 1)
                for n in range(1, NL):
                    if n + 1 < NL:
                        distance(n + 1)
                    dve.wait_ge(decay_ready, 15 * h + 2 * n + 1)
                    cols = slice(0, T if LEVELS[n - 1] <= 2 else SEQ)
                    nc.vector.tensor_tensor(qL[:, n - 1, cols], qL[:, NL - 1, cols], decay[:, n % 2, cols], ALU.mult
                                            ).then_inc(qL_ready, 1)
                for n in range(TT):
                    w = P if n < TILES else NS
                    lv = 0 if n < TILES else NL - 3
                    dve.wait_ge(pairs_done, TT * h + n + 1)
                    if n or not first:
                        dve.wait_ge(attn_done, TT * h + n)
                    nc.vector.tensor_tensor(kept[0:w, lv:NL, 0:w], pairs[0:w, lv:NL, 0:w], masks[0:w, lv:NL, 0:w], ALU.mult
                                            ).then_inc(kept_done, 1)
                    dve.wait_ge(kept_done, TT * h + n + 1)
                    if n >= 2 or not first:
                        dve.wait_ge(o_done, TT * h + n - 1)
                    nc.vector.tensor_reduce(attn[0:w, n % 2, 0:w], kept[0:w, lv:NL, 0:w].rearrange("p l t -> p t l"), AX.X,
                                            ALU.add).then_inc(attn_done, 1)
                    if n < TILES:
                        dve.wait_ge(st_done, TILES * h + n + 1)
                        if n or not first:
                            dve.wait_ge(S_ready, TILES * h + n)
                        if n:
                            dve.wait_ge(o_done, TT * h + n)
                            nc.vector.scalar_tensor_tensor(S[:, n % 2, :], S[:, (n + 1) % 2, :], eG[:, n * P + P - 1:n * P + P],
                                                           st_ps[:, 0:P], ALU.mult, ALU.add).then_inc(S_ready, 1)
                        else:
                            nc.vector.tensor_copy(S[:, 0, :], st_ps[:, 0:P]).then_inc(S_ready, 1)
                            dve.wait_ge(hv_loaded, 32 * h + 32)
                            if not first:
                                dve.wait_ge(new_done, h)
                                dve.wait_ge(S_stored, 16 * h)
                            nc.vector.tensor_tensor(own_v[:, :, :], hv[0:NS, TILES:TT, :].broadcast_to([NS, DB, P]),
                                                    own[:, :].unsqueeze(2).broadcast_to([NS, DB, P]), ALU.mult
                                                    ).then_inc(own_ready, 1)
                dve.wait_ge(st_loaded, 16 * h + 16)
                if not first:
                    dve.wait_ge(new_stored, 16 * h)
                    dve.wait_ge(new_ready, h)
                ends = eG[:, SEQ:T].rearrange("p (b j) -> p b j", j=DT)[:, :, DT - 1:DT]
                nc.vector.tensor_tensor(new_st[:, :, :], st[:, :, :], ends.broadcast_to([P, DB, P]), ALU.mult
                                        ).then_inc(new_scaled, 1)
                dve.wait_ge(new_scaled, h + 1)
                dve.wait_ge(new_done, h + 1)
                nc.vector.tensor_tensor(new_st[:, :, :], new_st[:, :, :], pairs[:, :, :], ALU.add).then_inc(new_ready, 1)
                dve.wait_ge(summed, h + 1)
                nc.vector.tensor_scalar(var[:, :].rearrange("p (c t) -> p c t", c=NCH), sum_ps[:, :, 0:CH], 1.0 / P, EPS,
                                        ALU.mult, ALU.add).then_inc(var_ready, 1)
                dve.wait_ge(var_ready, h + 1)
                dve.wait_ge(decay_ready, 15 * h + 15)
                nc.vector.reciprocal(inv, var[:, :]).then_inc(inv_ready, 1)
                dve.wait_ge(nstep, 2 * h + 2)
                nc.vector.tensor_scalar(tmp, tmp, -0.5, 1.5, ALU.mult, ALU.add).then_inc(factor_ready, 1)
                dve.wait_ge(root_ready, h + 1)
                nc.vector.scalar_tensor_tensor(inv, oT[:, :], gain[:, 0:1], root, ALU.mult, ALU.mult).then_inc(normed, 1)
                dve.wait_ge(normed, h + 1)
                dve.wait_ge(gate_loaded, 16 * h + 16)
                if not first:
                    dve.wait_ge(rec_stored, 16 * h)
                nc.vector.tensor_tensor(rec[:, :], inv, gate[:, :], ALU.mult).then_inc(rec_ready, 1)

            heads(dve, body)

        @block.tensor
        def _(pe):
            def body(h, first):
                def pair_products(n):
                    w = P if n < TILES else NS
                    lv = 0 if n < TILES else NL - 3
                    if n or not first:
                        pe.wait_ge(kept_done, TT * h + n)
                    if n == 0:
                        pe.wait_ge(qL_ready, (NL - 1) * (h + 1))
                        pe.wait_ge(kL_ready, NL * (h + 1))
                        if not first:
                            pe.wait_ge(new_ready, h)
                    for x in range(lv, NL):
                        last = nc.tensor.matmul(pairs[0:w, x, 0:w], kL[:, x, tile(n)], qL[:, x, tile(n)], start=True,
                                                stop=True)
                    last.then_inc(pairs_done, 1)

                def turn(n):
                    w = P if n < TILES else NS
                    if n or not first:
                        pe.wait_ge(kdT_ready, TT * h + n)
                    nc.tensor.transpose(kd_ps[0:w, 0:P], kd[:, tile(n)], ident[:, :]).then_inc(kd_turned, 1)

                def states(n):
                    pe.wait_ge(kdT_ready, TT * h + n + 1)
                    if n == 0:
                        pe.wait_ge(hv_loaded, 32 * h + 32)
                    if n < TILES:
                        if n or not first:
                            pe.wait_ge(S_ready, TILES * h + n)
                        nc.tensor.matmul(st_ps[:, 0:P], kdT[:, n % 2, :], hv[:, n, :], start=True, stop=True
                                         ).then_inc(st_done, 1)
                    else:
                        pe.wait_ge(kept_done, TT * h + TT)
                        pe.wait_ge(own_ready, h + 1)
                        for x in range(2):
                            last = nc.tensor.matmul(pairs[:, 4 * x:4 * x + 4, :].rearrange("p a b -> p (a b)"),
                                                    kdT[0:NS, n % 2, :],
                                                    own_v[:, 4 * x:4 * x + 4, :].rearrange("p a b -> p (a b)"),
                                                    start=True, stop=True)
                        last.then_inc(new_done, 1)

                def outputs(n):
                    w = P if n < TILES else NS
                    pe.wait_ge(attn_done, TT * h + n + 1)
                    if n or not first:
                        pe.wait_ge(o_kept, TT * h + n)
                    last = nc.tensor.matmul(o_ps[:, 0:w], hv[0:w, n, :], attn[0:w, n % 2, 0:w], start=True, stop=(n == 0))
                    if n == 0:
                        last.then_inc(o_done, 1)
                    elif n < TILES:
                        pe.wait_ge(S_ready, TILES * h + n)
                        pe.wait_ge(q_in_ready, h + 1)
                        nc.tensor.matmul(o_ps[:, 0:w], S[:, (n + 1) % 2, :], q_in[:, tile(n)], start=False, stop=True
                                         ).then_inc(o_done, 1)
                    else:
                        pe.wait_ge(st_loaded, 16 * h + 16)
                        pe.wait_ge(q_in_ready, h + 1)
                        for b in range(DB):
                            last = nc.tensor.matmul(o_ps[:, DT * b:DT * (b + 1)], st[:, b, :],
                                                    q_in[:, SEQ + DT * b:SEQ + DT * (b + 1)], start=False, stop=(b == DB - 1))
                        last.then_inc(o_done, 1)

                for n in range(TT):
                    pair_products(n)
                    turn(n)
                    states(n)
                    outputs(n)
                pe.wait_ge(squared, h + 1)
                if not first:
                    pe.wait_ge(var_ready, h)
                for c in range(NCH):
                    last = nc.tensor.matmul(sum_ps[:, c, 0:CH], ones[:, :], sq[:, c * CH:(c + 1) * CH], start=True, stop=True)
                last.then_inc(summed, 1)

            heads(pe, body)


def merge(nc, xT, mixed_d, feat_d, w_attn, w_hgrn, w_out):
    with Scope(nc, "merge") as s:
        bhi = s.sb("bhi", [P, 8, T], F32R)
        blo = s.sb("blo", [P, 8, T], F32R)
        mhi = s.sb("mhi", [P, KD, T], F32R)
        mlo = s.sb("mlo", [P, KD, T], F32R)
        raw = s.sb("raw", [P, 2, UNIT])
        whi = s.sb("whi", [P, 2, UNIT], F32R)
        wlo = s.sb("wlo", [P, 2, UNIT], F32R)
        branch = s.sb("branch", [P, 2, CH])
        gates = s.sb("gates", [P, 2, 2, CH])
        both = s.sb("both", [P, 2, CH])
        ps = s.ps("ps", [P, 2, 2, 512])
        out_ps = s.ps("out_ps", [P, 4, 512])
        w_loaded = [s.sem(f"w_loaded{n}") for n in range(2)]
        branch_in = [s.sem(f"branch_in{n}") for n in range(2)]
        gates_in = [s.sem(f"gates_in{n}") for n in range(2)]
        b_hi_done, b_lo_done = s.sem("b_hi_done"), s.sem("b_lo_done")
        w_hi_done, w_lo_done = s.sem("w_hi_done"), s.sem("w_lo_done")
        mult_done = s.sem("mult_done")
        ps_done, gated, summed, m_hi_done, m_lo_done = (s.sem("ps_done"), s.sem("gated"), s.sem("summed"),
                                                        s.sem("m_hi_done"), s.sem("m_lo_done"))
        out_done, out_added = s.sem("out_done"), s.sem("out_added")
        block = s.block()
        parts = [(b, c) for c in range(NCH) for b in range(8)]
        wa = w_attn.rearrange("(G g r d) n -> g d G r n", G=2, g=2, r=2)
        wr = w_hgrn.rearrange("(k p) n -> p k n", p=P)
        wo = w_out.rearrange("(k p) n -> p k n", p=P)

        def pairs(engine, body):
            body(0, 0, 0, True)
            with engine.Fori(1, 4) as i:
                body(0, i, i, False)
            with engine.Fori(0, 4) as i:
                body(1, i, i + 4, False)

        @block.sync
        def _(sp):
            for n, (b, c) in enumerate(parts):
                if n >= 2:
                    sp.wait_ge(b_lo_done, n - 1)
                sp.dma_start(branch[:, n % 2, :], mixed_d[b][:, c * CH:(c + 1) * CH]).then_inc(branch_in[n % 2], 16)

            def body(kind, i, pair, first):
                for u in range(2):
                    if kind == 0:
                        for c in range(NCH):
                            y = 3 * u + c
                            if not (first and y < 2):
                                sp.wait_ge(gated, 12 * pair + 2 * y - 2)
                            for m in range(2):
                                sp.dma_start(gates[:, y % 2, m, :],
                                             feat_d[DynSlice(16 + 8 * m + 2 * i + u, 1)][:, :, c * CH:(c + 1) * CH
                                                                                         ].rearrange("a p t -> (a p) t")
                                             ).then_inc(gates_in[y % 2], 16)

            body(0, 0, 0, True)
            with sp.Fori(1, 4) as i:
                body(0, i, i, False)

        @block.gpsimd
        def _(pool):
            def body(kind, i, pair, first):
                for u in range(2):
                    if not first:
                        pool.wait_ge(w_lo_done, 2 * pair + u - 1)
                    col = (2 * i + u) * P
                    if kind == 0:
                        halves = raw[:, u, :].rearrange("p (m k f) -> p m k f", m=2, k=4)
                        for g in range(2):
                            for G in range(2):
                                pool.dma_start(halves[g * HD:(g + 1) * HD, 0, 2 * G:2 * G + 2, :],
                                               wa[g][:, G, :, DynSlice(col, P)]).then_inc(w_loaded[u], 16)
                        pool.dma_start(halves[:, 1, :, :], wr[:, :, DynSlice(col, P)]).then_inc(w_loaded[u], 16)
                    else:
                        pool.dma_start(raw[:, u, :].rearrange("p (k f) -> p k f", k=KD), wo[:, :, DynSlice(col, P)]
                                       ).then_inc(w_loaded[u], 16)

            pairs(pool, body)

        @block.scalar
        def _(act):
            def hi(u):
                nc.scalar.activation(whi[:, u, :], raw[:, u, :], ACT.Copy).then_inc(w_hi_done, 1)

            for n, (b, c) in enumerate(parts):
                act.wait_ge(branch_in[n % 2], 16 * (n // 2) + 16)
                nc.scalar.activation(bhi[:, b, c * CH:(c + 1) * CH], branch[:, n % 2, :], ACT.Copy).then_inc(b_hi_done, 1)
                if n == 3:
                    for u in range(2):
                        act.wait_ge(w_loaded[u], 80)
                        hi(u)
            with act.Fori(1, 4) as i:
                for u in range(2):
                    act.wait_ge(w_loaded[u], 80 * i + 80)
                    act.wait_ge(ps_done, 6 * i + 3 * u - 3)
                    hi(u)
            for u in range(2):
                act.wait_ge(w_loaded[u], 16 + 320)
                act.wait_ge(ps_done, 24 - 3 * (1 - u))
                hi(u)
            with act.Fori(1, 4) as i:
                for u in range(2):
                    act.wait_ge(w_loaded[u], 16 * i + 16 + 320)
                    act.wait_ge(out_done, 6 * i + 3 * u - 3)
                    hi(u)

        @block.vector
        def _(dve):
            def lo(u, pair):
                dve.wait_ge(w_hi_done, 2 * pair + u + 1)
                nc.vector.tensor_tensor(wlo[:, u, :], raw[:, u, :], whi[:, u, :], ALU.subtract).then_inc(w_lo_done, 1)

            def gate(i, u, c, first):
                y = 3 * u + c
                e = 6 * i + y
                dve.wait_ge(ps_done, e + 1)
                dve.wait_ge(gates_in[y % 2], 32 * (3 * i + y // 2) + 32)
                for m in range(2):
                    g = gates[:, y % 2, m, :]
                    nc.vector.tensor_tensor(g, g, ps[:, y % 2, m, 0:CH], ALU.mult).then_inc(mult_done, 1)
                dve.wait_ge(mult_done, 2 * e + 2)
                nc.vector.tensor_tensor(both[:, y % 2, :], gates[:, y % 2, 0, :], gates[:, y % 2, 1, :], ALU.add
                                        ).then_inc(gated, 2)
                dve.wait_ge(gated, 2 * e + 2)
                hi = mhi[:, DynSlice(2 * i + u, 1), c * CH:(c + 1) * CH].rearrange("p a t -> p (a t)")
                lo_ = mlo[:, DynSlice(2 * i + u, 1), c * CH:(c + 1) * CH].rearrange("p a t -> p (a t)")
                nc.vector.tensor_copy(hi, both[:, y % 2, :]).then_inc(m_hi_done, 1)
                dve.wait_ge(m_hi_done, e + 1)
                nc.vector.tensor_tensor(lo_, both[:, y % 2, :], hi, ALU.subtract).then_inc(m_lo_done, 1)

            def add(i, u, c):
                y = 3 * u + c
                dve.wait_ge(out_done, 6 * i + y + 1)
                x = xT[:, DynSlice(2 * i + u, 1), c * CH:(c + 1) * CH].rearrange("p a t -> p (a t)")
                nc.vector.tensor_tensor(x, x, out_ps[:, y % 3, 0:CH], ALU.add).then_inc(out_added, 1)

            for n, (b, c) in enumerate(parts):
                cols = slice(c * CH, (c + 1) * CH)
                dve.wait_ge(b_hi_done, n + 1)
                nc.vector.tensor_tensor(blo[:, b, cols], branch[:, n % 2, :], bhi[:, b, cols], ALU.subtract
                                        ).then_inc(b_lo_done, 1)
                if n == 4:
                    lo(0, 0)
                    lo(1, 0)

            def gates_of(i, u, first=False):
                for c in range(NCH):
                    gate(i, u, c, first)

            with dve.Fori(0, 3) as i:
                for u in range(2):
                    gates_of(i, u)
                    lo(u, i + 1)
            gates_of(3, 0)
            lo(0, 4)
            gates_of(3, 1)
            lo(1, 4)
            with dve.Fori(0, 3) as i:
                for u in range(2):
                    for c in range(NCH):
                        add(i, u, c)
                    lo(u, i + 5)
            for u in range(2):
                for c in range(NCH):
                    add(3, u, c)

        @block.tensor
        def _(pe):
            def body(kind, i, pair, first):
                for u in range(2):
                    pe.wait_ge(w_lo_done, 2 * pair + u + 1)
                    for c in range(NCH):
                        y = 3 * u + c
                        cols = slice(c * CH, (c + 1) * CH)
                        if kind == 0:
                            if first and u == 0:
                                pe.wait_ge(b_lo_done, 8 * c + 8)
                            if not (first and y < 2):
                                pe.wait_ge(gated, 12 * i + 2 * y - 2)
                            for m in range(2):
                                for k in range(4):
                                    w = slice((4 * m + k) * P, (4 * m + k + 1) * P)
                                    last = split_product(nc, ps[:, y % 2, m, 0:CH], whi[:, u, w], wlo[:, u, w],
                                                         bhi[:, 4 * m + k, cols], blo[:, 4 * m + k, cols], k == 0, k == 3)
                            last.then_inc(ps_done, 1)
                        else:
                            if first or (u == 0):
                                pe.wait_ge(m_lo_done, 18 + c + 4)
                            if not (first and y < 3):
                                pe.wait_ge(out_added, 6 * i + y - 2)
                            for k in range(KD):
                                w = slice(k * P, (k + 1) * P)
                                last = split_product(nc, out_ps[:, y % 3, 0:CH], whi[:, u, w], wlo[:, u, w],
                                                     mhi[:, k, cols], mlo[:, k, cols], k == 0, k == KD - 1)
                            last.then_inc(out_done, 1)

            body(0, 0, 0, True)
            with pe.Fori(1, 4) as i:
                body(0, i, i, False)
            body(1, 0, 4, True)
            with pe.Fori(1, 4) as i:
                body(1, i, i + 4, False)

OUTS = [("y_prompt", (1, SEQ, D)), ("y_sample", (DB, DT, D)), ("k_prompt", (1, 1, SEQ, KV, HD)), ("v_prompt", (1, 1, SEQ, KV, HD)),
        ("idx_k_prompt", (1, 1, SEQ, HD)), ("hgrn_prompt", (1, 1, HG, P, P)), ("k_sample", (1, DB, DT, KV, HD)),
        ("v_sample", (1, DB, DT, KV, HD)), ("idx_k_sample", (1, DB, DT, HD)), ("hgrn_sample", (1, DB, HG, P, P))]


def build(nc, a, o):
    scratch = {name: nc.dram_tensor(f"scratch_{name}", shape, F32).ap()
               for name, shape in (("qT", (4, P, T)), ("kT", (2, P, T)), ("qiT", (4, P, T)), ("kiT", (1, P, T)),
                                   ("wi", (T, HEADS)), ("hv", (T, HG * P)), ("feat", (FEATS, P, T)), ("mixed", (8, P, T)))}
    rows = {n: o[n].rearrange("a b t h d -> (a b t) (h d)") for n in ("k_prompt", "v_prompt", "k_sample", "v_sample")}
    rows |= {n: o[n].rearrange("a b t d -> (a b t) d") for n in ("idx_k_prompt", "idx_k_sample")}
    cache_k, cache_v = (a[n][0].rearrange("n s h d -> n s (h d)") for n in ("cache_k", "cache_v"))
    with Scope(nc, "core") as s:
        xT = s.sb("xT", [P, KD, T])
        ident = s.sb("ident", [P, P])
        ones = s.sb("ones", [P, P])
        ident_in, ones_set = s.sem("ident_in"), s.sem("ones_set")
        with nc.Block() as block:
            @block.sync
            def _(sp):
                sp.dma_start(ident[:, :], a["t_ident"]).then_inc(ident_in, 16)
                sp.wait_ge(ident_in, 16)

            @block.vector
            def _(dve):
                nc.vector.memset(ones[:, :], 1.0).then_inc(ones_set, 1)

        load_and_turn(nc, a["x_prompt"], a["x_sample"], xT, ident)

        def feed_forward(n):
            with Scope(nc, f"half{n}") as half:
                hhi = half.sb("hhi", [P, KD, T], F32R)
                hlo = half.sb("hlo", [P, KD, T], F32R)
                normalise(nc, f"norm{n}", xT, a[f"ffn{n}_norm"], hhi, hlo, ones)
                swiglu(nc, f"ff{n}", xT, hhi, hlo, a[f"ffn{n}_w_gate"], a[f"ffn{n}_w_up"], a[f"ffn{n}_w_down"])

        feed_forward(1)
        with Scope(nc, "mix") as mix:
            masks = mix.sb("masks", [P, SLABS, SW], mybir.dt.bfloat16)
            with Scope(nc, "proj") as proj:
                hhi = proj.sb("hhi", [P, KD, T], F32R)
                hlo = proj.sb("hlo", [P, KD, T], F32R)
                normalise(nc, "normm", xT, a["mix_norm"], hhi, hlo, ones)
                token_projections(nc, hhi, hlo, a["w_in"], a["q_norm"], a["k_norm"], a["t_cos"], a["t_sin"], ident,
                                  scratch["qT"], scratch["kT"], scratch["qiT"], scratch["kiT"], scratch["wi"],
                                  scratch["hv"], rows["k_prompt"], rows["k_sample"], rows["v_prompt"], rows["v_sample"],
                                  rows["idx_k_prompt"], rows["idx_k_sample"])
                scores = proj.sb("scores", [P, SLABS, SW])
                index_scores(nc, scores, scratch["qiT"], scratch["kiT"], scratch["wi"], a["cache_idx_k"], a["page_table"],
                             a["t_same_token"], a["t_new_floor"], ident)
                select_keys_and_project(nc, scores, masks, hhi, hlo, a["w_in"], scratch["feat"])
            attention(nc, scratch["mixed"], masks, scratch["qT"], scratch["kT"], rows["v_prompt"], rows["v_sample"],
                      cache_k, cache_v, a["page_table"], a["t_causal"], a["t_own"], ident)
        recurrence(nc, scratch["mixed"], scratch["feat"], scratch["hv"], a["state_hgrn"][0].rearrange("b h k v -> h k b v"),
                   o["hgrn_prompt"].rearrange("a b h k v -> (a b h) k v"),
                   o["hgrn_sample"].rearrange("a b h k v -> h k (a b) v"), a["hg_lower_bound"], a["hg_norm"],
                   a["t_resets"], a["t_levels"], a["t_owner"], ident, ones)
        merge(nc, xT, scratch["mixed"], scratch["feat"], a["w_branch_attn"][0], a["w_branch_hgrn"][0], a["w_out"][0])
        feed_forward(2)
        turn_and_store(nc, xT, o["y_prompt"], o["y_sample"], ident)


GAINS = ('ffn1_norm', 'mix_norm', 'ffn2_norm')


def shape_tables():
    half = HD // 2
    inv = (10000.0 ** (-np.arange(half) * 2.0 / HD)).astype(np.float32)
    pos = np.concatenate([np.arange(SEQ), np.zeros(P - NS), SEQ + np.tile(np.arange(DT), DB)]).astype(np.float32)
    ang = pos[:, None] * inv[None, :]
    c, s = np.cos(ang), np.sin(ang)
    cos = np.concatenate([c, c], 1).reshape(TT, P, HD).transpose(1, 0, 2)
    sin = np.concatenate([-s, s], 1).reshape(TT, P, HD).transpose(1, 0, 2)
    row = np.arange(P)
    same = row[:, None] % NS == row[None, :] % NS
    causal = np.concatenate([np.zeros((P, P)), np.where(row[None, :] <= row[:, None], 0.0, MASKED)], 1)
    own = np.repeat(row[:, None, None] % NS // DT == np.arange(DB)[None, :, None], DT, 2)
    t = np.arange(T)
    start = np.where(t < SEQ, t % P == 0, (t - SEQ) % DT == 0)
    resets = np.broadcast_to(np.where(start, 0.0, 1.0)[None, :], (P, T))
    s_, t_ = row[:, None], row[None, :]
    levels = np.stack([(s_ // (2 * b) == t_ // (2 * b)) & (s_ % (2 * b) < b) & (t_ % (2 * b) >= b) for b in LEVELS]
                      + [s_ == t_], 1)
    return {"t_cos": cos, "t_sin": sin, "t_ident": np.eye(P),
            "t_causal": causal, "t_own": own,
            "t_resets": resets, "t_levels": levels, "t_owner": row[0:NS, None] // DT == np.arange(DB)[None, :],
            "t_same_token": same, "t_new_floor": np.where(np.arange(DT)[None] <= np.arange(P)[:, None] % DT, 0.0, FLOOR)}


def kernel(**inputs):
    import concourse.bacc as bacc
    from concourse.bass_utils import run_bass_kernel_spmd
    nc = bacc.Bacc("TRN2", target_bir_lowering=False, num_devices=1)
    arrays, a = {}, {}
    for name, v in inputs.items():
        v = np.ascontiguousarray(v)
        if name in GAINS:
            v = v.reshape(KD, P).T
        elif name == 'hg_lower_bound':
            v = v.reshape(2, HG, P).transpose(2, 0, 1)
        elif name == 'hg_norm':
            v = v.reshape(P, 1)
        v = np.ascontiguousarray(v)
        arrays[f"in_{name}"] = v
    for name, v in shape_tables().items():
        arrays[f"in_{name}"] = np.ascontiguousarray(v, dtype=np.float32)
    for name, v in arrays.items():
        a[name[3:]] = nc.dram_tensor(name, v.shape, mybir.dt.from_np(v.dtype), kind="ExternalInput").ap()
    o = {}
    for name, shape in OUTS:
        o[name] = nc.dram_tensor(f"out_{name}", shape, F32, kind="ExternalOutput").ap()
    build(nc, a, o)
    r = run_bass_kernel_spmd(nc, [arrays], core_ids=[0])
    return tuple(r.results[0][f"out_{name}"] for name, _ in OUTS)
```

```python
import math
from contextlib import ExitStack

import numpy as np

import concourse.bass as bass
from concourse import mybir
from concourse.bass import DynSlice

F32 = mybir.dt.float32
F32R = mybir.dt.float32r
I32 = mybir.dt.int32
ACT = mybir.ActivationFunctionType
ALU = mybir.AluOpType
AX = mybir.AxisListType

P = 128
D = 1024
KD = D // P
SEQ = 1024
TILES = SEQ // P
DB, DT = 8, 4
NS = DB * DT
T = SEQ + NS
CH = 352
NCH = T // CH
FF = 2816
NFF = FF // P
PAIRS = NFF // 2
EPS = 1e-6
RAW = 6
UNIT = 1024


class Scope:

    def __init__(self, nc, tag):
        self.nc, self.tag, self.stack, self.sems = nc, tag, ExitStack(), []
        self.blocks = ExitStack()

    def __enter__(self):
        self.stack.__enter__()
        return self

    def __exit__(self, *a):
        self.blocks.close()
        if self.sems and a[0] is None:
            with self.nc.Block() as block:
                @block.gpsimd
                def _(pool):
                    for sem in self.sems:
                        pool.sem_clear(sem)
        return self.stack.__exit__(*a)

    def sb(self, name, shape, dt=F32):
        return self.stack.enter_context(self.nc.sbuf_tensor(f"{self.tag}_{name}", shape, dt))

    def ps(self, name, shape, dt=F32):
        return self.stack.enter_context(self.nc.psum_tensor(f"{self.tag}_{name}", shape, dt))

    def sem(self, name):
        self.sems.append(self.stack.enter_context(self.nc.semaphore(f"{self.tag}_{name}")))
        return self.sems[-1]

    def block(self):
        return self.blocks.enter_context(self.nc.Block())


def load_and_turn(nc, x_prompt, x_sample, xT, ident):
    with Scope(nc, "turn") as s:
        rows = s.sb("rows", [P, 2, D])
        turned = s.ps("turned", [P, 4, 4, P])
        loaded = [s.sem(f"loaded{n}") for n in range(2)]
        half_turned = s.sem("half_turned")
        half_kept = s.sem("half_kept")
        xp = x_prompt[0].rearrange("(n p) d -> n p d", p=P)
        xs = x_sample.rearrange("b t d -> (b t) d")
        block = s.block()

        @block.sync
        def _(sp):
            def load(i, n):
                sp.dma_start(rows[:, n, :], xp[DynSlice(2 * i + n, 1)].rearrange("a p d -> (a p) d")
                             ).then_inc(loaded[n], 16)

            load(0, 0)
            load(0, 1)
            with sp.Fori(1, TILES // 2) as i:
                for n in range(2):
                    sp.wait_ge(half_turned, 4 * i - 2 + 2 * n)
                    load(i, n)
            sp.wait_ge(half_turned, 4 * (TILES // 2))
            sp.dma_start(rows[0:NS, 0, :], xs).then_inc(loaded[0], 16)

        @block.tensor
        def _(pe):
            def turn_pair(i, first):
                for n in range(2):
                    pe.wait_ge(loaded[n], 16 * i + 16)
                    for h in range(2):
                        if not first:
                            pe.wait_ge(half_kept, 4 * i - 3 + 2 * n + h)
                        for k in range(4):
                            m = nc.tensor.transpose(turned[:, 2 * n + h, k, :],
                                                    rows[:, n, (4 * h + k) * P:(4 * h + k + 1) * P], ident[:, :])
                        m.then_inc(half_turned, 1)

            turn_pair(0, True)
            with pe.Fori(1, TILES // 2) as i:
                turn_pair(i, False)
            pe.wait_ge(loaded[0], 16 * (TILES // 2) + 16)
            pe.wait_ge(half_kept, 4 * (TILES // 2))
            for h in range(2):
                for k in range(4):
                    m = nc.tensor.transpose(turned[:, h, k, 0:NS],
                                            rows[0:NS, 0, (4 * h + k) * P:(4 * h + k + 1) * P], ident[0:NS, 0:NS])
                m.then_inc(half_turned, 1)

        @block.vector
        def _(dve):
            with dve.Fori(0, TILES // 2) as i:
                for n in range(2):
                    for h in range(2):
                        dve.wait_ge(half_turned, 4 * i + 2 * n + h + 1)
                        nc.vector.tensor_copy(xT[:, 4 * h:4 * h + 4, DynSlice(2 * P * i + P * n, P)],
                                              turned[:, 2 * n + h, :, :]).then_inc(half_kept, 1)
            for h in range(2):
                dve.wait_ge(half_turned, 4 * (TILES // 2) + h + 1)
                nc.vector.tensor_copy(xT[:, 4 * h:4 * h + 4, SEQ:T], turned[:, h, :, 0:NS]).then_inc(half_kept, 1)


def turn_and_store(nc, xT, y_prompt, y_sample, ident):
    with Scope(nc, "back") as s:
        rows = s.sb("rows", [P, 2, D])
        turned = s.ps("turned", [P, 4, 4, P])
        half_turned = s.sem("half_turned")
        half_kept = s.sem("half_kept")
        stored = [s.sem(f"stored{n}") for n in range(2)]
        yp = y_prompt[0].rearrange("(n p) d -> n p d", p=P)
        block = s.block()

        @block.sync
        def _(sp):
            for n in range(TILES + 1):
                sp.wait_ge(half_kept, 2 * n + 2)
                if n < TILES:
                    sp.dma_start(yp[n], rows[:, n % 2, :]).then_inc(stored[n % 2], 16)
                else:
                    sp.dma_start(y_sample.rearrange("b t d -> (b t) d"), rows[0:NS, n % 2, :]).then_inc(stored[n % 2], 16)
            sp.wait_ge(stored[0], 16 * (TILES // 2 + 1))
            sp.wait_ge(stored[1], 16 * (TILES // 2))

        @block.tensor
        def _(pe):
            for n in range(TILES + 1):
                w = P if n < TILES else NS
                for h in range(2):
                    if n >= 2:
                        pe.wait_ge(half_kept, 2 * n - 3 + h)
                    for k in range(4):
                        m = nc.tensor.transpose(turned[0:w, 2 * (n % 2) + h, k, :],
                                                xT[:, 4 * h + k, n * P:n * P + w], ident[:, :])
                    m.then_inc(half_turned, 1)

        @block.vector
        def _(dve):
            for n in range(TILES + 1):
                w = P if n < TILES else NS
                for h in range(2):
                    dve.wait_ge(half_turned, 2 * n + h + 1)
                    if n >= 2 and h == 0:
                        dve.wait_ge(stored[n % 2], 16 * (n // 2))
                    nc.vector.tensor_copy(rows[0:w, n % 2, 4 * h * P:4 * (h + 1) * P],
                                          turned[0:w, 2 * (n % 2) + h, :, :].rearrange("p a b -> p (a b)")
                                          ).then_inc(half_kept, 1)


def normalise(nc, tag, xT, gain, hhi, hlo, ones):
    with Scope(nc, tag) as s:
        sq = s.sb("sq", [P, 2, KD, CH])
        full = s.sb("full", [P, 2, KD, CH])
        var = s.sb("var", [P, NCH, CH])
        inv = s.sb("inv", [P, NCH, CH])
        root = s.sb("root", [P, NCH, CH])
        tmp = s.sb("tmp", [P, CH])
        total = s.ps("total", [P, NCH, 512])
        g = s.sb("gain", [P, KD])
        gain_in = s.sem("gain_in")
        squared = s.sem("squared")
        summed = s.sem("summed")
        step = s.sem("step")
        inverted = s.sem("inverted")
        rooted = s.sem("rooted")
        scaled = s.sem("scaled")
        hi_done = s.sem("hi_done")
        lo_done = s.sem("lo_done")
        block = s.block()
        HALF = KD // 2

        def cols(c):
            return slice(c * CH, (c + 1) * CH)

        @block.sync
        def _(sp):
            sp.dma_start(g[:, :], gain).then_inc(gain_in, 16)

        @block.scalar
        def _(act):
            def square(c):
                if c >= 2:
                    act.wait_ge(summed, c - 1)
                for h in range(2):
                    nc.scalar.activation(sq[:, c % 2, h * HALF:(h + 1) * HALF, :], xT[:, h * HALF:(h + 1) * HALF, cols(c)],
                                         ACT.Square).then_inc(squared, 1)

            def hi(c):
                for h in range(2):
                    act.wait_ge(scaled, 2 * c + h + 1)
                    k = slice(h * HALF, (h + 1) * HALF)
                    nc.scalar.activation(hhi[:, k, cols(c)], full[:, c % 2, k, :], ACT.Copy).then_inc(hi_done, 1)

            square(0)
            square(1)
            for c in range(NCH):
                act.wait_ge(inverted, c + 1)
                nc.scalar.activation(root[:, c, :], inv[:, c, :], ACT.Sqrt).then_inc(rooted, 1)
                if c + 2 < NCH:
                    square(c + 2)
                hi(c)

        @block.tensor
        def _(pe):
            for c in range(NCH):
                for k in range(KD):
                    if k % HALF == 0:
                        pe.wait_ge(squared, 2 * c + k // HALF + 1)
                    m = nc.tensor.matmul(total[:, c, 0:CH], ones[:, :], sq[:, c % 2, k, :], start=(k == 0),
                                         stop=(k == KD - 1))
                m.then_inc(summed, 1)

        @block.gpsimd
        def _(pool):
            for c in range(NCH):
                k = slice(0, HALF)
                pool.wait_ge(hi_done, 2 * c + 1)
                nc.gpsimd.tensor_tensor(hlo[:, k, cols(c)], full[:, c % 2, k, :], hhi[:, k, cols(c)], ALU.subtract
                                        ).then_inc(lo_done, 1)

        @block.vector
        def _(dve):
            steps = [0]

            def done(ins):
                ins.then_inc(step, 1)
                steps[0] += 1
                dve.wait_ge(step, steps[0])

            def lo(c):
                k = slice(HALF, KD)
                dve.wait_ge(hi_done, 2 * c + 2)
                done(nc.vector.tensor_tensor(hlo[:, k, cols(c)], full[:, c % 2, k, :], hhi[:, k, cols(c)], ALU.subtract))

            dve.wait_ge(gain_in, 16)
            for c in range(NCH):
                dve.wait_ge(summed, c + 1)
                done(nc.vector.tensor_scalar(var[:, c, :], total[:, c, 0:CH], 1.0 / D, EPS, ALU.mult, ALU.add))
                nc.vector.reciprocal(inv[:, c, :], var[:, c, :]).then_inc(inverted, 1)
                dve.wait_ge(rooted, c + 1)
                done(nc.vector.tensor_tensor(tmp[:, :], root[:, c, :], root[:, c, :], ALU.mult))
                done(nc.vector.tensor_tensor(tmp[:, :], tmp[:, :], var[:, c, :], ALU.mult))
                done(nc.vector.tensor_scalar(tmp[:, :], tmp[:, :], -0.5, 1.5, ALU.mult, ALU.add))
                done(nc.vector.tensor_tensor(root[:, c, :], root[:, c, :], tmp[:, :], ALU.mult))
                if c >= 2:
                    dve.wait_ge(lo_done, c - 1)
                for k in range(KD):
                    m = nc.vector.scalar_tensor_tensor(full[:, c % 2, k, :], xT[:, k, cols(c)], g[:, k:k + 1],
                                                       root[:, c, :], ALU.mult, ALU.mult)
                    if k % HALF == HALF - 1:
                        m.then_inc(scaled, 1)
                lo(c)


def split_product(nc, out, w_hi, w_lo, x_hi, x_lo, first, last):
    nc.tensor.matmul(out, w_hi, x_hi, start=first, stop=False)
    nc.tensor.matmul(out, w_hi, x_lo, start=False, stop=False)
    return nc.tensor.matmul(out, w_lo, x_hi, start=False, stop=last)


def swiglu(nc, tag, xT, hhi, hlo, w_gate, w_up, w_down):
    with Scope(nc, tag) as s:
        raw = s.sb("raw", [P, RAW, UNIT])
        whi = s.sb("whi", [P, RAW, UNIT], F32R)
        wlo = s.sb("wlo", [P, RAW, UNIT], F32R)
        act_out = s.sb("silu", [P, 2, CH])
        prod = s.sb("prod", [P, 2, CH])
        ahi = s.sb("ahi", [P, 2, T], F32R)
        alo = s.sb("alo", [P, 2, T], F32R)
        gu = s.ps("gu", [P, 2, 2, 512])
        dn = s.ps("dn", [P, 4, 512])
        raw_loaded = [s.sem(f"raw_loaded{n}") for n in range(RAW)]
        w_hi_done = s.sem("w_hi_done")
        w_lo_done = s.sem("w_lo_done")
        gu_done = s.sem("gu_done")
        silu_done = s.sem("silu_done")
        prod_done = s.sem("prod_done")
        a_hi_done = s.sem("a_hi_done")
        a_lo_done = s.sem("a_lo_done")
        down_done = s.sem("down_done")
        down_free = s.sem("down_free")
        block = s.block()
        wg = w_gate[0].rearrange("(k p) f -> p k f", p=P)
        wu = w_up[0].rearrange("(k p) f -> p k f", p=P)
        wd = w_down[0].rearrange("(j p) n -> j p n", p=P)

        @block.sync
        def _(sp):
            def load(g, u, wait):
                if wait:
                    sp.wait_ge(w_lo_done, 6 * g + u - RAW + 1)
                if u < 4:
                    src = (wg, wu)[u % 2][:, :, DynSlice((2 * g + u // 2) * P, P)]
                    dst = raw[:, u, :].rearrange("p (k f) -> p k f", k=KD)
                else:
                    src = wd[DynSlice(2 * g + u - 4, 1)].rearrange("a p n -> (a p) n")
                    dst = raw[:, u, :]
                sp.dma_start(dst, src).then_inc(raw_loaded[u], 16)

            for u in range(6):
                load(0, u, False)
            with sp.Fori(1, PAIRS) as g:
                for u in range(6):
                    load(g, u, True)

        @block.scalar
        def _(act):
            def hi(i, k, wait=True):
                if wait and k in (2, 3):
                    act.wait_ge(gu_done, 6 * i)
                elif wait and k in (4, 5):
                    act.wait_ge(down_done, 24 * i)
                elif wait:
                    act.wait_ge(gu_done, 6 * i + 3)
                act.wait_ge(raw_loaded[k % 6], 16 * (i + k // 6) + 16)
                nc.scalar.activation(whi[:, k % 6, :], raw[:, k % 6, :], ACT.Copy).then_inc(w_hi_done, 1)

            def silu(i, q):
                act.wait_ge(gu_done, 6 * i + q + 1)
                nc.scalar.activation(act_out[:, q % 2, :], gu[:, q % 2, 0, 0:CH], ACT.Silu).then_inc(silu_done, 1)

            def round_(i, last=False):
                hi(i, 2)
                hi(i, 3)
                hi(i, 4)
                hi(i, 5)
                for q in range(3):
                    silu(i, q)
                if not last:
                    hi(i, 6)
                    hi(i, 7)
                for q in range(3, 6):
                    silu(i, q)

            for k in range(6):
                hi(0, k, False)
            for q in range(3):
                silu(0, q)
            hi(0, 6)
            hi(0, 7)
            for q in range(3, 6):
                silu(0, q)
            with act.Fori(1, PAIRS - 1) as i:
                round_(i)
            round_(PAIRS - 1, True)

        @block.vector
        def _(dve):
            def lo(i, k):
                dve.wait_ge(w_hi_done, 6 * i + k + 1)
                nc.vector.tensor_tensor(wlo[:, k % 6, :], raw[:, k % 6, :], whi[:, k % 6, :], ALU.subtract
                                        ).then_inc(w_lo_done, 1)

            def product(i, q, first=False):
                b, cols = q // 3, slice(q % 3 * CH, (q % 3 + 1) * CH)
                dve.wait_ge(silu_done, 6 * i + q + 1)
                nc.vector.tensor_tensor(prod[:, q % 2, :], act_out[:, q % 2, :], gu[:, q % 2, 1, 0:CH], ALU.mult
                                        ).then_inc(prod_done, 1)
                dve.wait_ge(prod_done, 6 * i + q + 1)
                if not first:
                    dve.wait_ge(down_done, 24 * i)
                nc.vector.tensor_copy(ahi[:, b, cols], prod[:, q % 2, :]).then_inc(a_hi_done, 1)
                dve.wait_ge(a_hi_done, 6 * i + q + 1)
                nc.vector.tensor_tensor(alo[:, b, cols], prod[:, q % 2, :], ahi[:, b, cols], ALU.subtract
                                        ).then_inc(a_lo_done, 1)

            def add_down(i):
                for j in range(NCH * KD):
                    c, k = j // KD, j % KD
                    dve.wait_ge(down_done, 24 * i + j + 1)
                    x = xT[:, k, c * CH:(c + 1) * CH]
                    nc.vector.scalar_tensor_tensor(x, dn[:, j % 4, 0:CH], 0.5, x, ALU.mult, ALU.add
                                                   ).then_inc(down_free, 1)

            def round_(i, last=False):
                lo(i, 2)
                lo(i, 3)
                add_down(i - 1)
                lo(i, 4)
                lo(i, 5)
                for q in range(3):
                    product(i, q)
                if not last:
                    lo(i, 6)
                    lo(i, 7)
                for q in range(3, 6):
                    product(i, q)

            dve.sem_inc(down_free, 4)
            for k in range(6):
                lo(0, k)
            for q in range(3):
                product(0, q, True)
            lo(0, 6)
            lo(0, 7)
            for q in range(3, 6):
                product(0, q, True)
            with dve.Fori(1, PAIRS - 1) as i:
                round_(i)
            round_(PAIRS - 1, True)
            add_down(PAIRS - 1)

        @block.tensor
        def _(pe):
            def gate_up(i, b, first=False):
                pe.wait_ge(w_lo_done, 6 * i + 2 * b + 2)
                for c in range(NCH):
                    q = 3 * b + c
                    cols = slice(c * CH, (c + 1) * CH)
                    if not (first and q < 2):
                        pe.wait_ge(prod_done, 6 * i + q - 1)
                    for m in range(2):
                        u = 2 * b + m
                        for k in range(KD):
                            w = slice(k * P, (k + 1) * P)
                            last = split_product(nc, gu[:, q % 2, m, 0:CH], whi[:, u, w], wlo[:, u, w],
                                                 hhi[:, k, cols], hlo[:, k, cols], k == 0, k == KD - 1)
                    last.then_inc(gu_done, 1)

            def down(i):
                pe.wait_ge(w_lo_done, 6 * i + 6)
                for j in range(NCH * KD):
                    c, k = j // KD, j % KD
                    cols = slice(c * CH, (c + 1) * CH)
                    if k == 0:
                        pe.wait_ge(a_lo_done, 6 * i + 3 + c + 1)
                    pe.wait_ge(down_free, 24 * i + j + 1)
                    for b in range(2):
                        last = split_product(nc, dn[:, j % 4, 0:CH], whi[:, 4 + b, k * P:(k + 1) * P],
                                             wlo[:, 4 + b, k * P:(k + 1) * P], ahi[:, b, cols], alo[:, b, cols],
                                             b == 0, b == 1)
                    last.then_inc(down_done, 1)

            gate_up(0, 0, True)
            gate_up(0, 1)
            with pe.Fori(1, PAIRS) as i:
                down(i - 1)
                gate_up(i, 0)
                gate_up(i, 1)
            down(PAIRS - 1)


HD = 64
HEADS, KV = 8, 4
TT = TILES + 1
CW = 256
SROW = P - NS
CHUNKS = [("q", 0), ("q", 256), ("k", 512), ("v", 768), ("qi", 1024), ("qi", 1280), ("ki", 1536),
          ("hv", 2632), ("hv", 2888)]
KI_COLS = HD + HEADS


def newton_rsqrt(nc, done, root, var, tmp):
    done(nc.vector.tensor_tensor(tmp, root, root, ALU.mult))
    done(nc.vector.tensor_tensor(tmp, tmp, var, ALU.mult))
    done(nc.vector.tensor_scalar(tmp, tmp, -0.5, 1.5, ALU.mult, ALU.add))
    done(nc.vector.tensor_tensor(root, root, tmp, ALU.mult))


def token_projections(nc, hhi, hlo, w_in, q_gain, k_gain, cos, sin, ident, qT_d, kT_d, qiT_d, kiT_d, wi_d, hv_d,
                      k_prompt, k_sample, v_prompt, v_sample, ki_prompt, ki_sample):
    NC = len(CHUNKS)
    M = NC * TT
    with Scope(nc, "tok") as s:
        raw = s.sb("raw", [P, 2, KD, CW])
        whi = s.sb("whi", [P, 2, KD, CW], F32R)
        wlo = s.sb("wlo", [P, 2, KD, CW], F32R)
        taken = s.sb("taken", [P, 4, CW])
        sq = s.sb("sq", [P, 2, CW])
        var = s.sb("var", [P, 4])
        inv = s.sb("inv", [P, 4])
        root = s.sb("root", [P, 4])
        tmp = s.sb("tmp", [P, 4])
        xn = s.sb("xn", [P, CW])
        ra = s.sb("ra", [P, CW])
        rb = s.sb("rb", [P, CW])
        out = s.sb("out", [P, 4, CW])
        stage = s.sb("stage", [P, 2, 2, T])
        gains = s.sb("gains", [P, 2, HD])
        cs = s.sb("cs", [P, TT, HD])
        sn = s.sb("sn", [P, TT, HD])
        proj = s.ps("proj", [P, 4, 512])
        turned = s.ps("turned", [P, 2, 4, P])
        w_loaded = [s.sem(f"w_loaded{n}") for n in range(2)]
        tables_in = s.sem("tables_in")
        w_hi_done, w_lo_done = s.sem("w_hi_done"), s.sem("w_lo_done")
        proj_done, take_done, sq_done = s.sem("proj_done"), s.sem("take_done"), s.sem("sq_done")
        inv_done, root_done = s.sem("inv_done"), s.sem("root_done")
        step, out_done = s.sem("step"), s.sem("out_done")
        turn_done, kept_done = s.sem("turn_done"), s.sem("kept_done")
        out_stored = [s.sem(f"out_stored{n}") for n in range(4)]
        stage_stored = [s.sem(f"stage_stored{n}") for n in range(2)]
        block = s.block()

        def kind(m):
            return CHUNKS[m // TT][0]

        def width(c):
            return KI_COLS if CHUNKS[c][0] == "ki" else CW

        def normed(m):
            return kind(m) in "qk"

        def turns(m):
            return kind(m) not in ("v", "hv")

        def stores(m):
            return {"k": 1, "v": 1, "hv": 1, "ki": 2}.get(kind(m), 0)

        def count(f, m):
            return sum(1 for x in range(m) if f(x))

        def stored_before(m, slot):
            return sum(stores(x) for x in range(m) if x % 4 == slot)

        wv = w_in[0].rearrange("(k p) f -> p k f", p=P)

        @block.sync
        def _(sp):
            def load(c):
                if c >= 2:
                    sp.wait_ge(w_lo_done, c - 1)
                w, at = width(c), CHUNKS[c][1]
                sp.dma_start(raw[:, c % 2, :, 0:w], wv[:, :, at:at + w]).then_inc(w_loaded[c % 2], 16)

            load(0)
            for dst, src in ((gains[:, 0, :], q_gain.partition_broadcast(P)), (gains[:, 1, :], k_gain.partition_broadcast(P)),
                             (cs[:, :, :], cos), (sn[:, :, :], sin)):
                sp.dma_start(dst, src).then_inc(tables_in, 16)
            load(1)
            for m in range(M):
                c, n = m // TT, m % TT
                if n == 4 and c + 2 < NC:
                    load(c + 2)
                rows = slice(0, P) if n < TILES else slice(SROW, P)
                at = slice(n * P, (n + 1) * P)
                o = out[rows, m % 4, :]
                if stores(m):
                    sp.wait_ge(out_done, m + 1)
                if kind(m) == "k":
                    dst = k_prompt[at] if n < TILES else k_sample
                    sp.dma_start(dst, o).then_inc(out_stored[m % 4], 16)
                elif kind(m) == "v":
                    dst = v_prompt[at] if n < TILES else v_sample
                    sp.dma_start(dst, o).then_inc(out_stored[m % 4], 16)
                elif kind(m) == "hv":
                    dst = hv_d[n * P:n * P + (P if n < TILES else NS), (c - 7) * CW:(c - 6) * CW]
                    sp.dma_start(dst, o).then_inc(out_stored[m % 4], 16)
                elif kind(m) == "ki":
                    dst = ki_prompt[at] if n < TILES else ki_sample
                    sp.dma_start(dst, o[:, 0:HD]).then_inc(out_stored[m % 4], 16)
                    dst = wi_d[n * P:n * P + (P if n < TILES else NS)]
                    sp.dma_start(dst, o[:, 2 * HD:2 * HD + HEADS]).then_inc(out_stored[m % 4], 16)
                if n == TT - 1 and turns(m):
                    sp.wait_ge(kept_done, count(turns, m + 1))
                    dst = {"q": qT_d, "k": kT_d, "qi": qiT_d, "ki": kiT_d}[kind(m)]
                    b = {"q": 2 * c, "k": 0, "qi": 2 * (c - 4), "ki": 0}[kind(m)]
                    nb = 1 if kind(m) == "ki" else 2
                    sp.dma_start(dst[b:b + nb].rearrange("b p t -> p b t"), stage[:, c % 2, 0:nb, :]
                                 ).then_inc(stage_stored[c % 2], 16)
            for slot in range(4):
                sp.wait_ge(out_stored[slot], 16 * stored_before(M, slot))
            for slot in range(2):
                sp.wait_ge(stage_stored[slot], 16 * sum(1 for c in range(NC) if c % 2 == slot and turns(TT * c)))

        @block.gpsimd
        def _(pool):
            for c in range(NC):
                w = width(c)
                pool.wait_ge(w_hi_done, c + 1)
                nc.gpsimd.tensor_tensor(wlo[:, c % 2, :, 0:w], raw[:, c % 2, :, 0:w], whi[:, c % 2, :, 0:w],
                                        ALU.subtract).then_inc(w_lo_done, 1)

        @block.tensor
        def _(pe):
            def turn(m):
                if m < 0 or m >= M or not turns(m):
                    return
                x = count(turns, m)
                if x >= 2:
                    pe.wait_ge(kept_done, x - 1)
                pe.wait_ge(out_done, m + 1)
                for b in range(1 if kind(m) == "ki" else 2):
                    last = nc.tensor.transpose(turned[:, x % 2, b, :], out[:, m % 4, b * P:(b + 1) * P], ident[:, :])
                last.then_inc(turn_done, 1)

            for m in range(M):
                c, n = m // TT, m % TT
                w = width(c)
                if n == 0:
                    pe.wait_ge(w_lo_done, c + 1)
                if m >= 4:
                    pe.wait_ge(take_done, m - 3)
                tok = slice(n * P, (n + 1) * P) if n < TILES else slice(T - P, T)
                for k in range(KD):
                    ps = proj[:, m % 4, 0:w]
                    nc.tensor.matmul(ps, hhi[:, k, tok], whi[:, c % 2, k, 0:w], start=(k == 0), stop=False)
                    nc.tensor.matmul(ps, hhi[:, k, tok], wlo[:, c % 2, k, 0:w], start=False, stop=False)
                    last = nc.tensor.matmul(ps, hlo[:, k, tok], whi[:, c % 2, k, 0:w], start=False, stop=(k == KD - 1))
                last.then_inc(proj_done, 1)
                turn(m - 2)
            turn(M - 2)
            turn(M - 1)

        @block.scalar
        def _(act):
            def hi(c):
                w = width(c)
                act.wait_ge(w_loaded[c % 2], 16 * (c // 2) + 16)
                if c >= 2:
                    act.wait_ge(proj_done, TT * (c - 1))
                nc.scalar.activation(whi[:, c % 2, :, 0:w], raw[:, c % 2, :, 0:w], ACT.Copy).then_inc(w_hi_done, 1)

            def keep(m):
                if m < 0 or m >= M or not turns(m):
                    return
                c, n = m // TT, m % TT
                act.wait_ge(turn_done, count(turns, m + 1))
                prior = sum(1 for x in range(c) if x % 2 == c % 2 and turns(TT * x))
                if n == 0 and prior:
                    act.wait_ge(stage_stored[c % 2], 16 * prior)
                nb = 1 if kind(m) == "ki" else 2
                x = count(turns, m) % 2
                if n < TILES:
                    dst, src = stage[:, c % 2, 0:nb, n * P:(n + 1) * P], turned[:, x, 0:nb, :]
                else:
                    dst, src = stage[:, c % 2, 0:nb, SEQ:T], turned[:, x, 0:nb, SROW:P]
                nc.scalar.activation(dst, src, ACT.Copy).then_inc(kept_done, 1)

            hi(0)
            hi(1)
            for m in range(M):
                c, n = m // TT, m % TT
                w = width(c)
                act.wait_ge(proj_done, m + 1)
                if m >= 4:
                    act.wait_ge(out_done, m - 3)
                nc.scalar.activation(taken[:, m % 4, 0:w], proj[:, m % 4, 0:w], ACT.Copy).then_inc(take_done, 1)
                if normed(m):
                    act.wait_ge(take_done, m + 1)
                    nc.scalar.activation(sq[:, m % 2, :], taken[:, m % 4, :], ACT.Square).then_inc(sq_done, 1)
                    act.wait_ge(inv_done, count(normed, m + 1))
                    nc.scalar.activation(root[:, :], inv[:, :], ACT.Sqrt).then_inc(root_done, 1)
                keep(m - 3)
                if n == 0 and 1 <= c < NC - 1:
                    hi(c + 1)
            for m in range(M - 3, M):
                keep(m)

        @block.vector
        def _(dve):
            steps = [0]

            def done(ins):
                ins.then_inc(step, 1)
                steps[0] += 1
                dve.wait_ge(step, steps[0])

            def rope(src, n, heads):
                def over(table, a, b):
                    return table[:, n, a:b].unsqueeze(1).broadcast_to([P, heads, b - a])

                h = HD // 2
                a = ra[:, 0:heads * HD].rearrange("p (h d) -> p h d", d=HD)
                b = rb[:, 0:heads * HD].rearrange("p (h d) -> p h d", d=HD)
                done(nc.vector.tensor_tensor(a, src, over(cs, 0, HD), ALU.mult))
                done(nc.vector.tensor_tensor(b[:, :, 0:h], src[:, :, h:HD], over(sn, 0, h), ALU.mult))
                done(nc.vector.tensor_tensor(b[:, :, h:HD], src[:, :, 0:h], over(sn, h, HD), ALU.mult))
                return a, b

            dve.wait_ge(tables_in, 64)
            for m in range(M):
                c, n = m // TT, m % TT
                slot = m % 4
                x = taken[:, slot, :].rearrange("p (h d) -> p h d", d=HD)
                if normed(m):
                    dve.wait_ge(sq_done, count(normed, m + 1))
                    done(nc.vector.tensor_reduce(var[:, :], sq[:, m % 2, :].rearrange("p (h d) -> p h d", d=HD),
                                                 AX.X, ALU.add))
                    done(nc.vector.tensor_scalar(var[:, :], var[:, :], 1.0 / HD, EPS, ALU.mult, ALU.add))
                    nc.vector.reciprocal(inv[:, :], var[:, :]).then_inc(inv_done, 1)
                    dve.wait_ge(root_done, count(normed, m + 1))
                    newton_rsqrt(nc, done, root[:, :], var[:, :], tmp[:, :])
                    y = xn[:, :].rearrange("p (h d) -> p h d", d=HD)
                    done(nc.vector.tensor_tensor(y, x, root[:, :].unsqueeze(2).broadcast_to([P, 4, HD]), ALU.mult))
                    g = gains[:, 0 if kind(m) == "q" else 1, :].unsqueeze(1).broadcast_to([P, 4, HD])
                    done(nc.vector.tensor_tensor(y, y, g, ALU.mult))
                    x = y
                if m:
                    dve.wait_ge(out_done, m)
                if m >= 4:
                    dve.wait_ge(take_done, m + 1)
                    if turns(m - 4):
                        dve.wait_ge(turn_done, count(turns, m - 3))
                    if stores(m - 4):
                        dve.wait_ge(out_stored[slot], 16 * stored_before(m, slot))
                else:
                    dve.wait_ge(take_done, m + 1)
                if not turns(m):
                    nc.vector.tensor_copy(out[:, slot, :], taken[:, slot, :]).then_inc(out_done, 1)
                elif kind(m) == "ki":
                    x = x[:, 0:1, :]
                    a, b = rope(x, n, 1)
                    o = out[:, slot, :].rearrange("p (h d) -> p h d", d=HD)
                    done(nc.vector.tensor_tensor(o[:, 0:1, :], a, b, ALU.add))
                    done(nc.vector.tensor_copy(o[:, 1:2, :], o[:, 0:1, :]))
                    nc.vector.tensor_scalar(out[:, slot, 2 * HD:2 * HD + HEADS], taken[:, slot, HD:HD + HEADS],
                                            float(HEADS) ** -0.5, None, ALU.mult).then_inc(out_done, 1)
                else:
                    a, b = rope(x, n, 4)
                    if kind(m) == "q":
                        o = out[:, slot, :].rearrange("p (r g d) -> p g r d", g=2, d=HD)
                        a = a.rearrange("p (g r) d -> p g r d", g=2)
                        b = b.rearrange("p (g r) d -> p g r d", g=2)
                    else:
                        o = out[:, slot, :].rearrange("p (h d) -> p h d", d=HD)
                    nc.vector.tensor_tensor(o, a, b, ALU.add).then_inc(out_done, 1)


SLABS = TILES - 2 + 1
TOPK = 256
PAGES = 8
PS = 128
PAST = PAGES * PS
SW = PAST + DT
PADB = P + DT
FLOOR = -3.0e38
MASKED = -1.0e30
N_POOL = 80


def slab_width(s):
    return (s + 3) * P if s < SLABS - 1 else SW


def spread(wide):
    return wide[:, :].rearrange("p (b c) -> p b c", c=PADB)[:, :, 0:P].rearrange("p b (h t) -> p b h t", t=NS)[:, :, :, 0:DT]


def index_scores(nc, scores, qiT_d, kiT_d, wi_d, cache_idx_k, page_table, same_token, new_floor, ident):
    with Scope(nc, "idx") as s:
        qiT = s.sb("qiT", [P, 4, T])
        kiT = s.sb("kiT", [P, T])
        w = s.sb("w", [P, TILES, HEADS])
        w_rows = s.sb("w_rows", [P, 2])
        wide = s.sb("wide", [P, DB * PADB])
        pages = s.sb("pages", [P, 2, PAGES, HD])
        past = s.sb("past", [P, 2, PAST])
        relus = s.sb("relus", [P, 3, SW])
        part = s.sb("part", [P, SW])
        sel = s.sb("sel", [P, P])
        floor = s.sb("floor", [P, DT])
        table = s.sb("table", [1, DB * PAGES], I32)
        big = s.ps("big", [P, 6 * 512])
        turned = s.ps("turned", [P, 2, 512])
        loads = [s.sem("qiT_in"), s.sem("kiT_in"), s.sem("w_in"), s.sem("w_rows_in"), s.sem("sel_in"), s.sem("floor_in")]
        qiT_in, kiT_in, w_in, w_rows_in, sel_in, floor_in = loads
        table_in = s.sem("table_in")
        pages_in = [s.sem(f"pages_in{n}") for n in range(2)]
        zeroed, spread_done = s.sem("zeroed"), s.sem("spread_done")
        page_turned, low_kept, high_kept = s.sem("page_turned"), s.sem("low_kept"), s.sem("high_kept")
        seq_scored = s.sem("seq_scored")
        sample_relu, sample_part, sample_sum, sample_done = (s.sem("sample_relu"), s.sem("sample_part"),
                                                             s.sem("sample_sum"), s.sem("sample_done"))
        head_scored, relu_done, head_added, masked = (s.sem("head_scored"), s.sem("relu_done"), s.sem("head_added"),
                                                      s.sem("masked"))
        block = s.block()
        steps = [(t, h) for t in range(2, TILES) for h in range(HEADS)]

        @block.sync
        def _(sp):
            sp.dma_start(table[:, :], page_table.rearrange("(a b) n -> a (b n)", a=1)).then_inc(table_in, 16)
            sp.dma_start(qiT[:, :, :], qiT_d.rearrange("b p t -> p b t")).then_inc(qiT_in, 16)
            sp.dma_start(kiT[:, :], kiT_d[0]).then_inc(kiT_in, 16)
            sp.dma_start(w[:, :, :], wi_d[0:SEQ].rearrange("(n p) h -> p n h", p=P)).then_inc(w_in, 16)
            for h in range(4):
                sp.dma_start(w_rows[NS * h:NS * (h + 1), :], wi_d[SEQ:T, 2 * h:2 * h + 2]).then_inc(w_rows_in, 16)
            sp.dma_start(sel[:, :], same_token).then_inc(sel_in, 16)
            sp.dma_start(floor[:, :], new_floor).then_inc(floor_in, 16)
            sp.wait_ge(table_in, 16)

            def load(i, n, wait):
                if wait:
                    sp.wait_ge(page_turned, 4 * i - 2 + 2 * n)
                for g in range(PAGES):
                    page = sp.value_load(table[0:1, DynSlice(PAGES * (2 * i + n) + g, 1)], min_val=0, max_val=N_POOL - 1)
                    sp.dma_start(pages[:, n, g, :], cache_idx_k[0][DynSlice(page, 1)].rearrange("a s d -> (a s) d")
                                 ).then_inc(pages_in[n], 16)

            load(0, 0, False)
            load(0, 1, False)
            with sp.Fori(1, DB // 2) as i:
                for n in range(2):
                    load(i, n, True)

        @block.gpsimd
        def _(pool):
            for t in range(2, TILES):
                pool.wait_ge(head_added, HEADS * (t - 1))
                d = scores[:, t - 2, t * P:(t + 1) * P]
                nc.gpsimd.affine_select(out=d, in_=d, compare_op=ALU.is_ge, fill=FLOOR, base=0, pattern=[[-1, P]],
                                        channel_multiplier=1).then_inc(masked, 1)

        @block.tensor
        def _(pe):
            def turn(b):
                pe.wait_ge(pages_in[b % 2], 16 * PAGES * (b // 2 + 1))
                if b:
                    pe.wait_ge(low_kept, 2 * b)
                for x in range(2):
                    for g in range(4):
                        last = nc.tensor.transpose(turned[0:HD, x, g * PS:(g + 1) * PS], pages[:, b % 2, 4 * x + g, :],
                                                   ident[:, :])
                    last.then_inc(page_turned, 1)

            turn(0)
            pe.wait_ge(spread_done, 1)
            pe.wait_ge(kiT_in, 16)
            for b in range(DB):
                if b + 1 < DB:
                    turn(b + 1)
                pe.wait_ge(low_kept, 2 * b + 2)
                pe.wait_ge(high_kept, 2 * b + 2)
                for half in range(2):
                    r = slice(half * HD, (half + 1) * HD)
                    q = wide[r, b * P:(b + 1) * P]
                    for x in range(2):
                        nc.tensor.matmul(big[:, (3 * half + x) * 512:(3 * half + x + 1) * 512], q,
                                         past[r, b % 2, x * 512:(x + 1) * 512], start=(b == 0), stop=(b == DB - 1))
                    last = nc.tensor.matmul(big[:, (3 * half + 2) * 512:(3 * half + 2) * 512 + DT], q,
                                            kiT[r, SEQ + DT * b:SEQ + DT * (b + 1)], start=(b == 0), stop=(b == DB - 1))
                last.then_inc(seq_scored, 1)
            pe.wait_ge(sel_in, 16)
            pe.wait_ge(sample_part, 2)
            for x in range(3):
                n = 512 if x < 2 else DT
                last = nc.tensor.matmul(big[:, x * 512:x * 512 + n], sel[:, :], part[:, x * 512:x * 512 + n],
                                        start=True, stop=True)
            last.then_inc(sample_sum, 1)
            for a, (t, h) in enumerate(steps):
                if a < 2:
                    pe.wait_ge(sample_done, a + 1)
                if a >= 3:
                    pe.wait_ge(relu_done, a - 2)
                r = slice(h % 2 * HD, (h % 2 + 1) * HD)
                at = (a + 2) % 3 * 1024
                for x in range(0, (t + 1) * P, 512):
                    n = min(512, (t + 1) * P - x)
                    last = nc.tensor.matmul(big[:, at + x:at + x + n], qiT[r, h // 2, t * P:(t + 1) * P], kiT[r, x:x + n],
                                            start=True, stop=True)
                last.then_inc(head_scored, 1)

        @block.scalar
        def _(act):
            for b in range(DB):
                for x in range(2):
                    act.wait_ge(page_turned, 2 * b + x + 1)
                    if b >= 2:
                        act.wait_ge(seq_scored, b - 1)
                    nc.scalar.activation(past[0:HD, b % 2, x * 512:(x + 1) * 512], turned[0:HD, x, :], ACT.Copy
                                         ).then_inc(low_kept, 1)
            act.wait_ge(seq_scored, DB)
            for half in range(2):
                nc.scalar.activation(relus[:, half, 0:SW], big[:, half * 1536:half * 1536 + SW], ACT.Relu,
                                     scale=HD ** -0.5).then_inc(sample_relu, 1)
            for a, (t, h) in enumerate(steps):
                act.wait_ge(head_scored, a + 1)
                if a < 3:
                    act.wait_ge(sample_part, 2)
                else:
                    act.wait_ge(head_added, a - 2)
                n = (t + 1) * P
                at = (a + 2) % 3 * 1024
                nc.scalar.activation(relus[:, a % 3, 0:n], big[:, at:at + n], ACT.Relu, scale=HD ** -0.5
                                     ).then_inc(relu_done, 1)

        @block.vector
        def _(dve):
            nc.vector.memset(wide[:, :], 0.0).then_inc(zeroed, 1)
            dve.wait_ge(zeroed, 1)
            dve.wait_ge(qiT_in, 16)
            nc.vector.tensor_copy(spread(wide), qiT[:, :, SEQ:T].rearrange("p h (b j) -> p b h j", j=DT)
                                  ).then_inc(spread_done, 1)
            for b in range(DB):
                for x in range(2):
                    dve.wait_ge(low_kept, 2 * b + x + 1)
                    nc.vector.tensor_copy(past[HD:P, b % 2, x * 512:(x + 1) * 512], past[0:HD, b % 2, x * 512:(x + 1) * 512]
                                          ).then_inc(high_kept, 1)
            dve.wait_ge(w_rows_in, 64)
            dve.wait_ge(sample_relu, 1)
            nc.vector.tensor_scalar(part[:, :], relus[:, 0, 0:SW], w_rows[:, 0:1], None, ALU.mult).then_inc(sample_part, 1)
            dve.wait_ge(sample_part, 1)
            dve.wait_ge(sample_relu, 2)
            nc.vector.scalar_tensor_tensor(part[:, :], relus[:, 1, 0:SW], w_rows[:, 1:2], part[:, :], ALU.mult, ALU.add
                                           ).then_inc(sample_part, 1)
            dve.wait_ge(sample_sum, 1)
            dve.wait_ge(floor_in, 16)
            nc.vector.tensor_tensor(scores[:, SLABS - 1, PAST:SW], big[:, PAST:SW], floor[:, :], ALU.add
                                    ).then_inc(sample_done, 1)
            nc.vector.tensor_copy(scores[:, SLABS - 1, 0:PAST], big[:, 0:PAST]).then_inc(sample_done, 1)
            dve.wait_ge(w_in, 16)
            for a, (t, h) in enumerate(steps):
                dve.wait_ge(relu_done, a + 1)
                n = (t + 1) * P
                sc = scores[:, t - 2, 0:n]
                if h == 0:
                    i = nc.vector.tensor_scalar(sc, relus[:, a % 3, 0:n], w[:, t, 0:1], None, ALU.mult)
                else:
                    dve.wait_ge(head_added, a)
                    i = nc.vector.scalar_tensor_tensor(sc, relus[:, a % 3, 0:n], w[:, t, h:h + 1], sc, ALU.mult, ALU.add)
                i.then_inc(head_added, 1)


SECTIONS = [("silu", 1608, 2, 0), ("silu", 3144, 2, 4), ("forget", 2120, 2, 8), ("gate", 3656, 8, 16)]
FEATS = 32


def select_keys_and_project(nc, scores, masks, hhi, hlo, w_in, feat_d):
    with Scope(nc, "sel") as s:
        raw = s.sb("raw", [P, 2, UNIT])
        whi = s.sb("whi", [P, 2, UNIT], F32R)
        wlo = s.sb("wlo", [P, 2, UNIT], F32R)
        stage = s.sb("stage", [P, 2, 2, T])
        over = s.sb("over", [P, SW], mybir.dt.bfloat16)
        equal = s.sb("equal", [P, SW], mybir.dt.bfloat16)
        rank = s.sb("rank", [P, SW])
        count = s.sb("count", [P, SLABS])
        bits = s.sb("bits", [P, SLABS], I32)
        cand = s.sb("cand", [P, SLABS], I32)
        flip = s.sb("flip", [P, SLABS], I32)
        gain = s.sb("gain", [P, SLABS], I32)
        bit = s.sb("bit", [P, SLABS], I32)
        bitf = s.sb("bitf", [P, SLABS])
        thr = s.sb("thr", [P, SLABS], I32)
        proj = s.ps("proj", [P, 2, NCH, 512])
        w_loaded = [s.sem(f"w_loaded{n}") for n in range(2)]
        w_hi_done, w_lo_done = s.sem("w_hi_done"), s.sem("w_lo_done")
        proj_done, proj_read, kept_done = s.sem("proj_done"), s.sem("proj_read"), s.sem("kept_done")
        stage_stored = [s.sem(f"stage_stored{n}") for n in range(2)]
        step, passes = s.sem("step"), s.sem("passes")
        block = s.block()
        wv = w_in[0].rearrange("(k p) f -> p k f", p=P)
        pairs_before = [sum(x[2] for x in SECTIONS[:n]) for n in range(len(SECTIONS) + 1)]
        stored_per = {"silu": 1, "forget": 2, "gate": 1}
        stored_before = [sum(x[2] * stored_per[x[0]] for x in SECTIONS[:n]) for n in range(len(SECTIONS) + 1)]

        def sections(engine, body, peel_last=False):
            for n, (_, _, pairs, _) in enumerate(SECTIONS):
                first = 0
                end = pairs - 1 if peel_last and n == len(SECTIONS) - 1 else pairs
                if n == 0:
                    body(0, 0, 0, True)
                    first = 1
                with engine.Fori(first, end) as i:
                    body(n, i, i + pairs_before[n], False)
            if peel_last:
                body(len(SECTIONS) - 1, end, end + pairs_before[-2], False, True)

        @block.sync
        def _(sp):
            def body(n, i, pair, first):
                kind, col, _, at = SECTIONS[n]
                for u in range(2):
                    if not first:
                        sp.wait_ge(w_lo_done, 2 * pair + u - 1)
                    sp.dma_start(raw[:, u, :].rearrange("p (k f) -> p k f", k=KD), wv[:, :, DynSlice(col + (2 * i + u) * P, P)]
                                 ).then_inc(w_loaded[u], 16)

            sections(sp, body)

        @block.gpsimd
        def _(pool):
            def body(n, i, pair, first):
                for u in range(2):
                    pool.wait_ge(w_hi_done, 2 * pair + u + 1)
                    nc.gpsimd.tensor_tensor(wlo[:, u, :], raw[:, u, :], whi[:, u, :], ALU.subtract).then_inc(w_lo_done, 1)

            sections(pool, body)

        @block.tensor
        def _(pe):
            def body(n, i, pair, first):
                for u in range(2):
                    pe.wait_ge(w_lo_done, 2 * pair + u + 1)
                    for c in range(NCH):
                        cols = slice(c * CH, (c + 1) * CH)
                        if not first:
                            pe.wait_ge(proj_read, 6 * pair + 3 * u + c - 5)
                        for k in range(KD):
                            w = slice(k * P, (k + 1) * P)
                            last = split_product(nc, proj[:, u, c, 0:CH], whi[:, u, w], wlo[:, u, w], hhi[:, k, cols],
                                                 hlo[:, k, cols], k == 0, k == KD - 1)
                        last.then_inc(proj_done, 1)

            sections(pe, body)

        @block.scalar
        def _(act):
            def hi(u, pair):
                act.wait_ge(w_loaded[u], 16 * pair + 16)
                nc.scalar.activation(whi[:, u, :], raw[:, u, :], ACT.Copy).then_inc(w_hi_done, 1)

            def body(n, i, pair, first, last=False):
                kind, _, _, at = SECTIONS[n]
                for u in range(2):
                    if not first:
                        stored = stored_before[n] + stored_per[kind] * i
                        act.wait_ge(stage_stored[u], 16 * stored)
                    for c in range(NCH):
                        cols = slice(c * CH, (c + 1) * CH)
                        act.wait_ge(proj_done, 6 * pair + 3 * u + c + 1)
                        if kind == "forget":
                            nc.scalar.activation(stage[:, u, 1, cols], proj[:, u, c, 0:CH], ACT.Sigmoid, scale=-1.0
                                                 ).then_inc(kept_done, 1)
                        func = ACT.Silu if kind == "silu" else ACT.Sigmoid
                        nc.scalar.activation(stage[:, u, 0, cols], proj[:, u, c, 0:CH], func).then_inc(proj_read, 1)
                    if not last:
                        hi(u, pair + 1)
                    act.wait_ge(proj_read, 6 * pair + 3 * u + 3)
                    act.dma_start(feat_d[DynSlice(at + 2 * i + u, 1)].rearrange("a p t -> (a p) t"), stage[:, u, 0, :]
                                  ).then_inc(stage_stored[u], 16)
                    if kind == "forget":
                        act.wait_ge(kept_done, 6 * i + 3 * u + 3)
                        act.dma_start(feat_d[DynSlice(at + 4 + 2 * i + u, 1)].rearrange("a p t -> (a p) t"),
                                      stage[:, u, 1, :]).then_inc(stage_stored[u], 16)

            hi(0, 0)
            hi(1, 0)
            sections(act, body, True)
            for u in range(2):
                act.wait_ge(stage_stored[u], 16 * stored_before[-1])

        @block.vector
        def _(dve):
            steps = [0]

            def count_all(r):
                for x in range(SLABS):
                    n = slab_width(x)
                    if x >= 2:
                        dve.wait_ge(passes, SLABS * r + x - 1)
                    flags = (over, equal)[x % 2]
                    nc.vector.tensor_scalar(flags[:, 0:n], scores[:, x, 0:n], thr[:, x:x + 1].bitcast(F32), None,
                                            ALU.is_ge, ALU.add, accum_out=count[:, x:x + 1]).then_inc(passes, 1)
                dve.wait_ge(passes, SLABS * (r + 1))

            def done(ins, at=None):
                ins.then_inc(step, 1)
                steps[0] += 1
                dve.wait_ge(step, steps[0] if at is None else at)

            done(nc.vector.memset(thr[:, :], 0))
            done(nc.vector.memset(bits[:, :], 0))
            done(nc.vector.memset(bit[:, :], 1 << 30))
            done(nc.vector.memset(bitf[:, :], float(1 << 30)))
            count_all(0)
            done(nc.vector.tensor_scalar(flip[:, :], count[:, :], TOPK - 0.5, -1.0, ALU.is_ge, ALU.add))
            base, per = steps[0], 7
            with dve.Fori(0, 31) as r:
                at = [per * r + (base + 1 + n) for n in range(per)]
                done(nc.vector.tensor_tensor(cand[:, :], bits[:, :], bit[:, :], ALU.bitwise_or), at[0])
                done(nc.vector.tensor_tensor(thr[:, :], cand[:, :], flip[:, :], ALU.bitwise_xor), at[1])
                count_all(r + 1)
                done(nc.vector.tensor_scalar(gain[:, :], count[:, :], TOPK - 0.5, None, ALU.is_ge), at[2])
                done(nc.vector.tensor_tensor(gain[:, :], gain[:, :], bitf[:, :], ALU.mult), at[3])
                done(nc.vector.tensor_tensor(bits[:, :], bits[:, :], gain[:, :], ALU.bitwise_or), at[4])
                done(nc.vector.tensor_scalar(bit[:, :], bit[:, :], 1, None, ALU.logical_shift_right), at[5])
                done(nc.vector.tensor_scalar(bitf[:, :], bitf[:, :], 0.5, None, ALU.mult), at[6])
            steps[0] = base + per * 31
            done(nc.vector.tensor_tensor(thr[:, :], bits[:, :], flip[:, :], ALU.bitwise_xor))
            for x in range(SLABS):
                n = slab_width(x)
                sc, t = scores[:, x, 0:n], thr[:, x:x + 1].bitcast(F32)
                done(nc.vector.tensor_scalar(over[:, 0:n], sc, t, None, ALU.is_gt, ALU.add, accum_out=count[:, x:x + 1]))
                done(nc.vector.tensor_scalar(count[:, x:x + 1], count[:, x:x + 1], -1.0, float(TOPK), ALU.mult, ALU.add))
                done(nc.vector.tensor_scalar(equal[:, 0:n], sc, t, None, ALU.is_equal))
                done(nc.vector.tensor_tensor_scan(rank[:, 0:n], equal[:, 0:n], equal[:, 0:n], 0.0, ALU.add, ALU.max))
                done(nc.vector.scalar_tensor_tensor(equal[:, 0:n], rank[:, 0:n], count[:, x:x + 1], equal[:, 0:n],
                                                    ALU.is_le, ALU.mult))
                done(nc.vector.scalar_tensor_tensor(over[:, 0:n], equal[:, 0:n], -1.0, over[:, 0:n], ALU.add, ALU.add))
                done(nc.vector.tensor_scalar(masks[:, x, 0:n], over[:, 0:n], -MASKED, None, ALU.mult))


def attention(nc, mixed_d, masks, qT_d, kT_d, v_prompt, v_sample, cache_k, cache_v, page_table, causal, own, ident):
    with Scope(nc, "att") as s:
        attT = s.sb("attT", [P, 4, T])
        qT = s.sb("qT", [P, 4, T])
        kT = s.sb("kT", [P, 2, T])
        v = s.sb("v", [P, TILES, KV * HD])
        v_new = s.sb("v_new", [NS, KV * HD])
        causal_sb = s.sb("causal", [P, 2 * P])
        own_sb = s.sb("own", [P, DB, DT])
        table = s.sb("table", [1, DB * PAGES], I32)
        wide = s.sb("wide", [P, DB * PADB])
        pages = s.sb("pages", [P, 2, PAGES, KV * HD])
        past = s.sb("past", [P, 2, 2, PAST])
        logits = s.sb("logits", [P, 2, SW])
        probs = s.sb("probs", [P, 2, SW])
        new_probs = s.sb("new_probs", [P, 2, DB, DT])
        probsT = s.sb("probsT", [P, 2, PAGES, P])
        new_probsT = s.sb("new_probsT", [NS, 2, P])
        top = s.sb("top", [P, 2])
        bias = s.sb("bias", [P, 2])
        mass = s.sb("mass", [P, 2, HEADS])
        share = s.sb("share", [P, HEADS])
        heads = s.sb("heads", [P, HEADS * HD])
        big = s.ps("big", [P, 6 * 512])
        turned = s.ps("turned", [P, 2, 512])
        names = ("table", "qT", "kT", "v", "v_new", "causal", "own")
        loaded = {n: s.sem(f"{n}_in") for n in names}
        pages_in = [s.sem(f"pages_in{n}") for n in range(2)]
        zeroed, spread_done = s.sem("zeroed"), s.sem("spread_done")
        page_turned, low_kept, high_kept = s.sem("page_turned"), s.sem("low_kept"), s.sem("high_kept")
        seq_scored, s_logits, s_bias, s_exp, s_norm = (s.sem("seq_scored"), s.sem("s_logits"), s.sem("s_bias"),
                                                       s.sem("s_exp"), s.sem("s_norm"))
        s_share, s_new, s_out, s_kept = s.sem("s_share"), s.sem("s_new"), s.sem("s_out"), s.sem("s_kept")
        new_turned, new_kept = s.sem("new_turned"), s.sem("new_kept")
        scored, masked, top_done, bias_done, exp_done = (s.sem("scored"), s.sem("masked"), s.sem("top_done"),
                                                         s.sem("bias_done"), s.sem("exp_done"))
        low_turned, high_turned, low_ready, high_ready = (s.sem("low_turned"), s.sem("high_turned"), s.sem("low_ready"),
                                                          s.sem("high_ready"))
        mixed, share_done, heads_done, out_turned, out_kept = (s.sem("mixed"), s.sem("share_done"), s.sem("heads_done"),
                                                               s.sem("out_turned"), s.sem("out_kept"))
        stored = s.sem("stored")
        block = s.block()
        steps = [(t, h) for t in range(TILES) for h in range(HEADS)]
        SCALE = HD ** -0.5
        out_ps = big[:, 4 * 512:5 * 512]
        back_ps = big[:, 5 * 512:6 * 512]

        def high_before(a):
            return sum(1 for t, _ in steps[:a] if t >= 4)

        @block.sync
        def _(sp):
            for n, dst, src in (("table", table[:, :], page_table.rearrange("(a b) n -> a (b n)", a=1)),
                                ("qT", qT[:, :, :], qT_d.rearrange("b p t -> p b t")),
                                ("kT", kT[:, :, :], kT_d.rearrange("b p t -> p b t"))):
                sp.dma_start(dst, src).then_inc(loaded[n], 16)
            sp.wait_ge(loaded["table"], 16)

            def load(cache, i, n, sem=None, value=None):
                if sem is not None:
                    sp.wait_ge(sem, value)
                for g in range(PAGES):
                    page = sp.value_load(table[0:1, DynSlice(PAGES * (2 * i + n) + g, 1)], min_val=0, max_val=N_POOL - 1)
                    sp.dma_start(pages[:, n, g, :], cache[DynSlice(page, 1)].rearrange("a s d -> (a s) d")
                                 ).then_inc(pages_in[n], 16)

            load(cache_k, 0, 0)
            load(cache_k, 0, 1)
            for n, dst, src in (("v", v[:, :, :], v_prompt.rearrange("(n p) d -> p n d", p=P)),
                                ("v_new", v_new[:, :], v_sample), ("causal", causal_sb[:, :], causal),
                                ("own", own_sb[:, :, :], own)):
                sp.dma_start(dst, src).then_inc(loaded[n], 16)
            with sp.Fori(1, DB // 2) as i:
                for n in range(2):
                    load(cache_k, i, n, page_turned, 8 * i - 4 + 4 * n)
            for n in range(2):
                load(cache_v, 0, n, page_turned, 4 * (DB - 1 + n))
            with sp.Fori(1, DB // 2) as i:
                for n in range(2):
                    load(cache_v, i, n, s_out, 2 * i - 1 + n)
            sp.wait_ge(s_kept, 2)
            sp.wait_ge(out_kept, TILES)
            sp.dma_start(mixed_d[0:4].rearrange("b p t -> p b t"), attT[:, :, :]).then_inc(stored, 16)
            sp.wait_ge(stored, 16)

        @block.tensor
        def _(pe):
            def turn(b):
                pe.wait_ge(pages_in[b % 2], 16 * PAGES * (b // 2 + 1))
                for f in range(4):
                    x = f % 2
                    if 2 * b + f // 2:
                        pe.wait_ge((low_kept, high_kept)[x], 2 * b + f // 2)
                    for g in range(4):
                        last = nc.tensor.transpose(turned[:, x, g * PS:(g + 1) * PS],
                                                   pages[:, b % 2, 4 * x + g, f // 2 * P:(f // 2 + 1) * P], ident[:, :])
                    last.then_inc(page_turned, 1)

            turn(0)
            pe.wait_ge(spread_done, 1)
            pe.wait_ge(loaded["kT"], 16)
            for b in range(DB):
                if b + 1 < DB:
                    turn(b + 1)
                pe.wait_ge(low_kept, 2 * b + 2)
                pe.wait_ge(high_kept, 2 * b + 2)
                for G in range(2):
                    for g in range(2):
                        r = slice(g * HD, (g + 1) * HD)
                        q = wide[r, b * P + G * 2 * NS:b * P + (G + 1) * 2 * NS]
                        for x in range(2):
                            nc.tensor.matmul(big[r, (3 * G + x) * 512:(3 * G + x + 1) * 512], q,
                                             past[r, b % 2, G, x * 512:(x + 1) * 512], start=(b == 0), stop=(b == DB - 1))
                        last = nc.tensor.matmul(big[r, (3 * G + 2) * 512:(3 * G + 2) * 512 + DT], q,
                                                kT[r, G, SEQ + DT * b:SEQ + DT * (b + 1)], start=(b == 0),
                                                stop=(b == DB - 1))
                last.then_inc(seq_scored, 1)
            for f in range(4):
                G, x = f // 2, f % 2
                pe.wait_ge(s_norm, G + 1)
                pe.wait_ge((low_kept, high_kept)[x], 2 * DB + G)
                for g in range(4):
                    last = nc.tensor.transpose(turned[:, x, g * P:(g + 1) * P],
                                               probs[:, G, (4 * x + g) * PS:(4 * x + g + 1) * PS], ident[:, :])
                last.then_inc(page_turned, 1)
            pe.wait_ge(s_new, 2)
            pe.wait_ge(s_logits, 2)
            for G in range(2):
                last = nc.tensor.transpose(big[0:NS, 512 + G * P:512 + (G + 1) * P],
                                           new_probs[:, G, :, :].rearrange("p b j -> p (b j)"), ident[:, :])
            last.then_inc(new_turned, 1)
            pe.wait_ge(new_kept, 1)
            pe.wait_ge(loaded["v_new"], 16)
            for G in range(2):
                for g in range(2):
                    r = slice(g * HD, (g + 1) * HD)
                    kv = 2 * G + g
                    nc.tensor.matmul(big[r, 3 * G * 512:3 * G * 512 + 2 * NS], v_new[:, kv * HD:(kv + 1) * HD],
                                     new_probsT[:, G, r], start=True, stop=False)
            pe.wait_ge(low_kept, 2 * DB + 2)
            pe.wait_ge(high_kept, 2 * DB + 2)
            for b in range(DB):
                pe.wait_ge(pages_in[b % 2], 16 * PAGES * (DB // 2 + b // 2 + 1))
                for G in range(2):
                    for g in range(2):
                        r = slice(g * HD, (g + 1) * HD)
                        kv = 2 * G + g
                        o = big[r, 3 * G * 512:3 * G * 512 + 2 * NS].rearrange("p (r t) -> p r t", t=NS)
                        for n in range(PAGES):
                            p = probsT[:, G, n, r].rearrange("p (r t) -> p r t", t=NS)
                            last = nc.tensor.matmul(o[:, :, DT * b:DT * (b + 1)], pages[:, b % 2, n, kv * HD:(kv + 1) * HD],
                                                    p[:, :, DT * b:DT * (b + 1)], start=False,
                                                    stop=(b == DB - 1 and n == PAGES - 1))
                last.then_inc(s_out, 1)

            def score(a):
                t, h = steps[a]
                if a < 2:
                    pe.wait_ge(s_kept, 2)
                else:
                    pe.wait_ge(masked, a - 1)
                g, rr = h // 2, h % 2
                r = slice(g % 2 * HD, (g % 2 + 1) * HD)
                for x in range(0, (t + 1) * P, 512):
                    n = min(512, (t + 1) * P - x)
                    last = nc.tensor.matmul(big[:, a % 2 * 1024 + x:a % 2 * 1024 + x + n],
                                            qT[r, g // 2 * 2 + rr, t * P:(t + 1) * P], kT[r, g // 2, x:x + n],
                                            start=True, stop=True)
                last.then_inc(scored, 1)

            def turn_probs(a):
                t, h = steps[a]
                pe.wait_ge(exp_done, a + 1)
                for x in range(1 if t < 4 else 2):
                    if x == 0 and a:
                        pe.wait_ge(low_ready, a)
                    if x == 1 and high_before(a):
                        pe.wait_ge(high_ready, high_before(a))
                    for j in range(4 * x, min(4 * x + 4, t + 1)):
                        last = nc.tensor.transpose(turned[:, x, (j - 4 * x) * P:(j - 4 * x + 1) * P],
                                                   probs[:, a % 2, j * P:(j + 1) * P], ident[:, :])
                    last.then_inc((low_turned, high_turned)[x], 1)

            def mix(a):
                t, h = steps[a]
                if h == 0 and t:
                    pe.wait_ge(heads_done, 2 * t)
                pe.wait_ge(low_ready, a + 1)
                if t >= 4:
                    pe.wait_ge(high_ready, high_before(a + 1))
                for j in range(t + 1):
                    last = nc.tensor.matmul(out_ps[:, h * HD:(h + 1) * HD], probsT[:, a % 2, j, :],
                                            v[:, j, h // 2 * HD:(h // 2 + 1) * HD], start=(j == 0), stop=(j == t))
                last.then_inc(mixed, 1)

            def turn_out(t):
                pe.wait_ge(heads_done, 2 * t + 2)
                if t:
                    pe.wait_ge(out_kept, t)
                for n in range(4):
                    last = nc.tensor.transpose(back_ps[:, n * P:(n + 1) * P], heads[:, n * P:(n + 1) * P], ident[:, :])
                last.then_inc(out_turned, 1)

            pe.wait_ge(loaded["v"], 16)
            for a in range(len(steps) + 4):
                if a < len(steps):
                    score(a)
                if 1 <= a <= len(steps):
                    turn_probs(a - 1)
                if 2 <= a <= len(steps) + 1:
                    mix(a - 2)
                if a >= 11 and (a - 3) % HEADS == 0:
                    turn_out((a - 3) // HEADS - 1)

        @block.scalar
        def _(act):
            act.wait_ge(spread_done, 1)
            for b in range(DB):
                for G in range(2):
                    act.wait_ge(page_turned, 4 * b + 2 * G + 2)
                    if b >= 2:
                        act.wait_ge(seq_scored, b - 1)
                    nc.scalar.activation(past[:, b % 2, G, 512:1024], turned[:, 1, :], ACT.Copy).then_inc(high_kept, 1)
            for G in range(2):
                act.wait_ge(s_bias, G + 1)
                nc.scalar.activation(probs[:, G, :], logits[:, G, :], ACT.Exp, bias=bias[:, G:G + 1], scale=SCALE,
                                     accum_out=mass[:, 0, G:G + 1]).then_inc(s_exp, 1)
            for G in range(2):
                act.wait_ge(page_turned, 4 * DB + 2 * G + 2)
                nc.scalar.activation(probsT[:, G, 4:8, :].rearrange("p a b -> p (a b)"), turned[:, 1, :], ACT.Copy
                                     ).then_inc(high_kept, 1)
            act.wait_ge(s_out, DB)
            for G in range(2):
                nc.scalar.activation(attT[:, 2 * G:2 * G + 2, SEQ:T],
                                     big[:, 3 * G * 512:3 * G * 512 + 2 * NS].rearrange("p (r t) -> p r t", t=NS), ACT.Copy
                                     ).then_inc(s_kept, 1)
            for a in range(len(steps) + 4):
                if a < len(steps):
                    t, h = steps[a]
                    n = (t + 1) * P
                    act.wait_ge(bias_done, a + 1)
                    if a < 2:
                        act.wait_ge(s_out, DB)
                    else:
                        act.wait_ge(low_turned, a - 1)
                        if high_before(a - 1):
                            act.wait_ge(high_turned, high_before(a - 1))
                    if h == 0 and t >= 2:
                        act.wait_ge(share_done, t - 1)
                    nc.scalar.activation(probs[:, a % 2, 0:n], logits[:, a % 2, 0:n], ACT.Exp, bias=bias[:, a % 2:a % 2 + 1],
                                         scale=SCALE, accum_out=mass[:, t % 2, h:h + 1]).then_inc(exp_done, 1)
                if 1 <= a <= len(steps) and steps[a - 1][0] >= 4:
                    t, h = steps[a - 1]
                    act.wait_ge(high_turned, high_before(a))
                    if a >= 3:
                        act.wait_ge(mixed, a - 2)
                    nc.scalar.activation(probsT[:, (a - 1) % 2, 4:t + 1, :],
                                         turned[:, 1, 0:(t - 3) * P].rearrange("p (a b) -> p a b", b=P), ACT.Copy
                                         ).then_inc(high_ready, 1)
                if a >= 11 and (a - 3) % HEADS == 0:
                    t = (a - 3) // HEADS - 1
                    act.wait_ge(out_turned, t + 1)
                    nc.scalar.activation(attT[:, :, t * P:(t + 1) * P], back_ps.rearrange("p (a b) -> p a b", b=P), ACT.Copy
                                         ).then_inc(out_kept, 1)

        @block.vector
        def _(dve):
            nc.vector.memset(wide[:, :], 0.0).then_inc(zeroed, 1)
            dve.wait_ge(zeroed, 1)
            dve.wait_ge(loaded["qT"], 16)
            nc.vector.tensor_copy(spread(wide), qT[:, :, SEQ:T].rearrange("p h (b j) -> p b h j", j=DT)
                                  ).then_inc(spread_done, 1)
            for b in range(DB):
                for G in range(2):
                    dve.wait_ge(page_turned, 4 * b + 2 * G + 1)
                    if b >= 2:
                        dve.wait_ge(seq_scored, b - 1)
                    nc.vector.tensor_copy(past[:, b % 2, G, 0:512], turned[:, 0, :]).then_inc(low_kept, 1)
            dve.wait_ge(seq_scored, DB)
            for G in range(2):
                nc.vector.tensor_tensor_reduce(logits[:, G, :], masks[:, SLABS - 1, :], big[:, 1536 * G:1536 * G + SW], 1.0,
                                               FLOOR, ALU.add, ALU.max, top[:, G:G + 1]).then_inc(s_logits, 1)
                dve.wait_ge(s_logits, G + 1)
                nc.vector.tensor_scalar(bias[:, G:G + 1], top[:, G:G + 1], -SCALE, None, ALU.mult).then_inc(s_bias, 1)
            dve.wait_ge(loaded["own"], 16)
            for G in range(2):
                dve.wait_ge(s_exp, G + 1)
                nc.vector.reciprocal(share[:, G:G + 1], mass[:, 0, G:G + 1]).then_inc(s_share, 1)
                dve.wait_ge(s_share, G + 1)
                nc.vector.tensor_scalar(probs[:, G, :], probs[:, G, :], share[:, G:G + 1], None, ALU.mult).then_inc(s_norm, 1)
                dve.wait_ge(s_norm, G + 1)
                nc.vector.tensor_tensor(new_probs[:, G, :, :], own_sb[:, :, :],
                                        probs[:, G, PAST:SW].unsqueeze(1).broadcast_to([P, DB, DT]), ALU.mult
                                        ).then_inc(s_new, 1)
            for G in range(2):
                dve.wait_ge(page_turned, 4 * DB + 2 * G + 1)
                nc.vector.tensor_copy(probsT[:, G, 0:4, :].rearrange("p a b -> p (a b)"), turned[:, 0, :]
                                      ).then_inc(low_kept, 1)
            dve.wait_ge(new_turned, 1)
            nc.vector.tensor_copy(new_probsT[:, :, :].rearrange("p a b -> p (a b)"), big[0:NS, 512:512 + 2 * P]
                                  ).then_inc(new_kept, 1)
            dve.wait_ge(loaded["causal"], 16)
            for a in range(len(steps) + 4):
                if a < len(steps):
                    t, h = steps[a]
                    n = (t + 1) * P
                    dve.wait_ge(scored, a + 1)
                    if a < 2:
                        dve.wait_ge(s_exp, 2)
                    else:
                        dve.wait_ge(exp_done, a - 1)
                    m = masks[:, t - 2, 0:n] if t >= 2 else causal_sb[:, (1 - t) * P:2 * P]
                    nc.vector.tensor_tensor_reduce(logits[:, a % 2, 0:n], m, big[:, a % 2 * 1024:a % 2 * 1024 + n], 1.0,
                                                   FLOOR, ALU.add, ALU.max, top[:, a % 2:a % 2 + 1]).then_inc(masked, 1)
                    dve.wait_ge(masked, a + 1)
                    nc.vector.tensor_scalar(bias[:, a % 2:a % 2 + 1], top[:, a % 2:a % 2 + 1], -SCALE, None, ALU.mult
                                            ).then_inc(bias_done, 1)
                if 1 <= a <= len(steps):
                    t, h = steps[a - 1]
                    n = min(t + 1, 4)
                    dve.wait_ge(low_turned, a)
                    if a == 1:
                        dve.wait_ge(s_out, DB)
                    if a >= 3:
                        dve.wait_ge(mixed, a - 2)
                    nc.vector.tensor_copy(probsT[:, (a - 1) % 2, 0:n, :],
                                          turned[:, 0, 0:n * P].rearrange("p (a b) -> p a b", b=P)).then_inc(low_ready, 1)
                if a >= 10 and (a - 2) % HEADS == 0:
                    t = (a - 2) // HEADS - 1
                    if t:
                        dve.wait_ge(heads_done, 2 * t)
                    nc.vector.reciprocal(share[:, :], mass[:, t % 2, :]).then_inc(share_done, 1)
                    dve.wait_ge(share_done, t + 1)
                    dve.wait_ge(mixed, HEADS * (t + 1))
                    if t:
                        dve.wait_ge(out_turned, t)
                    half = HEADS * HD // 2
                    for G in range(2):
                        src = out_ps[:, G * half:(G + 1) * half].rearrange("p (g r d) -> p g r d", g=2, r=2)
                        dst = heads[:, G * half:(G + 1) * half].rearrange("p (r g d) -> p g r d", g=2, r=2)
                        w = share[:, 4 * G:4 * G + 4].rearrange("p (g r) -> p g r", g=2).unsqueeze(3)
                        nc.vector.tensor_tensor(dst, src, w.broadcast_to([P, 2, 2, HD]), ALU.mult).then_inc(heads_done, 1)


HG = 4
LEVELS = [64, 32, 16, 8, 4, 2, 1]
NL = len(LEVELS) + 1
UW = SEQ // 2 + NS


def recurrence(nc, mixed_d, feat_d, hv_d, state_in, state_prompt, state_sample, bound, hg_gain, resets, level_masks, owner,
               ident, ones):
    with Scope(nc, "hg") as s:
        f = s.sb("f", [P, T])
        G = s.sb("G", [P, T])
        eG = s.sb("eG", [P, T])
        q_in = s.sb("q_in", [P, T])
        kd = s.sb("kd", [P, T])
        decay = s.sb("decay", [P, NL, UW])
        qL = s.sb("qL", [P, NL, T])
        kL = s.sb("kL", [P, NL, T])
        hv = s.sb("hv", [P, TT, P])
        st = s.sb("st", [P, DB, P])
        gate = s.sb("gate", [P, T])
        kept = s.sb("kept", [P, NL, P])
        attn = s.sb("attn", [P, 2, P])
        kdT = s.sb("kdT", [P, 2, P])
        S = s.sb("S", [P, 2, P])
        own_v = s.sb("own_v", [NS, DB, P])
        new_st = s.sb("new_st", [P, DB, P])
        oT = s.sb("oT", [P, T])
        rec = s.sb("rec", [P, T])
        sq = s.sb("sq", [P, UW])
        var = s.sb("var", [P, UW])
        root = s.sb("root", [P, UW])
        reset = s.sb("reset", [P, T])
        masks = s.sb("masks", [P, NL, P])
        own = s.sb("own", [NS, DB])
        lb_in = s.sb("lb_in", [P, 2, HG])
        lb = s.sb("lb", [P, HG])
        omlb = s.sb("omlb", [P, HG])
        lmax = s.sb("lmax", [P, HG])
        lexp = s.sb("lexp", [P, 2, HG])
        lsum = s.sb("lsum", [P, HG])
        gain = s.sb("gain", [P, 1])
        pairs = s.ps("pairs", [P, NL, P])
        o_ps = s.ps("o_ps", [P, 2, 512])
        kd_ps = s.ps("kd_ps", [P, 512])
        st_ps = s.ps("st_ps", [P, 512])
        sum_ps = s.ps("sum_ps", [P, 2, 512])
        tmp = sq

        def two(name):
            return [s.sem(f"{name}{u}") for u in range(2)]

        f_loaded, k_loaded, q_loaded, hv_loaded, gate_loaded = (two("f_loaded"), two("k_loaded"), two("q_loaded"),
                                                                two("hv_loaded"), two("gate_loaded"))
        st_loaded, consts = s.sem("st_loaded"), s.sem("consts")
        bound_step, bound_exp, bound_ready = s.sem("bound_step"), s.sem("bound_exp"), s.sem("bound_ready")
        f_ready, log_ready, G_ready, eG_ready = s.sem("f_ready"), s.sem("log_ready"), s.sem("G_ready"), s.sem("eG_ready")
        q_ready, k_ready, q_in_ready = s.sem("q_ready"), s.sem("k_ready"), s.sem("q_in_ready")
        dist_ready, decay_ready, qL_ready, kL_ready = (s.sem("dist_ready"), s.sem("decay_ready"), s.sem("qL_ready"),
                                                       s.sem("kL_ready"))
        pairs_done, kept_done, attn_done = s.sem("pairs_done"), s.sem("kept_done"), s.sem("attn_done")
        kd_turned, kdT_ready, o_done, o_kept = s.sem("kd_turned"), s.sem("kdT_ready"), s.sem("o_done"), s.sem("o_kept")
        st_done, S_ready = s.sem("st_done"), s.sem("S_ready")
        own_ready, new_done, new_scaled, new_ready, new_stored = (s.sem("own_ready"), s.sem("new_done"), s.sem("new_scaled"),
                                                                  s.sem("new_ready"), s.sem("new_stored"))
        S_stored, rec_stored = s.sem("S_stored"), two("rec_stored")
        squared, summed, var_ready, logged, rooted, multiplied, factor_ready, root_ready, normed, rec_ready = (
            s.sem("squared"), s.sem("summed"), s.sem("var_ready"), s.sem("logged"), s.sem("rooted"), s.sem("multiplied"),
            s.sem("factor_ready"), s.sem("root_ready"), s.sem("normed"), s.sem("rec_ready"))
        block = s.block()
        UNITS = 2 * HG
        CHUNKS_OF = (range(0, TILES // 2), range(TILES // 2, TT))
        COLS = (slice(0, SEQ // 2), slice(SEQ // 2, T))
        WIDTH = (SEQ // 2, T - SEQ // 2)

        def wait(engine, sem, value):
            if not isinstance(value, int) or value > 0:
                engine.wait_ge(sem, value)

        def chunks_through(h, u):
            return TT * h + CHUNKS_OF[u][-1] + 1

        def heads(engine, unit):
            def both(h, first=False, last=False):
                unit(h, 0, (h, 1), None if first else (h - 1, 1))
                unit(h, 1, None if last else (h + 1, 0), (h, 0))

            both(0, first=True)
            with engine.Fori(1, HG - 1) as h:
                both(h)
            both(HG - 1, last=True)

        def tile(n):
            return slice(n * P, (n + 1) * P) if n < TILES else slice(SEQ, T)

        @block.sync
        def _(sp):
            sp.dma_start(lb_in[:, :, :], bound).then_inc(consts, 16)

            def feat(b, h, u, dst, sem):
                sp.dma_start(dst[:, COLS[u]], feat_d[DynSlice(b + h, 1)][:, :, COLS[u]].rearrange("a p t -> (a p) t")
                             ).then_inc(sem[u], 16)

            def load_f(h, u):
                wait(sp, G_ready, 2 * h + u - 1)
                feat(8, h, u, f, f_loaded)

            def load(h, u):
                wait(sp, pairs_done, chunks_through(h - 1, u))
                feat(12, h, u, kL[:, NL - 1, :], k_loaded)
                feat(0, h, u, qL[:, NL - 1, :], q_loaded)
                wait(sp, o_done, chunks_through(h - 1, u))
                lo = u * TILES // 2
                sp.dma_start(hv[:, lo:lo + TILES // 2, :],
                             hv_d[lo * P:lo * P + SEQ // 2, DynSlice(P * h, P)].rearrange("(n p) v -> p n v", p=P)
                             ).then_inc(hv_loaded[u], 16)
                if u == 1:
                    sp.dma_start(hv[0:NS, TILES, :], hv_d[SEQ:T, DynSlice(P * h, P)]).then_inc(hv_loaded[u], 16)

            def load_gate(h, u):
                wait(sp, rec_ready, 2 * h + u - 1)
                feat(4, h, u, gate, gate_loaded)

            def load_state(h):
                wait(sp, o_done, TT * h)
                sp.dma_start(st[:, :, :], state_in[DynSlice(h, 1)].rearrange("a k b v -> (a k) b v")).then_inc(st_loaded, 16)

            def store(h, u, waited=False):
                if not waited:
                    sp.wait_ge(rec_ready, 2 * h + u + 1)
                sp.dma_start(mixed_d[DynSlice(h + 4, 1)][:, :, COLS[u]].rearrange("a p t -> (a p) t"), rec[:, COLS[u]]
                             ).then_inc(rec_stored[u], 16)

            load_f(0, 0)
            sp.dma_start(reset[:, :], resets).then_inc(consts, 16)
            load(0, 0)
            load_f(0, 1)
            sp.dma_start(masks[:, :, :], level_masks).then_inc(consts, 16)
            sp.dma_start(gain[:, :], hg_gain).then_inc(consts, 16)
            sp.dma_start(own[:, :], owner).then_inc(consts, 16)
            load_state(0)
            load_gate(0, 0)

            def unit(h, u, after, before):
                if after:
                    load(*after)
                if after:
                    load_gate(*after)
                if before:
                    store(*before, waited=after is not None)
                if not isinstance(h, int) or h + 1 < HG:
                    load_f(h + 1, u)
                if u == 1:
                    sp.wait_ge(S_ready, TILES * h + TILES)
                    sp.dma_start(state_prompt[DynSlice(h, 1)].rearrange("a k v -> (a k) v"), S[:, 1, :]
                                 ).then_inc(S_stored, 16)
                    sp.wait_ge(new_ready, h + 1)
                    sp.dma_start(state_sample[DynSlice(h, 1)].rearrange("a k b v -> (a k) b v"), new_st[:, :, :]
                                 ).then_inc(new_stored, 16)
                    if after:
                        load_state(h + 1)

            heads(sp, unit)
            store(HG - 1, 1)
            for u in range(2):
                sp.wait_ge(rec_stored[u], 16 * HG)
            sp.wait_ge(S_stored, 16 * HG)
            sp.wait_ge(new_stored, 16 * HG)

        @block.gpsimd
        def _(pool):
            def key_pass(h, u, n):
                U = 2 * h + u
                if n == 0:
                    pool.wait_ge(k_ready, U + 1)
                    wait(pool, kd_turned, chunks_through(h - 1, u))
                pool.wait_ge(decay_ready, NL * U + n + 1)
                w = WIDTH[u] if n == 0 or LEVELS[n - 1] <= 2 else SEQ // 2
                cols = slice(COLS[u].start, COLS[u].start + w)
                dst = kd[:, cols] if n == 0 else kL[:, n - 1, cols]
                nc.gpsimd.tensor_tensor(dst, kL[:, NL - 1, cols], decay[:, n, 0:w], ALU.mult).then_inc(kL_ready, 1)

            def newton(h, u):
                V, w = 2 * h + u, WIDTH[u]
                pool.wait_ge(rooted, V + 1)
                nc.gpsimd.tensor_tensor(tmp[:, 0:w], root[:, 0:w], root[:, 0:w], ALU.mult).then_inc(multiplied, 1)
                pool.wait_ge(multiplied, 2 * V + 1)
                nc.gpsimd.tensor_tensor(tmp[:, 0:w], tmp[:, 0:w], var[:, 0:w], ALU.mult).then_inc(multiplied, 1)

            def refine(h, u):
                V, w = 2 * h + u, WIDTH[u]
                pool.wait_ge(factor_ready, V + 1)
                nc.gpsimd.tensor_tensor(root[:, 0:w], root[:, 0:w], tmp[:, 0:w], ALU.mult).then_inc(root_ready, 1)

            def gated(h, u):
                V = 2 * h + u
                pool.wait_ge(normed, V + 1)
                pool.wait_ge(gate_loaded[u], 16 * h + 16)
                nc.gpsimd.tensor_tensor(rec[:, COLS[u]], rec[:, COLS[u]], gate[:, COLS[u]], ALU.mult).then_inc(rec_ready, 1)

            def unit(h, u, after, before):
                for n in range(NL):
                    if after:
                        key_pass(*after, n)
                    if before and n == 1:
                        newton(*before)
                    if before and n == 4:
                        refine(*before)
                if before:
                    gated(*before)

            for n in range(NL):
                key_pass(0, 0, n)
            heads(pool, unit)
            newton(HG - 1, 1)
            refine(HG - 1, 1)
            gated(HG - 1, 1)

        @block.scalar
        def _(act):
            act.wait_ge(bound_step, 3)
            for n in range(2):
                nc.scalar.activation(lexp[:, n, :], lb_in[:, n, :], ACT.Exp).then_inc(bound_exp, 1)

            def logs(h, u):
                U = 2 * h + u
                act.wait_ge(k_loaded[u], 16 * h + 16)
                nc.scalar.activation(kL[:, NL - 1, COLS[u]], kL[:, NL - 1, COLS[u]], ACT.Copy,
                                     scale=omlb[:, DynSlice(h, 1)]).then_inc(k_ready, 1)
                act.wait_ge(f_ready, U + 1)
                nc.scalar.activation(f[:, COLS[u]], f[:, COLS[u]], ACT.Ln).then_inc(log_ready, 1)

            def total_decay(h, u):
                U = 2 * h + u
                act.wait_ge(G_ready, U + 1)
                wait(act, S_ready, TILES * (h - 1) + TILES // 2 * (u + 1))
                wait(act, q_in_ready, U - 1)
                if u == 1:
                    wait(act, new_scaled, h)
                nc.scalar.activation(eG[:, COLS[u]], G[:, COLS[u]], ACT.Exp).then_inc(eG_ready, 1)

            def decays(h, u, passes):
                U = 2 * h + u
                for n in passes:
                    act.wait_ge(dist_ready, NL * U + n + 1)
                    if n == 0:
                        e = decay[:, 0, 0:WIDTH[u]]
                        nc.scalar.activation(e, e, ACT.Exp, scale=-1.0).then_inc(decay_ready, 1)
                    else:
                        b = LEVELS[n - 1]
                        w = WIDTH[u] if b <= 2 else SEQ // 2
                        e = decay[:, n, 0:w].rearrange("p (n b) -> p n b", b=2 * b)
                        nc.scalar.activation(e[:, :, b:2 * b], e[:, :, b:2 * b], ACT.Exp)
                        nc.scalar.activation(e[:, :, 0:b], e[:, :, 0:b], ACT.Exp, scale=-1.0).then_inc(decay_ready, 1)

            def square(h, u):
                V, w = 2 * h + u, WIDTH[u]
                act.wait_ge(o_kept, chunks_through(h, u))
                wait(act, root_ready, V)
                nc.scalar.activation(sq[:, 0:w], oT[:, COLS[u]], ACT.Square).then_inc(squared, 1)

            def inverse_root(h, u):
                V, w = 2 * h + u, WIDTH[u]
                act.wait_ge(var_ready, V + 1)
                wait(act, normed, V)
                nc.scalar.activation(root[:, 0:w], var[:, 0:w], ACT.Ln).then_inc(logged, 1)
                act.wait_ge(logged, V + 1)
                nc.scalar.activation(root[:, 0:w], root[:, 0:w], ACT.Exp, scale=-0.5).then_inc(rooted, 1)

            def keep_kd(h, n):
                w = P if n < TILES else NS
                act.wait_ge(kd_turned, TT * h + n + 1)
                if n >= 2:
                    act.wait_ge(st_done, TILES * h + n - 1)
                else:
                    wait(act, st_done, TILES * h)
                    wait(act, new_done, h)
                nc.scalar.activation(kdT[0:w, n % 2, :], kd_ps[0:w, 0:P], ACT.Copy).then_inc(kdT_ready, 1)

            def keep_o(h, n):
                w = P if n < TILES else NS
                act.wait_ge(o_done, TT * h + n + 1)
                nc.scalar.activation(oT[:, tile(n)], o_ps[:, n % 2, 0:w], ACT.Copy).then_inc(o_kept, 1)

            def unit(h, u, after, before):
                if before:
                    square(*before)
                keep_kd(h, CHUNKS_OF[u][0])
                for j, n in enumerate(CHUNKS_OF[u]):
                    if n != CHUNKS_OF[u][-1]:
                        keep_kd(h, n + 1)
                    if j == 0:
                        wait(act, normed, 2 * h + u - 1)
                    keep_o(h, n)
                    if after and j == 0:
                        logs(*after)
                    if after and j == 1:
                        decays(*after, (0,))
                        total_decay(*after)
                    if before and j == 1:
                        inverse_root(*before)
                    if after and 1 <= j <= 3:
                        decays(*after, {1: (1, 2), 2: (3, 4, 5), 3: (6, 7)}[j])

            act.wait_ge(bound_ready, 2)
            logs(0, 0)
            decays(0, 0, (0,))
            total_decay(0, 0)
            decays(0, 0, range(1, NL))
            heads(act, unit)
            square(HG - 1, 1)
            inverse_root(HG - 1, 1)

        @block.vector
        def _(dve):
            dve.wait_ge(consts, 80)
            nc.vector.tensor_tensor(lmax[:, :], lb_in[:, 0, :], lb_in[:, 1, :], ALU.max).then_inc(bound_step, 1)
            dve.wait_ge(bound_step, 1)
            nc.vector.tensor_tensor(lb_in[:, 0, :], lb_in[:, 0, :], lmax[:, :], ALU.subtract).then_inc(bound_step, 1)
            nc.vector.tensor_tensor(lb_in[:, 1, :], lb_in[:, 1, :], lmax[:, :], ALU.subtract).then_inc(bound_step, 1)
            dve.wait_ge(bound_exp, 2)
            nc.vector.tensor_tensor(lsum[:, :], lexp[:, 0, :], lexp[:, 1, :], ALU.add).then_inc(bound_step, 1)
            dve.wait_ge(bound_step, 4)
            nc.vector.reciprocal(lmax[:, :], lsum[:, :]).then_inc(bound_step, 1)
            dve.wait_ge(bound_step, 5)
            nc.vector.tensor_tensor(lb[:, :], lexp[:, 0, :], lmax[:, :], ALU.mult).then_inc(bound_ready, 1)
            dve.wait_ge(bound_ready, 1)
            nc.vector.tensor_scalar(omlb[:, :], lb[:, :], -1.0, 1.0, ALU.mult, ALU.add).then_inc(bound_ready, 1)
            dve.wait_ge(bound_ready, 2)

            def forget(h, u):
                dve.wait_ge(f_loaded[u], 16 * h + 16)
                nc.vector.tensor_scalar(f[:, COLS[u]], f[:, COLS[u]], omlb[:, DynSlice(h, 1)], lb[:, DynSlice(h, 1)],
                                        ALU.mult, ALU.add).then_inc(f_ready, 1)

            def scan(h, u):
                U = 2 * h + u
                dve.wait_ge(log_ready, U + 1)
                wait(dve, eG_ready, U - 1)
                wait(dve, decay_ready, NL * (U - 1))
                nc.vector.tensor_tensor_scan(G[:, COLS[u]], reset[:, COLS[u]], f[:, COLS[u]], 0.0, ALU.mult, ALU.add
                                             ).then_inc(G_ready, 1)
                dve.wait_ge(q_loaded[u], 16 * h + 16)
                q = qL[:, NL - 1, COLS[u]]
                nc.vector.tensor_scalar(q, q, float(P) ** -0.5, None, ALU.mult).then_inc(q_ready, 1)
                dve.wait_ge(G_ready, U + 1)

            def distances(h, u, passes):
                U = 2 * h + u
                lo = COLS[u].start
                for n in passes:
                    wait(dve, kL_ready, NL * (U - 1) + n + 1)
                    if n:
                        wait(dve, qL_ready, (NL - 1) * (U - 1) + n)
                    if n == 0:
                        parts = [(lo, lo + SEQ // 2, P, P - 1)]
                        if u == 1:
                            parts.append((SEQ, T, DT, DT - 1))
                    else:
                        b = LEVELS[n - 1]
                        parts = [(lo, COLS[u].stop if b <= 2 else lo + SEQ // 2, 2 * b, b - 1)]
                    for a, z, b, at in parts:
                        g = G[:, a:z].rearrange("p (n b) -> p n b", b=b)
                        d = decay[:, n, a - lo:z - lo].rearrange("p (n b) -> p n b", b=b)
                        last = nc.vector.tensor_tensor(d, g, g[:, :, at:at + 1].broadcast_to([P, (z - a) // b, b]),
                                                       ALU.subtract)
                    last.then_inc(dist_ready, 1)

            def carried_queries(h, u):
                U = 2 * h + u
                dve.wait_ge(eG_ready, U + 1)
                dve.wait_ge(q_ready, U + 1)
                wait(dve, o_done, chunks_through(h - 1, u))
                nc.vector.tensor_tensor(q_in[:, COLS[u]], qL[:, NL - 1, COLS[u]], eG[:, COLS[u]], ALU.mult
                                        ).then_inc(q_in_ready, 1)

            def queries(h, u, passes):
                U = 2 * h + u
                for n in passes:
                    w = WIDTH[u] if LEVELS[n - 1] <= 2 else SEQ // 2
                    cols = slice(COLS[u].start, COLS[u].start + w)
                    dve.wait_ge(decay_ready, NL * U + n + 1)
                    nc.vector.tensor_tensor(qL[:, n - 1, cols], qL[:, NL - 1, cols], decay[:, n, 0:w], ALU.mult
                                            ).then_inc(qL_ready, 1)

            def chunk(h, n):
                w = P if n < TILES else NS
                lv = 0 if n < TILES else NL - 3
                dve.wait_ge(pairs_done, TT * h + n + 1)
                wait(dve, attn_done, TT * h + n)
                nc.vector.tensor_tensor(kept[0:w, lv:NL, 0:w], pairs[0:w, lv:NL, 0:w], masks[0:w, lv:NL, 0:w], ALU.mult
                                        ).then_inc(kept_done, 1)
                dve.wait_ge(kept_done, TT * h + n + 1)
                wait(dve, o_done, TT * h + max(n - 1, 0))
                nc.vector.tensor_reduce(attn[0:w, n % 2, 0:w], kept[0:w, lv:NL, 0:w].rearrange("p l t -> p t l"), AX.X,
                                        ALU.add).then_inc(attn_done, 1)
                if n < TILES:
                    dve.wait_ge(st_done, TILES * h + n + 1)
                    wait(dve, S_ready, TILES * h + n)
                    wait(dve, o_done, TT * h + n)
                    if n == 1:
                        wait(dve, S_stored, 16 * h)
                    if n:
                        nc.vector.scalar_tensor_tensor(S[:, n % 2, :], S[:, (n + 1) % 2, :], eG[:, n * P + P - 1:n * P + P],
                                                       st_ps[:, 0:P], ALU.mult, ALU.add).then_inc(S_ready, 1)
                    else:
                        nc.vector.tensor_copy(S[:, 0, :], st_ps[:, 0:P]).then_inc(S_ready, 1)

            def own_values(h):
                dve.wait_ge(hv_loaded[1], 32 * h + 32)
                wait(dve, new_done, h)
                nc.vector.tensor_tensor(own_v[:, :, :], hv[0:NS, TILES:TT, :].broadcast_to([NS, DB, P]),
                                        own[:, :].unsqueeze(2).broadcast_to([NS, DB, P]), ALU.mult).then_inc(own_ready, 1)
                dve.wait_ge(st_loaded, 16 * h + 16)
                wait(dve, new_stored, 16 * h)
                wait(dve, new_ready, h)
                ends = eG[:, SEQ:T].rearrange("p (b j) -> p b j", j=DT)[:, :, DT - 1:DT]
                nc.vector.tensor_tensor(new_st[:, :, :], st[:, :, :], ends.broadcast_to([P, DB, P]), ALU.mult
                                        ).then_inc(new_scaled, 1)

            def new_states(h):
                dve.wait_ge(new_scaled, h + 1)
                dve.wait_ge(new_done, h + 1)
                nc.vector.tensor_tensor(new_st[:, :, :], new_st[:, :, :], pairs[:, :, :], ALU.add).then_inc(new_ready, 1)

            def variance(h, u):
                V, w = 2 * h + u, WIDTH[u]
                dve.wait_ge(summed, V + 1)
                wait(dve, multiplied, 2 * V)
                if u == 0:
                    v, total = var[:, 0:w], sum_ps[:, 0, 0:w]
                else:
                    v, total = var[:, 0:w].rearrange("p (c t) -> p c t", c=2), sum_ps[:, :, 0:w // 2]
                nc.vector.tensor_scalar(v, total, 1.0 / P, EPS, ALU.mult, ALU.add).then_inc(var_ready, 1)

            def factor(h, u):
                V, w = 2 * h + u, WIDTH[u]
                dve.wait_ge(multiplied, 2 * V + 2)
                nc.vector.tensor_scalar(tmp[:, 0:w], tmp[:, 0:w], -0.5, 1.5, ALU.mult, ALU.add).then_inc(factor_ready, 1)

            def norm(h, u):
                V, w = 2 * h + u, WIDTH[u]
                dve.wait_ge(root_ready, V + 1)
                wait(dve, rec_stored[u], 16 * h)
                nc.vector.scalar_tensor_tensor(rec[:, COLS[u]], oT[:, COLS[u]], gain[:, 0:1], root[:, 0:w], ALU.mult,
                                               ALU.mult).then_inc(normed, 1)

            def unit(h, u, after, before):
                for j, n in enumerate(CHUNKS_OF[u]):
                    chunk(h, n)
                    if before and j == 1:
                        variance(*before)
                    if after and j == 0:
                        forget(*after)
                    if after and j == 1:
                        scan(*after)
                        distances(*after, (0, 1, 2))
                    if after and j == 2:
                        distances(*after, (3, 4, 5))
                        carried_queries(*after)
                        queries(*after, (1, 2))
                    if before and j == 2:
                        factor(*before)
                    if after and j == 3:
                        distances(*after, (6, 7))
                        queries(*after, range(3, NL))
                    if before and j == 3:
                        norm(*before)
                    if u == 1 and j == 1:
                        own_values(h)
                if u == 1:
                    new_states(h)

            forget(0, 0)
            scan(0, 0)
            distances(0, 0, range(NL))
            carried_queries(0, 0)
            queries(0, 0, range(1, NL))
            heads(dve, unit)
            variance(HG - 1, 1)
            factor(HG - 1, 1)
            norm(HG - 1, 1)

        @block.tensor
        def _(pe):
            def pair_products(h, n):
                w = P if n < TILES else NS
                lv = 0 if n < TILES else NL - 3
                wait(pe, kept_done, TT * h + n)
                if n == 0:
                    wait(pe, new_ready, h)
                for x in range(lv, NL):
                    last = nc.tensor.matmul(pairs[0:w, x, 0:w], kL[:, x, tile(n)], qL[:, x, tile(n)], start=True,
                                            stop=True)
                last.then_inc(pairs_done, 1)

            def turn(h, n):
                w = P if n < TILES else NS
                wait(pe, kdT_ready, TT * h + n)
                nc.tensor.transpose(kd_ps[0:w, 0:P], kd[:, tile(n)], ident[:, :]).then_inc(kd_turned, 1)

            def states(h, n):
                pe.wait_ge(kdT_ready, TT * h + n + 1)
                if n < TILES:
                    wait(pe, S_ready, TILES * h + n)
                    nc.tensor.matmul(st_ps[:, 0:P], kdT[:, n % 2, :], hv[:, n, :], start=True, stop=True
                                     ).then_inc(st_done, 1)
                else:
                    pe.wait_ge(kept_done, TT * h + TT)
                    pe.wait_ge(own_ready, h + 1)
                    for x in range(2):
                        last = nc.tensor.matmul(pairs[:, 4 * x:4 * x + 4, :].rearrange("p a b -> p (a b)"),
                                                kdT[0:NS, n % 2, :],
                                                own_v[:, 4 * x:4 * x + 4, :].rearrange("p a b -> p (a b)"),
                                                start=True, stop=True)
                    last.then_inc(new_done, 1)

            def outputs(h, n):
                w = P if n < TILES else NS
                pe.wait_ge(attn_done, TT * h + n + 1)
                wait(pe, o_kept, TT * h + max(n - 1, 0))
                o = o_ps[:, n % 2, :]
                last = nc.tensor.matmul(o[:, 0:w], hv[0:w, n, :], attn[0:w, n % 2, 0:w], start=True, stop=(n == 0))
                if 0 < n < TILES:
                    pe.wait_ge(S_ready, TILES * h + n)
                    last = nc.tensor.matmul(o[:, 0:w], S[:, (n + 1) % 2, :], q_in[:, tile(n)], start=False, stop=True)
                if n == TILES:
                    pe.wait_ge(st_loaded, 16 * h + 16)
                    for b in range(DB):
                        last = nc.tensor.matmul(o[:, DT * b:DT * (b + 1)], st[:, b, :],
                                                q_in[:, SEQ + DT * b:SEQ + DT * (b + 1)], start=False, stop=(b == DB - 1))
                last.then_inc(o_done, 1)

            def sums(h, u):
                V, w = 2 * h + u, WIDTH[u]
                pe.wait_ge(squared, V + 1)
                wait(pe, var_ready, V)
                for x in range(u + 1):
                    c = w // (u + 1)
                    last = nc.tensor.matmul(sum_ps[:, x, 0:c], ones[:, :], sq[:, x * c:(x + 1) * c], start=True, stop=True)
                last.then_inc(summed, 1)

            def unit(h, u, after, before):
                U = 2 * h + u
                pe.wait_ge(qL_ready, (NL - 1) * (U + 1))
                pe.wait_ge(kL_ready, NL * (U + 1))
                pe.wait_ge(q_in_ready, U + 1)
                pe.wait_ge(hv_loaded[u], 16 * (u + 1) * (h + 1))
                first, end = CHUNKS_OF[u][0], CHUNKS_OF[u][-1]
                pair_products(h, first)
                turn(h, first)
                states(h, first)
                for n in CHUNKS_OF[u]:
                    if n < end:
                        pair_products(h, n + 1)
                        turn(h, n + 1)
                    outputs(h, n)
                    if n < end:
                        states(h, n + 1)
                    if before and n == first:
                        sums(*before)

            heads(pe, unit)
            sums(HG - 1, 1)



def merge(nc, xT, mixed_d, feat_d, w_attn, w_hgrn, w_out):
    with Scope(nc, "merge") as s:
        bhi = s.sb("bhi", [P, 8, T], F32R)
        blo = s.sb("blo", [P, 8, T], F32R)
        mhi = s.sb("mhi", [P, KD, T], F32R)
        mlo = s.sb("mlo", [P, KD, T], F32R)
        raw = s.sb("raw", [P, 2, UNIT])
        whi = s.sb("whi", [P, 2, UNIT], F32R)
        wlo = s.sb("wlo", [P, 2, UNIT], F32R)
        branch = s.sb("branch", [P, 2, CH])
        gates = s.sb("gates", [P, 2, 2, CH])
        both = s.sb("both", [P, 2, CH])
        ps = s.ps("ps", [P, 2, 2, 512])
        out_ps = s.ps("out_ps", [P, 4, 512])
        w_loaded = [s.sem(f"w_loaded{n}") for n in range(2)]
        branch_in = [s.sem(f"branch_in{n}") for n in range(2)]
        gates_in = [s.sem(f"gates_in{n}") for n in range(2)]
        b_hi_done, b_lo_done = s.sem("b_hi_done"), s.sem("b_lo_done")
        w_hi_done, w_lo_done = s.sem("w_hi_done"), s.sem("w_lo_done")
        mult_done = s.sem("mult_done")
        ps_done, gated, summed, m_hi_done, m_lo_done = (s.sem("ps_done"), s.sem("gated"), s.sem("summed"),
                                                        s.sem("m_hi_done"), s.sem("m_lo_done"))
        out_done, out_added = s.sem("out_done"), s.sem("out_added")
        block = s.block()
        parts = [(b, c) for c in range(NCH) for b in range(8)]
        wa = w_attn.rearrange("(G g r d) n -> g d G r n", G=2, g=2, r=2)
        wr = w_hgrn.rearrange("(k p) n -> p k n", p=P)
        wo = w_out.rearrange("(k p) n -> p k n", p=P)

        def pairs(engine, body):
            body(0, 0, 0, True)
            with engine.Fori(1, 4) as i:
                body(0, i, i, False)
            with engine.Fori(0, 4) as i:
                body(1, i, i + 4, False)

        @block.sync
        def _(sp):
            for n, (b, c) in enumerate(parts):
                if n >= 2:
                    sp.wait_ge(b_lo_done, n - 1)
                sp.dma_start(branch[:, n % 2, :], mixed_d[b][:, c * CH:(c + 1) * CH]).then_inc(branch_in[n % 2], 16)

            def body(kind, i, pair, first):
                for u in range(2):
                    if kind == 0:
                        for c in range(NCH):
                            y = 3 * u + c
                            if not (first and y < 2):
                                sp.wait_ge(gated, 12 * pair + 2 * y - 2)
                            for m in range(2):
                                sp.dma_start(gates[:, y % 2, m, :],
                                             feat_d[DynSlice(16 + 8 * m + 2 * i + u, 1)][:, :, c * CH:(c + 1) * CH
                                                                                         ].rearrange("a p t -> (a p) t")
                                             ).then_inc(gates_in[y % 2], 16)

            body(0, 0, 0, True)
            with sp.Fori(1, 4) as i:
                body(0, i, i, False)

        @block.gpsimd
        def _(pool):
            def body(kind, i, pair, first):
                for u in range(2):
                    if not first:
                        pool.wait_ge(w_lo_done, 2 * pair + u - 1)
                    col = (2 * i + u) * P
                    if kind == 0:
                        halves = raw[:, u, :].rearrange("p (m k f) -> p m k f", m=2, k=4)
                        for g in range(2):
                            for G in range(2):
                                pool.dma_start(halves[g * HD:(g + 1) * HD, 0, 2 * G:2 * G + 2, :],
                                               wa[g][:, G, :, DynSlice(col, P)]).then_inc(w_loaded[u], 16)
                        pool.dma_start(halves[:, 1, :, :], wr[:, :, DynSlice(col, P)]).then_inc(w_loaded[u], 16)
                    else:
                        pool.dma_start(raw[:, u, :].rearrange("p (k f) -> p k f", k=KD), wo[:, :, DynSlice(col, P)]
                                       ).then_inc(w_loaded[u], 16)

            pairs(pool, body)

        @block.scalar
        def _(act):
            def hi(u):
                nc.scalar.activation(whi[:, u, :], raw[:, u, :], ACT.Copy).then_inc(w_hi_done, 1)

            for n, (b, c) in enumerate(parts):
                act.wait_ge(branch_in[n % 2], 16 * (n // 2) + 16)
                nc.scalar.activation(bhi[:, b, c * CH:(c + 1) * CH], branch[:, n % 2, :], ACT.Copy).then_inc(b_hi_done, 1)
                if n == 3:
                    for u in range(2):
                        act.wait_ge(w_loaded[u], 80)
                        hi(u)
            with act.Fori(1, 4) as i:
                for u in range(2):
                    act.wait_ge(w_loaded[u], 80 * i + 80)
                    act.wait_ge(ps_done, 6 * i + 3 * u - 3)
                    hi(u)
            for u in range(2):
                act.wait_ge(w_loaded[u], 16 + 320)
                act.wait_ge(ps_done, 24 - 3 * (1 - u))
                hi(u)
            with act.Fori(1, 4) as i:
                for u in range(2):
                    act.wait_ge(w_loaded[u], 16 * i + 16 + 320)
                    act.wait_ge(out_done, 6 * i + 3 * u - 3)
                    hi(u)

        @block.vector
        def _(dve):
            def lo(u, pair):
                dve.wait_ge(w_hi_done, 2 * pair + u + 1)
                nc.vector.tensor_tensor(wlo[:, u, :], raw[:, u, :], whi[:, u, :], ALU.subtract).then_inc(w_lo_done, 1)

            def gate(i, u, c, first):
                y = 3 * u + c
                e = 6 * i + y
                dve.wait_ge(ps_done, e + 1)
                dve.wait_ge(gates_in[y % 2], 32 * (3 * i + y // 2) + 32)
                for m in range(2):
                    g = gates[:, y % 2, m, :]
                    nc.vector.tensor_tensor(g, g, ps[:, y % 2, m, 0:CH], ALU.mult).then_inc(mult_done, 1)
                dve.wait_ge(mult_done, 2 * e + 2)
                nc.vector.tensor_tensor(both[:, y % 2, :], gates[:, y % 2, 0, :], gates[:, y % 2, 1, :], ALU.add
                                        ).then_inc(gated, 2)
                dve.wait_ge(gated, 2 * e + 2)
                hi = mhi[:, DynSlice(2 * i + u, 1), c * CH:(c + 1) * CH].rearrange("p a t -> p (a t)")
                lo_ = mlo[:, DynSlice(2 * i + u, 1), c * CH:(c + 1) * CH].rearrange("p a t -> p (a t)")
                nc.vector.tensor_copy(hi, both[:, y % 2, :]).then_inc(m_hi_done, 1)
                dve.wait_ge(m_hi_done, e + 1)
                nc.vector.tensor_tensor(lo_, both[:, y % 2, :], hi, ALU.subtract).then_inc(m_lo_done, 1)

            def add(i, u, c):
                y = 3 * u + c
                dve.wait_ge(out_done, 6 * i + y + 1)
                x = xT[:, DynSlice(2 * i + u, 1), c * CH:(c + 1) * CH].rearrange("p a t -> p (a t)")
                nc.vector.tensor_tensor(x, x, out_ps[:, y % 3, 0:CH], ALU.add).then_inc(out_added, 1)

            for n, (b, c) in enumerate(parts):
                cols = slice(c * CH, (c + 1) * CH)
                dve.wait_ge(b_hi_done, n + 1)
                nc.vector.tensor_tensor(blo[:, b, cols], branch[:, n % 2, :], bhi[:, b, cols], ALU.subtract
                                        ).then_inc(b_lo_done, 1)
                if n == 4:
                    lo(0, 0)
                    lo(1, 0)

            def gates_of(i, u, first=False):
                for c in range(NCH):
                    gate(i, u, c, first)

            with dve.Fori(0, 3) as i:
                for u in range(2):
                    gates_of(i, u)
                    lo(u, i + 1)
            gates_of(3, 0)
            lo(0, 4)
            gates_of(3, 1)
            lo(1, 4)
            with dve.Fori(0, 3) as i:
                for u in range(2):
                    for c in range(NCH):
                        add(i, u, c)
                    lo(u, i + 5)
            for u in range(2):
                for c in range(NCH):
                    add(3, u, c)

        @block.tensor
        def _(pe):
            def body(kind, i, pair, first):
                for u in range(2):
                    pe.wait_ge(w_lo_done, 2 * pair + u + 1)
                    for c in range(NCH):
                        y = 3 * u + c
                        cols = slice(c * CH, (c + 1) * CH)
                        if kind == 0:
                            if first and u == 0:
                                pe.wait_ge(b_lo_done, 8 * c + 8)
                            if not (first and y < 2):
                                pe.wait_ge(gated, 12 * i + 2 * y - 2)
                            for m in range(2):
                                for k in range(4):
                                    w = slice((4 * m + k) * P, (4 * m + k + 1) * P)
                                    last = split_product(nc, ps[:, y % 2, m, 0:CH], whi[:, u, w], wlo[:, u, w],
                                                         bhi[:, 4 * m + k, cols], blo[:, 4 * m + k, cols], k == 0, k == 3)
                            last.then_inc(ps_done, 1)
                        else:
                            if first or (u == 0):
                                pe.wait_ge(m_lo_done, 18 + c + 4)
                            if not (first and y < 3):
                                pe.wait_ge(out_added, 6 * i + y - 2)
                            for k in range(KD):
                                w = slice(k * P, (k + 1) * P)
                                last = split_product(nc, out_ps[:, y % 3, 0:CH], whi[:, u, w], wlo[:, u, w],
                                                     mhi[:, k, cols], mlo[:, k, cols], k == 0, k == KD - 1)
                            last.then_inc(out_done, 1)

            body(0, 0, 0, True)
            with pe.Fori(1, 4) as i:
                body(0, i, i, False)
            body(1, 0, 4, True)
            with pe.Fori(1, 4) as i:
                body(1, i, i + 4, False)

OUTS = [("y_prompt", (1, SEQ, D)), ("y_sample", (DB, DT, D)), ("k_prompt", (1, 1, SEQ, KV, HD)), ("v_prompt", (1, 1, SEQ, KV, HD)),
        ("idx_k_prompt", (1, 1, SEQ, HD)), ("hgrn_prompt", (1, 1, HG, P, P)), ("k_sample", (1, DB, DT, KV, HD)),
        ("v_sample", (1, DB, DT, KV, HD)), ("idx_k_sample", (1, DB, DT, HD)), ("hgrn_sample", (1, DB, HG, P, P))]


def build(nc, a, o):
    scratch = {name: nc.dram_tensor(f"scratch_{name}", shape, F32).ap()
               for name, shape in (("qT", (4, P, T)), ("kT", (2, P, T)), ("qiT", (4, P, T)), ("kiT", (1, P, T)),
                                   ("wi", (T, HEADS)), ("hv", (T, HG * P)), ("feat", (FEATS, P, T)), ("mixed", (8, P, T)))}
    rows = {n: o[n].rearrange("a b t h d -> (a b t) (h d)") for n in ("k_prompt", "v_prompt", "k_sample", "v_sample")}
    rows |= {n: o[n].rearrange("a b t d -> (a b t) d") for n in ("idx_k_prompt", "idx_k_sample")}
    cache_k, cache_v = (a[n][0].rearrange("n s h d -> n s (h d)") for n in ("cache_k", "cache_v"))
    with Scope(nc, "core") as s:
        xT = s.sb("xT", [P, KD, T])
        ident = s.sb("ident", [P, P])
        ones = s.sb("ones", [P, P])
        ident_in, ones_set = s.sem("ident_in"), s.sem("ones_set")
        with nc.Block() as block:
            @block.sync
            def _(sp):
                sp.dma_start(ident[:, :], a["t_ident"]).then_inc(ident_in, 16)
                sp.wait_ge(ident_in, 16)

            @block.vector
            def _(dve):
                nc.vector.memset(ones[:, :], 1.0).then_inc(ones_set, 1)

        load_and_turn(nc, a["x_prompt"], a["x_sample"], xT, ident)

        def feed_forward(n):
            with Scope(nc, f"half{n}") as half:
                hhi = half.sb("hhi", [P, KD, T], F32R)
                hlo = half.sb("hlo", [P, KD, T], F32R)
                normalise(nc, f"norm{n}", xT, a[f"ffn{n}_norm"], hhi, hlo, ones)
                swiglu(nc, f"ff{n}", xT, hhi, hlo, a[f"ffn{n}_w_gate"], a[f"ffn{n}_w_up"], a[f"ffn{n}_w_down"])

        feed_forward(1)
        with Scope(nc, "mix") as mix:
            masks = mix.sb("masks", [P, SLABS, SW], mybir.dt.bfloat16)
            with Scope(nc, "proj") as proj:
                hhi = proj.sb("hhi", [P, KD, T], F32R)
                hlo = proj.sb("hlo", [P, KD, T], F32R)
                normalise(nc, "normm", xT, a["mix_norm"], hhi, hlo, ones)
                token_projections(nc, hhi, hlo, a["w_in"], a["q_norm"], a["k_norm"], a["t_cos"], a["t_sin"], ident,
                                  scratch["qT"], scratch["kT"], scratch["qiT"], scratch["kiT"], scratch["wi"],
                                  scratch["hv"], rows["k_prompt"], rows["k_sample"], rows["v_prompt"], rows["v_sample"],
                                  rows["idx_k_prompt"], rows["idx_k_sample"])
                scores = proj.sb("scores", [P, SLABS, SW])
                index_scores(nc, scores, scratch["qiT"], scratch["kiT"], scratch["wi"], a["cache_idx_k"], a["page_table"],
                             a["t_same_token"], a["t_new_floor"], ident)
                select_keys_and_project(nc, scores, masks, hhi, hlo, a["w_in"], scratch["feat"])
            attention(nc, scratch["mixed"], masks, scratch["qT"], scratch["kT"], rows["v_prompt"], rows["v_sample"],
                      cache_k, cache_v, a["page_table"], a["t_causal"], a["t_own"], ident)
        recurrence(nc, scratch["mixed"], scratch["feat"], scratch["hv"], a["state_hgrn"][0].rearrange("b h k v -> h k b v"),
                   o["hgrn_prompt"].rearrange("a b h k v -> (a b h) k v"),
                   o["hgrn_sample"].rearrange("a b h k v -> h k (a b) v"), a["hg_lower_bound"], a["hg_norm"],
                   a["t_resets"], a["t_levels"], a["t_owner"], ident, ones)
        merge(nc, xT, scratch["mixed"], scratch["feat"], a["w_branch_attn"][0], a["w_branch_hgrn"][0], a["w_out"][0])
        feed_forward(2)
        turn_and_store(nc, xT, o["y_prompt"], o["y_sample"], ident)


GAINS = ('ffn1_norm', 'mix_norm', 'ffn2_norm')


def shape_tables():
    half = HD // 2
    inv = (10000.0 ** (-np.arange(half) * 2.0 / HD)).astype(np.float32)
    pos = np.concatenate([np.arange(SEQ), np.zeros(P - NS), SEQ + np.tile(np.arange(DT), DB)]).astype(np.float32)
    ang = pos[:, None] * inv[None, :]
    c, s = np.cos(ang), np.sin(ang)
    cos = np.concatenate([c, c], 1).reshape(TT, P, HD).transpose(1, 0, 2)
    sin = np.concatenate([-s, s], 1).reshape(TT, P, HD).transpose(1, 0, 2)
    row = np.arange(P)
    same = row[:, None] % NS == row[None, :] % NS
    causal = np.concatenate([np.zeros((P, P)), np.where(row[None, :] <= row[:, None], 0.0, MASKED)], 1)
    own = np.repeat(row[:, None, None] % NS // DT == np.arange(DB)[None, :, None], DT, 2)
    t = np.arange(T)
    start = np.where(t < SEQ, t % P == 0, (t - SEQ) % DT == 0)
    resets = np.broadcast_to(np.where(start, 0.0, 1.0)[None, :], (P, T))
    s_, t_ = row[:, None], row[None, :]
    levels = np.stack([(s_ // (2 * b) == t_ // (2 * b)) & (s_ % (2 * b) < b) & (t_ % (2 * b) >= b) for b in LEVELS]
                      + [s_ == t_], 1)
    return {"t_cos": cos, "t_sin": sin, "t_ident": np.eye(P),
            "t_causal": causal, "t_own": own,
            "t_resets": resets, "t_levels": levels, "t_owner": row[0:NS, None] // DT == np.arange(DB)[None, :],
            "t_same_token": same, "t_new_floor": np.where(np.arange(DT)[None] <= np.arange(P)[:, None] % DT, 0.0, FLOOR)}


def kernel(**inputs):
    import concourse.bacc as bacc
    from concourse.bass_utils import run_bass_kernel_spmd
    nc = bacc.Bacc("TRN2", target_bir_lowering=False, num_devices=1)
    arrays, a = {}, {}
    for name, v in inputs.items():
        v = np.ascontiguousarray(v)
        if name in GAINS:
            v = v.reshape(KD, P).T
        elif name == 'hg_lower_bound':
            v = v.reshape(2, HG, P).transpose(2, 0, 1)
        elif name == 'hg_norm':
            v = v.reshape(P, 1)
        v = np.ascontiguousarray(v)
        arrays[f"in_{name}"] = v
    for name, v in shape_tables().items():
        arrays[f"in_{name}"] = np.ascontiguousarray(v, dtype=np.float32)
    for name, v in arrays.items():
        a[name[3:]] = nc.dram_tensor(name, v.shape, mybir.dt.from_np(v.dtype), kind="ExternalInput").ap()
    o = {}
    for name, shape in OUTS:
        o[name] = nc.dram_tensor(f"out_{name}", shape, F32, kind="ExternalOutput").ap()
    build(nc, a, o)
    r = run_bass_kernel_spmd(nc, [arrays], core_ids=[0])
    return tuple(r.results[0][f"out_{name}"] for name, _ in OUTS)
```

```python
import math
from contextlib import ExitStack

import numpy as np

import concourse.bass as bass
from concourse import mybir
from concourse.bass import DynSlice

F32 = mybir.dt.float32
F32R = mybir.dt.float32r
I32 = mybir.dt.int32
ACT = mybir.ActivationFunctionType
ALU = mybir.AluOpType
AX = mybir.AxisListType

P = 128
D = 1024
KD = D // P
SEQ = 1024
TILES = SEQ // P
DB, DT = 8, 4
NS = DB * DT
T = SEQ + NS
CH = 352
NCH = T // CH
FF = 2816
NFF = FF // P
PAIRS = NFF // 2
EPS = 1e-6
RAW = 6
UNIT = 1024


class Scope:

    def __init__(self, nc, tag):
        self.nc, self.tag, self.stack, self.sems = nc, tag, ExitStack(), []
        self.blocks = ExitStack()

    def __enter__(self):
        self.stack.__enter__()
        return self

    def __exit__(self, *a):
        self.blocks.close()
        if self.sems and a[0] is None:
            with self.nc.Block() as block:
                @block.gpsimd
                def _(pool):
                    for sem in self.sems:
                        pool.sem_clear(sem)
        return self.stack.__exit__(*a)

    def sb(self, name, shape, dt=F32):
        return self.stack.enter_context(self.nc.sbuf_tensor(f"{self.tag}_{name}", shape, dt))

    def ps(self, name, shape, dt=F32):
        return self.stack.enter_context(self.nc.psum_tensor(f"{self.tag}_{name}", shape, dt))

    def sem(self, name):
        self.sems.append(self.stack.enter_context(self.nc.semaphore(f"{self.tag}_{name}")))
        return self.sems[-1]

    def block(self):
        return self.blocks.enter_context(self.nc.Block())


def load_and_turn(nc, x_prompt, x_sample, xT, ident):
    R = 4
    ROUNDS = TILES // R
    with Scope(nc, "turn") as s:
        rows = s.sb("rows", [P, R, D])
        turned = s.ps("turned", [P, 2 * R, 4, P])
        loaded = [s.sem(f"loaded{n}") for n in range(R)]
        half_turned = s.sem("half_turned")
        half_kept = s.sem("half_kept")
        xp = x_prompt[0].rearrange("(n p) d -> n p d", p=P)
        xs = x_sample.rearrange("b t d -> (b t) d")
        block = s.block()

        @block.sync
        def _(sp):
            def load(i, n):
                sp.dma_start(rows[:, n, :], xp[DynSlice(R * i + n, 1)].rearrange("a p d -> (a p) d")
                             ).then_inc(loaded[n], 16)

            for n in range(R):
                load(0, n)
            with sp.Fori(1, ROUNDS) as i:
                for n in range(R):
                    sp.wait_ge(half_turned, 2 * R * (i - 1) + 2 * n + 2)
                    load(i, n)
            sp.wait_ge(half_turned, 2 * R * (ROUNDS - 1) + 2)
            sp.dma_start(rows[0:NS, 0, :], xs).then_inc(loaded[0], 16)

        @block.tensor
        def _(pe):
            def turn_round(i, first):
                for n in range(R):
                    pe.wait_ge(loaded[n], 16 * i + 16)
                    for h in range(2):
                        if not first:
                            pe.wait_ge(half_kept, 2 * R * (i - 1) + 2 * n + h + 1)
                        for k in range(4):
                            m = nc.tensor.transpose(turned[:, 2 * n + h, k, :],
                                                    rows[:, n, (4 * h + k) * P:(4 * h + k + 1) * P], ident[:, :])
                        m.then_inc(half_turned, 1)

            turn_round(0, True)
            with pe.Fori(1, ROUNDS) as i:
                turn_round(i, False)
            pe.wait_ge(loaded[0], 16 * ROUNDS + 16)
            pe.wait_ge(half_kept, 2 * R * (ROUNDS - 1) + 2)
            for h in range(2):
                for k in range(4):
                    m = nc.tensor.transpose(turned[:, h, k, 0:NS],
                                            rows[0:NS, 0, (4 * h + k) * P:(4 * h + k + 1) * P], ident[0:NS, 0:NS])
                m.then_inc(half_turned, 1)

        @block.vector
        def _(dve):
            with dve.Fori(0, ROUNDS) as i:
                for n in range(R):
                    for h in range(2):
                        dve.wait_ge(half_turned, 2 * R * i + 2 * n + h + 1)
                        nc.vector.tensor_copy(xT[:, 4 * h:4 * h + 4, DynSlice(R * P * i + P * n, P)],
                                              turned[:, 2 * n + h, :, :]).then_inc(half_kept, 1)
            for h in range(2):
                dve.wait_ge(half_turned, 2 * TILES + h + 1)
                nc.vector.tensor_copy(xT[:, 4 * h:4 * h + 4, SEQ:T], turned[:, h, :, 0:NS]).then_inc(half_kept, 1)


def turn_and_store(nc, xT, y_prompt, y_sample, ident):
    with Scope(nc, "back") as s:
        rows = s.sb("rows", [P, 2, D])
        turned = s.ps("turned", [P, 4, 4, P])
        half_turned = s.sem("half_turned")
        half_kept = s.sem("half_kept")
        stored = [s.sem(f"stored{n}") for n in range(2)]
        yp = y_prompt[0].rearrange("(n p) d -> n p d", p=P)
        block = s.block()

        @block.sync
        def _(sp):
            for n in range(TILES + 1):
                sp.wait_ge(half_kept, 2 * n + 2)
                if n < TILES:
                    sp.dma_start(yp[n], rows[:, n % 2, :]).then_inc(stored[n % 2], 16)
                else:
                    sp.dma_start(y_sample.rearrange("b t d -> (b t) d"), rows[0:NS, n % 2, :]).then_inc(stored[n % 2], 16)
            sp.wait_ge(stored[0], 16 * (TILES // 2 + 1))
            sp.wait_ge(stored[1], 16 * (TILES // 2))

        @block.tensor
        def _(pe):
            for n in range(TILES + 1):
                w = P if n < TILES else NS
                for h in range(2):
                    if n >= 2:
                        pe.wait_ge(half_kept, 2 * n - 3 + h)
                    for k in range(4):
                        m = nc.tensor.transpose(turned[0:w, 2 * (n % 2) + h, k, :],
                                                xT[:, 4 * h + k, n * P:n * P + w], ident[:, :])
                    m.then_inc(half_turned, 1)

        @block.vector
        def _(dve):
            for n in range(TILES + 1):
                w = P if n < TILES else NS
                for h in range(2):
                    dve.wait_ge(half_turned, 2 * n + h + 1)
                    if n >= 2 and h == 0:
                        dve.wait_ge(stored[n % 2], 16 * (n // 2))
                    nc.vector.tensor_copy(rows[0:w, n % 2, 4 * h * P:4 * (h + 1) * P],
                                          turned[0:w, 2 * (n % 2) + h, :, :].rearrange("p a b -> p (a b)")
                                          ).then_inc(half_kept, 1)


def normalise(nc, tag, xT, gain, hhi, hlo, ones):
    with Scope(nc, tag) as s:
        sq = s.sb("sq", [P, 2, KD, CH])
        full = s.sb("full", [P, 2, KD, CH])
        var = s.sb("var", [P, NCH, CH])
        root = s.sb("root", [P, NCH, CH])
        tmp = s.sb("tmp", [P, CH])
        total = s.ps("total", [P, NCH, 512])
        g = s.sb("gain", [P, KD])
        gain_in = s.sem("gain_in")
        squared = s.sem("squared")
        summed = s.sem("summed")
        step = s.sem("step")
        var_ready = s.sem("var_ready")
        logged = s.sem("logged")
        rooted = s.sem("rooted")
        scaled = s.sem("scaled")
        hi_done = s.sem("hi_done")
        lo_done = s.sem("lo_done")
        block = s.block()
        HALF = KD // 2

        def cols(c):
            return slice(c * CH, (c + 1) * CH)

        @block.sync
        def _(sp):
            sp.dma_start(g[:, :], gain).then_inc(gain_in, 16)

        @block.scalar
        def _(act):
            def square(c):
                if c >= 2:
                    act.wait_ge(summed, c - 1)
                for h in range(2):
                    nc.scalar.activation(sq[:, c % 2, h * HALF:(h + 1) * HALF, :], xT[:, h * HALF:(h + 1) * HALF, cols(c)],
                                         ACT.Square).then_inc(squared, 1)

            def hi(c):
                for h in range(2):
                    act.wait_ge(scaled, 2 * c + h + 1)
                    k = slice(h * HALF, (h + 1) * HALF)
                    nc.scalar.activation(hhi[:, k, cols(c)], full[:, c % 2, k, :], ACT.Copy).then_inc(hi_done, 1)

            square(0)
            square(1)
            for c in range(NCH):
                act.wait_ge(var_ready, c + 1)
                nc.scalar.activation(root[:, c, :], var[:, c, :], ACT.Ln).then_inc(logged, 1)
                act.wait_ge(logged, c + 1)
                nc.scalar.activation(root[:, c, :], root[:, c, :], ACT.Exp, scale=-0.5).then_inc(rooted, 1)
                if c + 2 < NCH:
                    square(c + 2)
                hi(c)

        @block.tensor
        def _(pe):
            for c in range(NCH):
                for k in range(KD):
                    if k % HALF == 0:
                        pe.wait_ge(squared, 2 * c + k // HALF + 1)
                    m = nc.tensor.matmul(total[:, c, 0:CH], ones[:, :], sq[:, c % 2, k, :], start=(k == 0),
                                         stop=(k == KD - 1))
                m.then_inc(summed, 1)

        @block.gpsimd
        def _(pool):
            for c in range(NCH):
                k = slice(0, HALF)
                pool.wait_ge(hi_done, 2 * c + 1)
                nc.gpsimd.tensor_tensor(hlo[:, k, cols(c)], full[:, c % 2, k, :], hhi[:, k, cols(c)], ALU.subtract
                                        ).then_inc(lo_done, 1)

        @block.vector
        def _(dve):
            steps = [0]

            def done(ins):
                ins.then_inc(step, 1)
                steps[0] += 1
                dve.wait_ge(step, steps[0])

            def lo(c):
                k = slice(HALF, KD)
                dve.wait_ge(hi_done, 2 * c + 2)
                done(nc.vector.tensor_tensor(hlo[:, k, cols(c)], full[:, c % 2, k, :], hhi[:, k, cols(c)], ALU.subtract))

            dve.wait_ge(gain_in, 16)
            for c in range(NCH):
                dve.wait_ge(summed, c + 1)
                nc.vector.tensor_scalar(var[:, c, :], total[:, c, 0:CH], 1.0 / D, EPS, ALU.mult, ALU.add).then_inc(var_ready, 1)
                dve.wait_ge(rooted, c + 1)
                done(nc.vector.tensor_tensor(tmp[:, :], root[:, c, :], root[:, c, :], ALU.mult))
                done(nc.vector.tensor_tensor(tmp[:, :], tmp[:, :], var[:, c, :], ALU.mult))
                done(nc.vector.tensor_scalar(tmp[:, :], tmp[:, :], -0.5, 1.5, ALU.mult, ALU.add))
                done(nc.vector.tensor_tensor(root[:, c, :], root[:, c, :], tmp[:, :], ALU.mult))
                if c >= 2:
                    dve.wait_ge(lo_done, c - 1)
                for k in range(KD):
                    m = nc.vector.scalar_tensor_tensor(full[:, c % 2, k, :], xT[:, k, cols(c)], g[:, k:k + 1],
                                                       root[:, c, :], ALU.mult, ALU.mult)
                    if k % HALF == HALF - 1:
                        m.then_inc(scaled, 1)
                lo(c)


def split_product(nc, out, w_hi, w_lo, x_hi, x_lo, first, last):
    nc.tensor.matmul(out, w_hi, x_hi, start=first, stop=False)
    nc.tensor.matmul(out, w_hi, x_lo, start=False, stop=False)
    return nc.tensor.matmul(out, w_lo, x_hi, start=False, stop=last)


def swiglu(nc, tag, xT, hhi, hlo, w_gate, w_up, w_down):
    with Scope(nc, tag) as s:
        raw = s.sb("raw", [P, RAW, UNIT])
        whi = s.sb("whi", [P, RAW, UNIT], F32R)
        wlo = s.sb("wlo", [P, RAW, UNIT], F32R)
        act_out = s.sb("silu", [P, 2, CH])
        prod = s.sb("prod", [P, 2, CH])
        ahi = s.sb("ahi", [P, 2, T], F32R)
        alo = s.sb("alo", [P, 2, T], F32R)
        gu = s.ps("gu", [P, 2, 2, 512])
        dn = s.ps("dn", [P, 4, 512])
        raw_loaded = [s.sem(f"raw_loaded{n}") for n in range(RAW)]
        w_hi_done = s.sem("w_hi_done")
        w_lo_done = s.sem("w_lo_done")
        gu_done = s.sem("gu_done")
        silu_done = s.sem("silu_done")
        prod_done = s.sem("prod_done")
        a_hi_done = s.sem("a_hi_done")
        a_lo_done = s.sem("a_lo_done")
        down_done = s.sem("down_done")
        down_free = s.sem("down_free")
        block = s.block()
        wg = w_gate[0].rearrange("(k p) f -> p k f", p=P)
        wu = w_up[0].rearrange("(k p) f -> p k f", p=P)
        wd = w_down[0].rearrange("(j p) n -> j p n", p=P)

        @block.sync
        def _(sp):
            def load(g, u, wait):
                if wait:
                    sp.wait_ge(w_lo_done, 6 * g + u - RAW + 1)
                if u < 4:
                    src = (wg, wu)[u % 2][:, :, DynSlice((2 * g + u // 2) * P, P)]
                    dst = raw[:, u, :].rearrange("p (k f) -> p k f", k=KD)
                else:
                    src = wd[DynSlice(2 * g + u - 4, 1)].rearrange("a p n -> (a p) n")
                    dst = raw[:, u, :]
                sp.dma_start(dst, src).then_inc(raw_loaded[u], 16)

            for u in range(6):
                load(0, u, False)
            with sp.Fori(1, PAIRS) as g:
                for u in range(6):
                    load(g, u, True)

        @block.scalar
        def _(act):
            def hi(i, k, wait=True):
                if wait and k in (2, 3):
                    act.wait_ge(gu_done, 6 * i)
                elif wait and k in (4, 5):
                    act.wait_ge(down_done, 24 * i)
                elif wait:
                    act.wait_ge(gu_done, 6 * i + 3)
                act.wait_ge(raw_loaded[k % 6], 16 * (i + k // 6) + 16)
                nc.scalar.activation(whi[:, k % 6, :], raw[:, k % 6, :], ACT.Copy).then_inc(w_hi_done, 1)

            def silu(i, q):
                act.wait_ge(gu_done, 6 * i + q + 1)
                nc.scalar.activation(act_out[:, q % 2, :], gu[:, q % 2, 0, 0:CH], ACT.Silu).then_inc(silu_done, 1)

            def round_(i, last=False):
                hi(i, 2)
                hi(i, 3)
                hi(i, 4)
                hi(i, 5)
                for q in range(3):
                    silu(i, q)
                if not last:
                    hi(i, 6)
                    hi(i, 7)
                for q in range(3, 6):
                    silu(i, q)

            for k in range(6):
                hi(0, k, False)
            for q in range(3):
                silu(0, q)
            hi(0, 6)
            hi(0, 7)
            for q in range(3, 6):
                silu(0, q)
            with act.Fori(1, PAIRS - 1) as i:
                round_(i)
            round_(PAIRS - 1, True)

        @block.vector
        def _(dve):
            def lo(i, k):
                dve.wait_ge(w_hi_done, 6 * i + k + 1)
                nc.vector.tensor_tensor(wlo[:, k % 6, :], raw[:, k % 6, :], whi[:, k % 6, :], ALU.subtract
                                        ).then_inc(w_lo_done, 1)

            def product(i, q, first=False):
                b, cols = q // 3, slice(q % 3 * CH, (q % 3 + 1) * CH)
                dve.wait_ge(silu_done, 6 * i + q + 1)
                nc.vector.tensor_tensor(prod[:, q % 2, :], act_out[:, q % 2, :], gu[:, q % 2, 1, 0:CH], ALU.mult
                                        ).then_inc(prod_done, 1)
                dve.wait_ge(prod_done, 6 * i + q + 1)
                if not first:
                    dve.wait_ge(down_done, 24 * i)
                nc.vector.tensor_copy(ahi[:, b, cols], prod[:, q % 2, :]).then_inc(a_hi_done, 1)
                dve.wait_ge(a_hi_done, 6 * i + q + 1)
                nc.vector.tensor_tensor(alo[:, b, cols], prod[:, q % 2, :], ahi[:, b, cols], ALU.subtract
                                        ).then_inc(a_lo_done, 1)

            def add_down(i):
                for j in range(NCH * KD):
                    c, k = j // KD, j % KD
                    dve.wait_ge(down_done, 24 * i + j + 1)
                    x = xT[:, k, c * CH:(c + 1) * CH]
                    nc.vector.scalar_tensor_tensor(x, dn[:, j % 4, 0:CH], 0.5, x, ALU.mult, ALU.add
                                                   ).then_inc(down_free, 1)

            def round_(i, last=False):
                lo(i, 2)
                lo(i, 3)
                add_down(i - 1)
                lo(i, 4)
                lo(i, 5)
                for q in range(3):
                    product(i, q)
                if not last:
                    lo(i, 6)
                    lo(i, 7)
                for q in range(3, 6):
                    product(i, q)

            dve.sem_inc(down_free, 4)
            for k in range(6):
                lo(0, k)
            for q in range(3):
                product(0, q, True)
            lo(0, 6)
            lo(0, 7)
            for q in range(3, 6):
                product(0, q, True)
            with dve.Fori(1, PAIRS - 1) as i:
                round_(i)
            round_(PAIRS - 1, True)
            add_down(PAIRS - 1)

        @block.tensor
        def _(pe):
            def gate_up(i, b, first=False):
                pe.wait_ge(w_lo_done, 6 * i + 2 * b + 2)
                for c in range(NCH):
                    q = 3 * b + c
                    cols = slice(c * CH, (c + 1) * CH)
                    if not (first and q < 2):
                        pe.wait_ge(prod_done, 6 * i + q - 1)
                    for m in range(2):
                        u = 2 * b + m
                        for k in range(KD):
                            w = slice(k * P, (k + 1) * P)
                            last = split_product(nc, gu[:, q % 2, m, 0:CH], whi[:, u, w], wlo[:, u, w],
                                                 hhi[:, k, cols], hlo[:, k, cols], k == 0, k == KD - 1)
                    last.then_inc(gu_done, 1)

            def down(i):
                pe.wait_ge(w_lo_done, 6 * i + 6)
                for j in range(NCH * KD):
                    c, k = j // KD, j % KD
                    cols = slice(c * CH, (c + 1) * CH)
                    if k == 0:
                        pe.wait_ge(a_lo_done, 6 * i + 3 + c + 1)
                    pe.wait_ge(down_free, 24 * i + j + 1)
                    for b in range(2):
                        last = split_product(nc, dn[:, j % 4, 0:CH], whi[:, 4 + b, k * P:(k + 1) * P],
                                             wlo[:, 4 + b, k * P:(k + 1) * P], ahi[:, b, cols], alo[:, b, cols],
                                             b == 0, b == 1)
                    last.then_inc(down_done, 1)

            gate_up(0, 0, True)
            gate_up(0, 1)
            with pe.Fori(1, PAIRS) as i:
                down(i - 1)
                gate_up(i, 0)
                gate_up(i, 1)
            down(PAIRS - 1)


HD = 64
HEADS, KV = 8, 4
TT = TILES + 1
CW = 256
SROW = P - NS
CHUNKS = [("q", 0), ("q", 256), ("k", 512), ("v", 768), ("qi", 1024), ("qi", 1280), ("ki", 1536),
          ("hv", 2632), ("hv", 2888)]
KI_COLS = HD + HEADS


def newton_rsqrt(nc, done, root, var, tmp):
    done(nc.vector.tensor_tensor(tmp, root, root, ALU.mult))
    done(nc.vector.tensor_tensor(tmp, tmp, var, ALU.mult))
    done(nc.vector.tensor_scalar(tmp, tmp, -0.5, 1.5, ALU.mult, ALU.add))
    done(nc.vector.tensor_tensor(root, root, tmp, ALU.mult))


def token_projections(nc, hhi, hlo, w_in, q_gain, k_gain, cos, sin, ident, qT_d, kT_d, qiT_d, kiT_d, wi_d, hv_d,
                      k_prompt, k_sample, v_prompt, v_sample, ki_prompt, ki_sample):
    NC = len(CHUNKS)
    M = NC * TT
    with Scope(nc, "tok") as s:
        raw = s.sb("raw", [P, 2, KD, CW])
        whi = s.sb("whi", [P, 2, KD, CW], F32R)
        wlo = s.sb("wlo", [P, 2, KD, CW], F32R)
        taken = s.sb("taken", [P, 4, CW])
        sq = s.sb("sq", [P, 2, CW])
        var = s.sb("var", [P, 4])
        inv = s.sb("inv", [P, 4])
        root = s.sb("root", [P, 4])
        tmp = s.sb("tmp", [P, 4])
        xn = s.sb("xn", [P, CW])
        ra = s.sb("ra", [P, CW])
        rb = s.sb("rb", [P, CW])
        out = s.sb("out", [P, 4, CW])
        stage = s.sb("stage", [P, 2, 2, T])
        gains = s.sb("gains", [P, 2, HD])
        cs = s.sb("cs", [P, TT, HD])
        sn = s.sb("sn", [P, TT, HD])
        proj = s.ps("proj", [P, 4, 512])
        turned = s.ps("turned", [P, 2, 4, P])
        w_loaded = [s.sem(f"w_loaded{n}") for n in range(2)]
        tables_in = s.sem("tables_in")
        w_hi_done, w_lo_done = s.sem("w_hi_done"), s.sem("w_lo_done")
        proj_done, take_done, sq_done = s.sem("proj_done"), s.sem("take_done"), s.sem("sq_done")
        inv_done, root_done = s.sem("inv_done"), s.sem("root_done")
        step, out_done = s.sem("step"), s.sem("out_done")
        turn_done, kept_done = s.sem("turn_done"), s.sem("kept_done")
        out_stored = [s.sem(f"out_stored{n}") for n in range(4)]
        stage_stored = [s.sem(f"stage_stored{n}") for n in range(2)]
        block = s.block()

        def kind(m):
            return CHUNKS[m // TT][0]

        def width(c):
            return KI_COLS if CHUNKS[c][0] == "ki" else CW

        def normed(m):
            return kind(m) in "qk"

        def turns(m):
            return kind(m) not in ("v", "hv")

        def stores(m):
            return {"k": 1, "v": 1, "hv": 1, "ki": 2}.get(kind(m), 0)

        def count(f, m):
            return sum(1 for x in range(m) if f(x))

        def stored_before(m, slot):
            return sum(stores(x) for x in range(m) if x % 4 == slot)

        wv = w_in[0].rearrange("(k p) f -> p k f", p=P)

        @block.sync
        def _(sp):
            def load(c):
                if c >= 2:
                    sp.wait_ge(w_lo_done, c - 1)
                w, at = width(c), CHUNKS[c][1]
                sp.dma_start(raw[:, c % 2, :, 0:w], wv[:, :, at:at + w]).then_inc(w_loaded[c % 2], 16)

            load(0)
            for dst, src in ((gains[:, 0, :], q_gain.partition_broadcast(P)), (gains[:, 1, :], k_gain.partition_broadcast(P)),
                             (cs[:, :, :], cos), (sn[:, :, :], sin)):
                sp.dma_start(dst, src).then_inc(tables_in, 16)
            load(1)
            for m in range(M):
                c, n = m // TT, m % TT
                if n == 4 and c + 2 < NC:
                    load(c + 2)
                rows = slice(0, P) if n < TILES else slice(SROW, P)
                at = slice(n * P, (n + 1) * P)
                o = out[rows, m % 4, :]
                if stores(m):
                    sp.wait_ge(out_done, m + 1)
                if kind(m) == "k":
                    dst = k_prompt[at] if n < TILES else k_sample
                    sp.dma_start(dst, o).then_inc(out_stored[m % 4], 16)
                elif kind(m) == "v":
                    dst = v_prompt[at] if n < TILES else v_sample
                    sp.dma_start(dst, o).then_inc(out_stored[m % 4], 16)
                elif kind(m) == "hv":
                    dst = hv_d[n * P:n * P + (P if n < TILES else NS), (c - 7) * CW:(c - 6) * CW]
                    sp.dma_start(dst, o).then_inc(out_stored[m % 4], 16)
                elif kind(m) == "ki":
                    dst = ki_prompt[at] if n < TILES else ki_sample
                    sp.dma_start(dst, o[:, 0:HD]).then_inc(out_stored[m % 4], 16)
                    dst = wi_d[n * P:n * P + (P if n < TILES else NS)]
                    sp.dma_start(dst, o[:, 2 * HD:2 * HD + HEADS]).then_inc(out_stored[m % 4], 16)
                if n == TT - 1 and turns(m):
                    sp.wait_ge(kept_done, count(turns, m + 1))
                    dst = {"q": qT_d, "k": kT_d, "qi": qiT_d, "ki": kiT_d}[kind(m)]
                    b = {"q": 2 * c, "k": 0, "qi": 2 * (c - 4), "ki": 0}[kind(m)]
                    nb = 1 if kind(m) == "ki" else 2
                    sp.dma_start(dst[b:b + nb].rearrange("b p t -> p b t"), stage[:, c % 2, 0:nb, :]
                                 ).then_inc(stage_stored[c % 2], 16)
            for slot in range(4):
                sp.wait_ge(out_stored[slot], 16 * stored_before(M, slot))
            for slot in range(2):
                sp.wait_ge(stage_stored[slot], 16 * sum(1 for c in range(NC) if c % 2 == slot and turns(TT * c)))

        @block.gpsimd
        def _(pool):
            for c in range(NC):
                w = width(c)
                pool.wait_ge(w_hi_done, c + 1)
                nc.gpsimd.tensor_tensor(wlo[:, c % 2, :, 0:w], raw[:, c % 2, :, 0:w], whi[:, c % 2, :, 0:w],
                                        ALU.subtract).then_inc(w_lo_done, 1)

        @block.tensor
        def _(pe):
            def turn(m):
                if m < 0 or m >= M or not turns(m):
                    return
                x = count(turns, m)
                if x >= 2:
                    pe.wait_ge(kept_done, x - 1)
                pe.wait_ge(out_done, m + 1)
                for b in range(1 if kind(m) == "ki" else 2):
                    last = nc.tensor.transpose(turned[:, x % 2, b, :], out[:, m % 4, b * P:(b + 1) * P], ident[:, :])
                last.then_inc(turn_done, 1)

            for m in range(M):
                c, n = m // TT, m % TT
                w = width(c)
                if n == 0:
                    pe.wait_ge(w_lo_done, c + 1)
                if m >= 4:
                    pe.wait_ge(take_done, m - 3)
                tok = slice(n * P, (n + 1) * P) if n < TILES else slice(T - P, T)
                for k in range(KD):
                    ps = proj[:, m % 4, 0:w]
                    nc.tensor.matmul(ps, hhi[:, k, tok], whi[:, c % 2, k, 0:w], start=(k == 0), stop=False)
                    nc.tensor.matmul(ps, hhi[:, k, tok], wlo[:, c % 2, k, 0:w], start=False, stop=False)
                    last = nc.tensor.matmul(ps, hlo[:, k, tok], whi[:, c % 2, k, 0:w], start=False, stop=(k == KD - 1))
                last.then_inc(proj_done, 1)
                turn(m - 2)
            turn(M - 2)
            turn(M - 1)

        @block.scalar
        def _(act):
            def hi(c):
                w = width(c)
                act.wait_ge(w_loaded[c % 2], 16 * (c // 2) + 16)
                if c >= 2:
                    act.wait_ge(proj_done, TT * (c - 1))
                nc.scalar.activation(whi[:, c % 2, :, 0:w], raw[:, c % 2, :, 0:w], ACT.Copy).then_inc(w_hi_done, 1)

            def keep(m):
                if m < 0 or m >= M or not turns(m):
                    return
                c, n = m // TT, m % TT
                act.wait_ge(turn_done, count(turns, m + 1))
                prior = sum(1 for x in range(c) if x % 2 == c % 2 and turns(TT * x))
                if n == 0 and prior:
                    act.wait_ge(stage_stored[c % 2], 16 * prior)
                nb = 1 if kind(m) == "ki" else 2
                x = count(turns, m) % 2
                if n < TILES:
                    dst, src = stage[:, c % 2, 0:nb, n * P:(n + 1) * P], turned[:, x, 0:nb, :]
                else:
                    dst, src = stage[:, c % 2, 0:nb, SEQ:T], turned[:, x, 0:nb, SROW:P]
                nc.scalar.activation(dst, src, ACT.Copy).then_inc(kept_done, 1)

            hi(0)
            hi(1)
            for m in range(M):
                c, n = m // TT, m % TT
                w = width(c)
                act.wait_ge(proj_done, m + 1)
                if m >= 4:
                    act.wait_ge(out_done, m - 3)
                nc.scalar.activation(taken[:, m % 4, 0:w], proj[:, m % 4, 0:w], ACT.Copy).then_inc(take_done, 1)
                if normed(m):
                    act.wait_ge(take_done, m + 1)
                    nc.scalar.activation(sq[:, m % 2, :], taken[:, m % 4, :], ACT.Square).then_inc(sq_done, 1)
                    act.wait_ge(inv_done, count(normed, m + 1))
                    nc.scalar.activation(root[:, :], inv[:, :], ACT.Sqrt).then_inc(root_done, 1)
                keep(m - 3)
                if n == 0 and 1 <= c < NC - 1:
                    hi(c + 1)
            for m in range(M - 3, M):
                keep(m)

        @block.vector
        def _(dve):
            steps = [0]

            def done(ins):
                ins.then_inc(step, 1)
                steps[0] += 1
                dve.wait_ge(step, steps[0])

            def rope(src, n, heads):
                def over(table, a, b):
                    return table[:, n, a:b].unsqueeze(1).broadcast_to([P, heads, b - a])

                h = HD // 2
                a = ra[:, 0:heads * HD].rearrange("p (h d) -> p h d", d=HD)
                b = rb[:, 0:heads * HD].rearrange("p (h d) -> p h d", d=HD)
                done(nc.vector.tensor_tensor(a, src, over(cs, 0, HD), ALU.mult))
                done(nc.vector.tensor_tensor(b[:, :, 0:h], src[:, :, h:HD], over(sn, 0, h), ALU.mult))
                done(nc.vector.tensor_tensor(b[:, :, h:HD], src[:, :, 0:h], over(sn, h, HD), ALU.mult))
                return a, b

            dve.wait_ge(tables_in, 64)
            for m in range(M):
                c, n = m // TT, m % TT
                slot = m % 4
                x = taken[:, slot, :].rearrange("p (h d) -> p h d", d=HD)
                if normed(m):
                    dve.wait_ge(sq_done, count(normed, m + 1))
                    done(nc.vector.tensor_reduce(var[:, :], sq[:, m % 2, :].rearrange("p (h d) -> p h d", d=HD),
                                                 AX.X, ALU.add))
                    done(nc.vector.tensor_scalar(var[:, :], var[:, :], 1.0 / HD, EPS, ALU.mult, ALU.add))
                    nc.vector.reciprocal(inv[:, :], var[:, :]).then_inc(inv_done, 1)
                    dve.wait_ge(root_done, count(normed, m + 1))
                    newton_rsqrt(nc, done, root[:, :], var[:, :], tmp[:, :])
                    y = xn[:, :].rearrange("p (h d) -> p h d", d=HD)
                    done(nc.vector.tensor_tensor(y, x, root[:, :].unsqueeze(2).broadcast_to([P, 4, HD]), ALU.mult))
                    g = gains[:, 0 if kind(m) == "q" else 1, :].unsqueeze(1).broadcast_to([P, 4, HD])
                    done(nc.vector.tensor_tensor(y, y, g, ALU.mult))
                    x = y
                if m:
                    dve.wait_ge(out_done, m)
                if m >= 4:
                    dve.wait_ge(take_done, m + 1)
                    if turns(m - 4):
                        dve.wait_ge(turn_done, count(turns, m - 3))
                    if stores(m - 4):
                        dve.wait_ge(out_stored[slot], 16 * stored_before(m, slot))
                else:
                    dve.wait_ge(take_done, m + 1)
                if not turns(m):
                    nc.vector.tensor_copy(out[:, slot, :], taken[:, slot, :]).then_inc(out_done, 1)
                elif kind(m) == "ki":
                    x = x[:, 0:1, :]
                    a, b = rope(x, n, 1)
                    o = out[:, slot, :].rearrange("p (h d) -> p h d", d=HD)
                    done(nc.vector.tensor_tensor(o[:, 0:1, :], a, b, ALU.add))
                    done(nc.vector.tensor_copy(o[:, 1:2, :], o[:, 0:1, :]))
                    nc.vector.tensor_scalar(out[:, slot, 2 * HD:2 * HD + HEADS], taken[:, slot, HD:HD + HEADS],
                                            float(HEADS) ** -0.5, None, ALU.mult).then_inc(out_done, 1)
                else:
                    a, b = rope(x, n, 4)
                    if kind(m) == "q":
                        o = out[:, slot, :].rearrange("p (r g d) -> p g r d", g=2, d=HD)
                        a = a.rearrange("p (g r) d -> p g r d", g=2)
                        b = b.rearrange("p (g r) d -> p g r d", g=2)
                    else:
                        o = out[:, slot, :].rearrange("p (h d) -> p h d", d=HD)
                    nc.vector.tensor_tensor(o, a, b, ALU.add).then_inc(out_done, 1)


SLABS = TILES - 2 + 1
TOPK = 256
PAGES = 8
PS = 128
PAST = PAGES * PS
SW = PAST + DT
PADB = P + DT
FLOOR = -3.0e38
MASKED = -1.0e30
N_POOL = 80


def slab_width(s):
    return (s + 3) * P if s < SLABS - 1 else SW


def spread(wide):
    return wide.rearrange("p (b c) -> p b c", c=PADB)[:, :, 0:P].rearrange("p b (h t) -> p b h t", t=NS)[:, :, :, 0:DT]


def index_scores(nc, scores, qiT_d, kiT_d, wi_d, cache_idx_k, page_table, same_token, new_floor, ident):
    with Scope(nc, "idx") as s:
        q_raw = s.sb("q_raw", [P, HEADS, P])
        q_both = s.sb("q_both", [P, 2, HEADS, P], F32R)
        q_new = s.sb("q_new", [P, 4, NS])
        k_lo = s.sb("k_lo", [P, T], F32R)
        k_hi = s.sb("k_hi", [P, T], F32R)
        w = s.sb("w", [P, TILES, HEADS])
        w_rows = s.sb("w_rows", [P, 2])
        wide_lo = s.sb("wide_lo", [P, DB * PADB], F32R)
        wide_hi = s.sb("wide_hi", [P, DB * PADB], F32R)
        pages = s.sb("pages", [P, 2, PAGES, HD])
        past_hi = s.sb("past_hi", [P, 2, PAST], F32R)
        past_lo = s.sb("past_lo", [P, 2, PAST], F32R)
        relu_room = s.sb("relus", [P, 3 * SW])
        relus = relu_room[:, :].rearrange("p (n k) -> p n k", n=3)
        k_raw, wide = relu_room[:, 0:T], relu_room[:, T:T + DB * PADB]
        sel = s.sb("sel", [P, P])
        floor = s.sb("floor", [P, DT])
        table = s.sb("table", [1, DB * PAGES], I32)
        part = relus[:, 2, :]
        big = s.ps("big", [P, 6 * 512])
        turned = s.ps("turned", [P, 2, 512])
        q_in = s.sem("q_in")
        q_hi_done, q_lo_done = s.sem("q_hi_done"), s.sem("q_lo_done")
        k_hi_done, k_lo_done, wide_hi_done, wide_lo_done = (s.sem("k_hi_done"), s.sem("k_lo_done"), s.sem("wide_hi_done"),
                                                            s.sem("wide_lo_done"))
        past_hi_done, past_lo_done = s.sem("past_hi_done"), s.sem("past_lo_done")
        loads = [s.sem("q_new_in"), s.sem("kiT_in"), s.sem("w_in"), s.sem("w_rows_in"), s.sem("sel_in"), s.sem("floor_in")]
        q_new_in, kiT_in, w_in, w_rows_in, sel_in, floor_in = loads
        table_in = s.sem("table_in")
        pages_in = [s.sem(f"pages_in{n}") for n in range(2)]
        zeroed, spread_done = s.sem("zeroed"), s.sem("spread_done")
        page_turned, hi_raised, lo_raised = s.sem("page_turned"), s.sem("hi_raised"), s.sem("lo_raised")
        seq_scored = s.sem("seq_scored")
        sample_relu, sample_part, sample_sum, sample_done = (s.sem("sample_relu"), s.sem("sample_part"),
                                                             s.sem("sample_sum"), s.sem("sample_done"))
        head_scored, relu_done, head_added, masked = (s.sem("head_scored"), s.sem("relu_done"), s.sem("head_added"),
                                                      s.sem("masked"))
        block = s.block()
        steps = [(t, h) for t in range(2, TILES) for h in range(HEADS)]

        def split_lo(pool, t):
            pool.wait_ge(q_hi_done, t - 1)
            if t > 4:
                pool.wait_ge(masked, t - 4)
            q = q_both[HD:P, t % 2, :, :]
            nc.gpsimd.tensor_tensor(q, q_raw[HD:P, :, :], q, ALU.subtract).then_inc(q_lo_done, 1)
            pool.wait_ge(q_lo_done, t - 1)

        @block.sync
        def _(sp):
            sp.dma_start(table[:, :], page_table.rearrange("(a b) n -> a (b n)", a=1)).then_inc(table_in, 16)
            sp.dma_start(q_new[:, :, :], qiT_d[:, :, SEQ:T].rearrange("b p t -> p b t")).then_inc(q_new_in, 16)
            sp.dma_start(k_raw, kiT_d[0]).then_inc(kiT_in, 16)
            sp.dma_start(w[:, :, :], wi_d[0:SEQ].rearrange("(n p) h -> p n h", p=P)).then_inc(w_in, 16)
            for h in range(4):
                sp.dma_start(w_rows[NS * h:NS * (h + 1), :], wi_d[SEQ:T, 2 * h:2 * h + 2]).then_inc(w_rows_in, 16)
            sp.dma_start(sel[:, :], same_token).then_inc(sel_in, 16)
            sp.dma_start(floor[:, :], new_floor).then_inc(floor_in, 16)
            sp.wait_ge(table_in, 16)

            def load(i, n, wait):
                if wait:
                    sp.wait_ge(page_turned, 4 * i - 2 + 2 * n)
                for g in range(PAGES):
                    page = sp.value_load(table[0:1, DynSlice(PAGES * (2 * i + n) + g, 1)], min_val=0, max_val=N_POOL - 1)
                    sp.dma_start(pages[:, n, g, :], cache_idx_k[0][DynSlice(page, 1)].rearrange("a s d -> (a s) d")
                                 ).then_inc(pages_in[n], 16)

            load(0, 0, False)
            load(0, 1, False)
            with sp.Fori(1, DB // 2) as i:
                for n in range(2):
                    load(i, n, True)

            for t in range(2, TILES):
                if t >= 3:
                    sp.wait_ge(q_lo_done, t - 2)
                for half in range(2):
                    for e in range(2):
                        sp.dma_start(q_raw[half * HD:(half + 1) * HD, :, :].rearrange("p (b e) t -> p e b t", e=2)[:, e],
                                     qiT_d[:, e * HD:(e + 1) * HD, t * P:(t + 1) * P].rearrange("b p t -> p b t")
                                     ).then_inc(q_in, 16)

        @block.gpsimd
        def _(pool):
            pool.wait_ge(k_hi_done, 1)
            nc.gpsimd.tensor_tensor(k_lo[:, :], k_raw, k_hi[:, :], ALU.subtract).then_inc(k_lo_done, 1)
            for b in range(DB):
                for x in range(2):
                    cols = slice(x * 512, (x + 1) * 512)
                    if b or x:
                        pool.wait_ge(lo_raised, 2 * b + x)
                    else:
                        pool.wait_ge(k_lo_done, 1)
                    pool.wait_ge(past_lo_done, 2 * b + x + 1)
                    nc.gpsimd.tensor_copy(past_lo[HD:P, b % 2, cols], past_lo[0:HD, b % 2, cols]).then_inc(lo_raised, 1)
            pool.wait_ge(lo_raised, 2 * DB)
            for t in range(2, 4):
                split_lo(pool, t)
            for t in range(2, TILES):
                if t + 2 < TILES:
                    split_lo(pool, t + 2)
                pool.wait_ge(head_added, HEADS * (t - 1))
                d = scores[:, t - 2, t * P:(t + 1) * P]
                nc.gpsimd.affine_select(out=d, in_=d, compare_op=ALU.is_ge, fill=FLOOR, base=0, pattern=[[-1, P]],
                                        channel_multiplier=1).then_inc(masked, 1)

        @block.tensor
        def _(pe):
            def turn(b):
                pe.wait_ge(pages_in[b % 2], 16 * PAGES * (b // 2 + 1))
                if b:
                    pe.wait_ge(past_lo_done, 2 * b)
                for x in range(2):
                    for g in range(4):
                        last = nc.tensor.transpose(turned[0:HD, x, g * PS:(g + 1) * PS], pages[:, b % 2, 4 * x + g, :],
                                                   ident[:, :])
                    last.then_inc(page_turned, 1)

            turn(0)
            pe.wait_ge(wide_lo_done, 1)
            pe.wait_ge(k_lo_done, 1)
            for b in range(DB):
                if b + 1 < DB:
                    turn(b + 1)
                pe.wait_ge(hi_raised, 2 * b + 2)
                pe.wait_ge(lo_raised, 2 * b + 2)
                for half in range(2):
                    r = slice(half * HD, (half + 1) * HD)
                    q_h, q_l = wide_hi[r, b * P:(b + 1) * P], wide_lo[r, b * P:(b + 1) * P]
                    for x in range(2):
                        cols = slice(x * 512, (x + 1) * 512)
                        split_product(nc, big[:, (3 * half + x) * 512:(3 * half + x + 1) * 512], q_h, q_l,
                                      past_hi[r, b % 2, cols], past_lo[r, b % 2, cols], b == 0, b == DB - 1)
                    cols = slice(SEQ + DT * b, SEQ + DT * (b + 1))
                    last = split_product(nc, big[:, (3 * half + 2) * 512:(3 * half + 2) * 512 + DT], q_h, q_l,
                                         k_hi[r, cols], k_lo[r, cols], b == 0, b == DB - 1)
                last.then_inc(seq_scored, 1)
            pe.wait_ge(sel_in, 16)
            pe.wait_ge(sample_part, 2)
            for x in range(3):
                n = 512 if x < 2 else DT
                last = nc.tensor.matmul(big[:, x * 512:x * 512 + n], sel[:, :], relus[:, 2, x * 512:x * 512 + n],
                                        start=True, stop=True)
            last.then_inc(sample_sum, 1)
            for a, (t, h) in enumerate(steps):
                if a < 2:
                    pe.wait_ge(sample_done, a + 1)
                if a >= 3:
                    pe.wait_ge(relu_done, a - 2)
                if h == 0:
                    pe.wait_ge(q_lo_done, t - 1)
                at = (a + 2) % 3 * 1024
                for x in range(0, (t + 1) * P, 512):
                    n = min(512, (t + 1) * P - x)
                    nc.tensor.matmul(big[:, at + x:at + x + n], q_both[:, t % 2, h, :], k_hi[:, x:x + n], start=True,
                                     stop=False)
                    last = nc.tensor.matmul(big[:, at + x:at + x + n], q_both[:, t % 2, h, :], k_lo[:, x:x + n],
                                            start=False, stop=True)
                last.then_inc(head_scored, 1)

        def split_hi(t):
            nc.scalar.wait_ge(q_in, 64 * (t - 1))
            if t >= 4:
                nc.scalar.wait_ge(head_scored, HEADS * (t - 3))
            nc.scalar.activation(q_both[:, t % 2, :, :], q_raw[:, :, :], ACT.Copy).then_inc(q_hi_done, 1)

        @block.scalar
        def _(act):
            act.wait_ge(kiT_in, 16)
            nc.scalar.activation(k_hi[:, :], k_raw, ACT.Copy).then_inc(k_hi_done, 1)
            act.wait_ge(spread_done, 1)
            nc.scalar.activation(wide_hi[:, :], wide, ACT.Copy).then_inc(wide_hi_done, 1)
            for b in range(DB):
                for x in range(2):
                    cols = slice(x * 512, (x + 1) * 512)
                    act.wait_ge(page_turned, 2 * b + x + 1)
                    if b >= 2:
                        act.wait_ge(seq_scored, b - 1)
                    nc.scalar.activation(past_hi[0:HD, b % 2, cols], turned[0:HD, x, :], ACT.Copy).then_inc(past_hi_done, 1)
                for x in range(2):
                    cols = slice(x * 512, (x + 1) * 512)
                    act.wait_ge(past_hi_done, 2 * b + x + 1)
                    nc.scalar.activation(past_hi[HD:P, b % 2, cols], past_hi[0:HD, b % 2, cols], ACT.Copy
                                         ).then_inc(hi_raised, 1)
            for t in range(2, 4):
                split_hi(t)
            act.wait_ge(seq_scored, DB)
            for half in range(2):
                nc.scalar.activation(relus[:, half, 0:SW], big[:, half * 1536:half * 1536 + SW], ACT.Relu,
                                     scale=HD ** -0.5).then_inc(sample_relu, 1)
            for a, (t, h) in enumerate(steps):
                if h == 0 and 3 <= t < TILES - 1:
                    split_hi(t + 1)
                act.wait_ge(head_scored, a + 1)
                if a < 3:
                    act.wait_ge(sample_part, 2)
                    if a == 2:
                        act.wait_ge(sample_sum, 1)
                else:
                    act.wait_ge(head_added, a - 2)
                n = (t + 1) * P
                at = (a + 2) % 3 * 1024
                nc.scalar.activation(relus[:, a % 3, 0:n], big[:, at:at + n], ACT.Relu, scale=HD ** -0.5
                                     ).then_inc(relu_done, 1)

        @block.vector
        def _(dve):
            nc.vector.memset(wide, 0.0).then_inc(zeroed, 1)
            dve.wait_ge(zeroed, 1)
            dve.wait_ge(q_new_in, 16)
            nc.vector.tensor_copy(spread(wide), q_new[:, :, :].rearrange("p h (b j) -> p b h j", j=DT)
                                  ).then_inc(spread_done, 1)
            dve.wait_ge(wide_hi_done, 1)
            nc.vector.tensor_tensor(wide_lo[:, :], wide, wide_hi[:, :], ALU.subtract
                                    ).then_inc(wide_lo_done, 1)
            for b in range(DB):
                for x in range(2):
                    cols = slice(x * 512, (x + 1) * 512)
                    dve.wait_ge(past_hi_done, 2 * b + x + 1)
                    nc.vector.tensor_tensor(past_lo[0:HD, b % 2, cols], turned[0:HD, x, :], past_hi[0:HD, b % 2, cols],
                                            ALU.subtract).then_inc(past_lo_done, 1)
            dve.wait_ge(w_rows_in, 64)
            dve.wait_ge(sample_relu, 1)
            nc.vector.tensor_scalar(part, relus[:, 0, 0:SW], w_rows[:, 0:1], None, ALU.mult).then_inc(sample_part, 1)
            dve.wait_ge(sample_part, 1)
            dve.wait_ge(sample_relu, 2)
            nc.vector.scalar_tensor_tensor(part, relus[:, 1, 0:SW], w_rows[:, 1:2], part, ALU.mult, ALU.add
                                           ).then_inc(sample_part, 1)
            dve.wait_ge(sample_sum, 1)
            dve.wait_ge(floor_in, 16)
            nc.vector.tensor_tensor(scores[:, SLABS - 1, PAST:SW], big[:, PAST:SW], floor[:, :], ALU.add
                                    ).then_inc(sample_done, 1)
            nc.vector.tensor_copy(scores[:, SLABS - 1, 0:PAST], big[:, 0:PAST]).then_inc(sample_done, 1)
            dve.wait_ge(w_in, 16)
            for a, (t, h) in enumerate(steps):
                dve.wait_ge(relu_done, a + 1)
                n = (t + 1) * P
                sc = scores[:, t - 2, 0:n]
                if h == 0:
                    i = nc.vector.tensor_scalar(sc, relus[:, a % 3, 0:n], w[:, t, 0:1], None, ALU.mult)
                else:
                    dve.wait_ge(head_added, a)
                    i = nc.vector.scalar_tensor_tensor(sc, relus[:, a % 3, 0:n], w[:, t, h:h + 1], sc, ALU.mult, ALU.add)
                i.then_inc(head_added, 1)


SECTIONS = [("silu", 1608, 2, 0), ("silu", 3144, 2, 4), ("forget", 2120, 2, 8), ("gate", 3656, 8, 16)]
FEATS = 32


def select_keys_and_project(nc, scores, masks, hhi, hlo, w_in, feat_d):
    with Scope(nc, "sel") as s:
        raw = s.sb("raw", [P, 2, UNIT])
        whi = s.sb("whi", [P, 2, UNIT], F32R)
        wlo = s.sb("wlo", [P, 2, UNIT], F32R)
        stage = s.sb("stage", [P, 2, 2, T])
        over = s.sb("over", [P, SW], mybir.dt.bfloat16)
        equal = s.sb("equal", [P, SW], mybir.dt.bfloat16)
        rank = s.sb("rank", [P, SW])
        count = s.sb("count", [P, SLABS])
        bits = s.sb("bits", [P, SLABS], I32)
        cand = s.sb("cand", [P, SLABS], I32)
        flip = s.sb("flip", [P, SLABS], I32)
        gain = s.sb("gain", [P, SLABS], I32)
        bit = s.sb("bit", [P, SLABS], I32)
        bitf = s.sb("bitf", [P, SLABS])
        thr = s.sb("thr", [P, SLABS], I32)
        proj = s.ps("proj", [P, 2, NCH, 512])
        w_loaded = [s.sem(f"w_loaded{n}") for n in range(2)]
        w_hi_done, w_lo_done = s.sem("w_hi_done"), s.sem("w_lo_done")
        proj_done, proj_read, kept_done = s.sem("proj_done"), s.sem("proj_read"), s.sem("kept_done")
        stage_stored = [s.sem(f"stage_stored{n}") for n in range(2)]
        step, passes = s.sem("step"), s.sem("passes")
        block = s.block()
        wv = w_in[0].rearrange("(k p) f -> p k f", p=P)
        pairs_before = [sum(x[2] for x in SECTIONS[:n]) for n in range(len(SECTIONS) + 1)]
        stored_per = {"silu": 1, "forget": 2, "gate": 1}
        stored_before = [sum(x[2] * stored_per[x[0]] for x in SECTIONS[:n]) for n in range(len(SECTIONS) + 1)]

        def sections(engine, body, peel_last=False):
            for n, (_, _, pairs, _) in enumerate(SECTIONS):
                first = 0
                end = pairs - 1 if peel_last and n == len(SECTIONS) - 1 else pairs
                if n == 0:
                    body(0, 0, 0, True)
                    first = 1
                with engine.Fori(first, end) as i:
                    body(n, i, i + pairs_before[n], False)
            if peel_last:
                body(len(SECTIONS) - 1, end, end + pairs_before[-2], False, True)

        @block.sync
        def _(sp):
            def body(n, i, pair, first):
                kind, col, _, at = SECTIONS[n]
                for u in range(2):
                    if not first:
                        sp.wait_ge(w_lo_done, 2 * pair + u - 1)
                    sp.dma_start(raw[:, u, :].rearrange("p (k f) -> p k f", k=KD), wv[:, :, DynSlice(col + (2 * i + u) * P, P)]
                                 ).then_inc(w_loaded[u], 16)

            sections(sp, body)

        @block.gpsimd
        def _(pool):
            def body(n, i, pair, first):
                for u in range(2):
                    pool.wait_ge(w_hi_done, 2 * pair + u + 1)
                    nc.gpsimd.tensor_tensor(wlo[:, u, :], raw[:, u, :], whi[:, u, :], ALU.subtract).then_inc(w_lo_done, 1)

            sections(pool, body)

        @block.tensor
        def _(pe):
            def body(n, i, pair, first):
                for u in range(2):
                    pe.wait_ge(w_lo_done, 2 * pair + u + 1)
                    for c in range(NCH):
                        cols = slice(c * CH, (c + 1) * CH)
                        if not first:
                            pe.wait_ge(proj_read, 6 * pair + 3 * u + c - 5)
                        for k in range(KD):
                            w = slice(k * P, (k + 1) * P)
                            last = split_product(nc, proj[:, u, c, 0:CH], whi[:, u, w], wlo[:, u, w], hhi[:, k, cols],
                                                 hlo[:, k, cols], k == 0, k == KD - 1)
                        last.then_inc(proj_done, 1)

            sections(pe, body)

        @block.scalar
        def _(act):
            def hi(u, pair):
                act.wait_ge(w_loaded[u], 16 * pair + 16)
                nc.scalar.activation(whi[:, u, :], raw[:, u, :], ACT.Copy).then_inc(w_hi_done, 1)

            def body(n, i, pair, first, last=False):
                kind, _, _, at = SECTIONS[n]
                for u in range(2):
                    if not first:
                        stored = stored_before[n] + stored_per[kind] * i
                        act.wait_ge(stage_stored[u], 16 * stored)
                    for c in range(NCH):
                        cols = slice(c * CH, (c + 1) * CH)
                        act.wait_ge(proj_done, 6 * pair + 3 * u + c + 1)
                        if kind == "forget":
                            nc.scalar.activation(stage[:, u, 1, cols], proj[:, u, c, 0:CH], ACT.Sigmoid, scale=-1.0
                                                 ).then_inc(kept_done, 1)
                        func = ACT.Silu if kind == "silu" else ACT.Sigmoid
                        nc.scalar.activation(stage[:, u, 0, cols], proj[:, u, c, 0:CH], func).then_inc(proj_read, 1)
                    if not last:
                        hi(u, pair + 1)
                    act.wait_ge(proj_read, 6 * pair + 3 * u + 3)
                    act.dma_start(feat_d[DynSlice(at + 2 * i + u, 1)].rearrange("a p t -> (a p) t"), stage[:, u, 0, :]
                                  ).then_inc(stage_stored[u], 16)
                    if kind == "forget":
                        act.wait_ge(kept_done, 6 * i + 3 * u + 3)
                        act.dma_start(feat_d[DynSlice(at + 4 + 2 * i + u, 1)].rearrange("a p t -> (a p) t"),
                                      stage[:, u, 1, :]).then_inc(stage_stored[u], 16)

            hi(0, 0)
            hi(1, 0)
            sections(act, body, True)
            for u in range(2):
                act.wait_ge(stage_stored[u], 16 * stored_before[-1])

        @block.vector
        def _(dve):
            steps = [0]

            def count_all(r):
                for x in range(SLABS):
                    n = slab_width(x)
                    if x >= 2:
                        dve.wait_ge(passes, SLABS * r + x - 1)
                    flags = (over, equal)[x % 2]
                    nc.vector.tensor_scalar(flags[:, 0:n], scores[:, x, 0:n], thr[:, x:x + 1].bitcast(F32), None,
                                            ALU.is_ge, ALU.add, accum_out=count[:, x:x + 1]).then_inc(passes, 1)
                dve.wait_ge(passes, SLABS * (r + 1))

            def done(ins, at=None):
                ins.then_inc(step, 1)
                steps[0] += 1
                dve.wait_ge(step, steps[0] if at is None else at)

            done(nc.vector.memset(thr[:, :], 0))
            done(nc.vector.memset(bits[:, :], 0))
            done(nc.vector.memset(bit[:, :], 1 << 30))
            done(nc.vector.memset(bitf[:, :], float(1 << 30)))
            count_all(0)
            done(nc.vector.tensor_scalar(flip[:, :], count[:, :], TOPK - 0.5, -1.0, ALU.is_ge, ALU.add))
            base, per = steps[0], 7
            with dve.Fori(0, 31) as r:
                at = [per * r + (base + 1 + n) for n in range(per)]
                done(nc.vector.tensor_tensor(cand[:, :], bits[:, :], bit[:, :], ALU.bitwise_or), at[0])
                done(nc.vector.tensor_tensor(thr[:, :], cand[:, :], flip[:, :], ALU.bitwise_xor), at[1])
                count_all(r + 1)
                done(nc.vector.tensor_scalar(gain[:, :], count[:, :], TOPK - 0.5, None, ALU.is_ge), at[2])
                done(nc.vector.tensor_tensor(gain[:, :], gain[:, :], bitf[:, :], ALU.mult), at[3])
                done(nc.vector.tensor_tensor(bits[:, :], bits[:, :], gain[:, :], ALU.bitwise_or), at[4])
                done(nc.vector.tensor_scalar(bit[:, :], bit[:, :], 1, None, ALU.logical_shift_right), at[5])
                done(nc.vector.tensor_scalar(bitf[:, :], bitf[:, :], 0.5, None, ALU.mult), at[6])
            steps[0] = base + per * 31
            done(nc.vector.tensor_tensor(thr[:, :], bits[:, :], flip[:, :], ALU.bitwise_xor))
            for x in range(SLABS):
                n = slab_width(x)
                sc, t = scores[:, x, 0:n], thr[:, x:x + 1].bitcast(F32)
                done(nc.vector.tensor_scalar(over[:, 0:n], sc, t, None, ALU.is_gt, ALU.add, accum_out=count[:, x:x + 1]))
                done(nc.vector.tensor_scalar(count[:, x:x + 1], count[:, x:x + 1], -1.0, float(TOPK), ALU.mult, ALU.add))
                done(nc.vector.tensor_scalar(equal[:, 0:n], sc, t, None, ALU.is_equal))
                done(nc.vector.tensor_tensor_scan(rank[:, 0:n], equal[:, 0:n], equal[:, 0:n], 0.0, ALU.add, ALU.max))
                done(nc.vector.scalar_tensor_tensor(equal[:, 0:n], rank[:, 0:n], count[:, x:x + 1], equal[:, 0:n],
                                                    ALU.is_le, ALU.mult))
                done(nc.vector.scalar_tensor_tensor(over[:, 0:n], equal[:, 0:n], -1.0, over[:, 0:n], ALU.add, ALU.add))
                done(nc.vector.tensor_scalar(masks[:, x, 0:n], over[:, 0:n], -MASKED, None, ALU.mult))


def attention(nc, mixed_d, masks, qT_d, kT_d, v_prompt, v_sample, cache_k, cache_v, page_table, causal, own, ident):
    SLOTS = 4
    SP_PAGES = 5
    FIRST = 3
    with Scope(nc, "att") as s:
        tile_out = s.sb("tile_out", [P, 2, 4, P])
        new_out = s.sb("new_out", [P, 4, NS])
        q_new = s.sb("q_new", [P, 4, NS])
        k_new = s.sb("k_new", [P, 2, NS])
        q_raw = s.sb("q_raw", [P, HEADS, P])
        q_both = s.sb("q_both", [P, 2, HEADS, P], F32R)
        k_lo = s.sb("k_lo", [P, KV, SEQ], F32R)
        k_hi = s.sb("k_hi", [P, KV, SEQ], F32R)
        v = s.sb("v", [P, TILES, KV * HD])
        v_new = s.sb("v_new", [NS, KV * HD])
        causal_sb = s.sb("causal", [P, 2 * P])
        own_sb = s.sb("own", [P, DB, DT])
        table = s.sb("table", [1, DB * PAGES], I32)
        wide = s.sb("wide", [P, DB * PADB])
        pages = s.sb("pages", [P, SLOTS, PAGES, KV * HD])
        past = s.sb("past", [P, 2, 2, PAST])
        logits = s.sb("logits", [P, 2, SW])
        probs_room = s.sb("probs", [P, 3 * SW])
        probs = probs_room[:, :].rearrange("p (n k) -> p n k", n=3)
        new_probs = s.sb("new_probs", [P, 2, DB, DT])
        s_probsT = s.sb("s_probsT", [P, 2, PAGES, P])
        probsT = s.sb("probsT", [P, 2, TILES, P])
        new_probsT = s.sb("new_probsT", [NS, 2, P])
        k_raw = [probsT[:, :, :, :].rearrange("p a b c -> p a (b c)"),
                 probs_room[:, 0:2 * SEQ].rearrange("p (e t) -> p e t", e=2)]
        top = s.sb("top", [P, 2])
        bias = s.sb("bias", [P, 2])
        mass = s.sb("mass", [P, 2, HEADS])
        share = s.sb("share", [P, HEADS])
        heads = s.sb("heads", [P, HEADS * HD])
        big = s.ps("big", [P, 6 * 512])
        turned = s.ps("turned", [P, 2, 512])
        names = ("table", "q_new", "k_new", "k0", "k1", "v", "v_new", "causal", "own")
        loaded = {n: s.sem(f"{n}_in") for n in names}
        pages_in = [s.sem(f"pages_in{n}") for n in range(SLOTS)]
        zeroed, spread_done = s.sem("zeroed"), s.sem("spread_done")
        page_turned, low_kept, high_kept = s.sem("page_turned"), s.sem("low_kept"), s.sem("high_kept")
        seq_scored, s_logits, s_bias, s_exp, s_norm = (s.sem("seq_scored"), s.sem("s_logits"), s.sem("s_bias"),
                                                       s.sem("s_exp"), s.sem("s_norm"))
        s_share, s_new, s_out, s_kept = s.sem("s_share"), s.sem("s_new"), s.sem("s_out"), s.sem("s_kept")
        new_turned, new_kept = s.sem("new_turned"), s.sem("new_kept")
        scored, masked, top_done, bias_done, exp_done = (s.sem("scored"), s.sem("masked"), s.sem("top_done"),
                                                         s.sem("bias_done"), s.sem("exp_done"))
        low_turned, high_turned, low_ready, high_ready = (s.sem("low_turned"), s.sem("high_turned"), s.sem("low_ready"),
                                                          s.sem("high_ready"))
        mixed, share_done, heads_done, out_turned, out_kept = (s.sem("mixed"), s.sem("share_done"), s.sem("heads_done"),
                                                               s.sem("out_turned"), s.sem("out_kept"))
        stored = [s.sem(f"stored{n}") for n in range(2)]
        new_stored = s.sem("new_stored")
        values_in = [s.sem(f"values_in{n}") for n in range(SLOTS)]
        q_in = s.sem("q_in")
        hi_done, lo_done = s.sem("hi_done"), s.sem("lo_done")
        block = s.block()
        steps = [(t, h) for t in range(TILES) for h in range(HEADS)]
        SCALE = HD ** -0.5
        out_ps = big[:, 4 * 512:5 * 512]
        back_ps = big[:, 5 * 512:6 * 512]
        s_out_ps = big[:, 5 * 512:5 * 512 + 4 * NS].rearrange("p (G c) -> p G c", G=2)

        def high_before(a):
            return sum(1 for t, _ in steps[:a] if t >= 4)

        def load_pages(engine, cache, b, sems, which):
            for g in which:
                page = engine.value_load(table[0:1, PAGES * b + g:PAGES * b + g + 1], min_val=0, max_val=N_POOL - 1)
                engine.dma_start(pages[:, b % SLOTS, g, :], cache[DynSlice(page, 1)].rearrange("a s d -> (a s) d")
                                 ).then_inc(sems[b % SLOTS], 16)

        def load_values(engine, which, sems):
            for b in range(SLOTS):
                engine.wait_ge(page_turned, 4 * (DB - SLOTS + b + 1))
                load_pages(engine, cache_v, b, sems, which)
            for b in range(SLOTS, DB):
                engine.wait_ge(s_out, b - SLOTS + 1)
                load_pages(engine, cache_v, b, sems, which)

        @block.gpsimd
        def _(pool):
            def split_q(t):
                pool.wait_ge(q_in, 32 * t + 32)
                if t >= 2:
                    pool.wait_ge(scored, HEADS * (t - 1))
                nc.gpsimd.tensor_copy(q_both[:, t % 2, :, :], q_raw[:, :, :]).then_inc(hi_done, 1)
                pool.wait_ge(hi_done, t + 3)
                lo = q_both[HD:P, t % 2, :, :]
                nc.gpsimd.tensor_tensor(lo, q_raw[HD:P, :, :], lo, ALU.subtract).then_inc(lo_done, 1)
                pool.wait_ge(lo_done, t + 3)

            for G in range(2):
                pool.wait_ge(loaded[f"k{G}"], 32)
                hi, lo = k_hi[:, 2 * G:2 * G + 2, :], k_lo[:, 2 * G:2 * G + 2, :]
                nc.gpsimd.tensor_copy(hi, k_raw[G]).then_inc(hi_done, 1)
                pool.wait_ge(hi_done, G + 1)
                nc.gpsimd.tensor_tensor(lo, k_raw[G], hi, ALU.subtract).then_inc(lo_done, 1)
            split_q(0)
            split_q(1)
            pool.wait_ge(loaded["table"], 16)
            load_values(pool, range(SP_PAGES, PAGES), values_in)
            for t in range(2, TILES):
                split_q(t)

        @block.sync
        def _(sp):
            for n, dst, src in (("table", table[:, :], page_table.rearrange("(a b) n -> a (b n)", a=1)),
                                ("q_new", q_new[:, :, :], qT_d[:, :, SEQ:T].rearrange("b p t -> p b t")),
                                ("k_new", k_new[:, :, :], kT_d[:, :, SEQ:T].rearrange("b p t -> p b t"))):
                sp.dma_start(dst, src).then_inc(loaded[n], 16)
            sp.wait_ge(loaded["table"], 16)

            for b in range(SLOTS):
                load_pages(sp, cache_k, b, pages_in, range(PAGES))

            def load_q(t):
                if t:
                    sp.wait_ge(lo_done, t + 2)
                for half in range(2):
                    sp.dma_start(q_raw[half * HD:(half + 1) * HD, :, :],
                                 qT_d[:, :, t * P:(t + 1) * P].rearrange("b (e p) t -> p (b e) t", e=2)).then_inc(q_in, 16)

            def store(t):
                sp.wait_ge(out_kept, t + 1)
                sp.dma_start(mixed_d[0:4, :, t * P:(t + 1) * P].rearrange("b p t -> p b t"), tile_out[:, t % 2, :, :]
                             ).then_inc(stored[t % 2], 16)

            for G in range(2):
                for half in range(2):
                    sp.dma_start(k_raw[G][half * HD:(half + 1) * HD],
                                 kT_d[G, :, 0:SEQ].rearrange("(e p) t -> p e t", e=2)).then_inc(loaded[f"k{G}"], 16)
            load_q(0)
            for n, dst, src in (("v", v[:, :, :], v_prompt.rearrange("(n p) d -> p n d", p=P)),
                                ("v_new", v_new[:, :], v_sample), ("causal", causal_sb[:, :], causal),
                                ("own", own_sb[:, :, :], own)):
                sp.dma_start(dst, src).then_inc(loaded[n], 16)
            for b in range(SLOTS, DB):
                sp.wait_ge(page_turned, 4 * (b - SLOTS + 1))
                load_pages(sp, cache_k, b, pages_in, range(PAGES))
            load_q(1)
            load_values(sp, range(SP_PAGES), pages_in)
            for t in range(2, TILES):
                load_q(t)
                store(t - 2)
                if t == 3:
                    sp.wait_ge(s_kept, 2)
                    sp.dma_start(mixed_d[0:4, :, SEQ:T].rearrange("b p t -> p b t"), new_out[:, :, :]).then_inc(new_stored, 16)
            store(TILES - 2)
            store(TILES - 1)
            for n in range(2):
                sp.wait_ge(stored[n], 16 * TILES // 2)
            sp.wait_ge(new_stored, 16)

        @block.tensor
        def _(pe):
            def turn(b):
                pe.wait_ge(pages_in[b % SLOTS], 16 * PAGES * (b // SLOTS + 1))
                for f in range(4):
                    x = f % 2
                    if 2 * b + f // 2:
                        pe.wait_ge((low_kept, high_kept)[x], 2 * b + f // 2)
                    for g in range(4):
                        last = nc.tensor.transpose(turned[:, x, g * PS:(g + 1) * PS],
                                                   pages[:, b % SLOTS, 4 * x + g, f // 2 * P:(f // 2 + 1) * P], ident[:, :])
                    last.then_inc(page_turned, 1)

            turn(0)
            pe.wait_ge(spread_done, 1)
            pe.wait_ge(loaded["k_new"], 16)
            for b in range(DB):
                if b + 1 < DB:
                    turn(b + 1)
                pe.wait_ge(low_kept, 2 * b + 2)
                pe.wait_ge(high_kept, 2 * b + 2)
                for G in range(2):
                    for g in range(2):
                        r = slice(g * HD, (g + 1) * HD)
                        q = wide[r, b * P + G * 2 * NS:b * P + (G + 1) * 2 * NS]
                        for x in range(2):
                            nc.tensor.matmul(big[r, (3 * G + x) * 512:(3 * G + x + 1) * 512], q,
                                             past[r, b % 2, G, x * 512:(x + 1) * 512], start=(b == 0), stop=(b == DB - 1))
                        last = nc.tensor.matmul(big[r, (3 * G + 2) * 512:(3 * G + 2) * 512 + DT], q,
                                                k_new[r, G, DT * b:DT * (b + 1)], start=(b == 0),
                                                stop=(b == DB - 1))
                last.then_inc(seq_scored, 1)
            for f in range(4):
                G, x = f // 2, f % 2
                pe.wait_ge(s_norm, G + 1)
                pe.wait_ge((low_kept, high_kept)[x], 2 * DB + G)
                for g in range(4):
                    last = nc.tensor.transpose(turned[:, x, g * P:(g + 1) * P],
                                               probs[:, G, (4 * x + g) * PS:(4 * x + g + 1) * PS], ident[:, :])
                last.then_inc(page_turned, 1)
            pe.wait_ge(s_new, 2)
            pe.wait_ge(s_logits, 2)
            for G in range(2):
                last = nc.tensor.transpose(big[0:NS, 512 + G * P:512 + (G + 1) * P],
                                           new_probs[:, G, :, :].rearrange("p b j -> p (b j)"), ident[:, :])
            last.then_inc(new_turned, 1)
            pe.wait_ge(new_kept, 1)
            pe.wait_ge(loaded["v_new"], 16)
            for G in range(2):
                for g in range(2):
                    r = slice(g * HD, (g + 1) * HD)
                    kv = 2 * G + g
                    nc.tensor.matmul(s_out_ps[r, G, :], v_new[:, kv * HD:(kv + 1) * HD],
                                     new_probsT[:, G, r], start=(G == 0), stop=False)
            pe.wait_ge(low_kept, 2 * DB + 2)
            pe.wait_ge(high_kept, 2 * DB + 2)

            def mix_pages(b):
                pe.wait_ge(pages_in[b % SLOTS], 16 * (PAGES * (DB // SLOTS) + SP_PAGES * (b // SLOTS + 1)))
                pe.wait_ge(values_in[b % SLOTS], 16 * (PAGES - SP_PAGES) * (b // SLOTS + 1))
                for G in range(2):
                    for g in range(2):
                        r = slice(g * HD, (g + 1) * HD)
                        kv = 2 * G + g
                        o = s_out_ps[r, G, :].rearrange("p (r t) -> p r t", t=NS)
                        for n in range(PAGES):
                            p = s_probsT[:, G, n, r].rearrange("p (r t) -> p r t", t=NS)
                            last = nc.tensor.matmul(o[:, :, DT * b:DT * (b + 1)],
                                                    pages[:, b % SLOTS, n, kv * HD:(kv + 1) * HD],
                                                    p[:, :, DT * b:DT * (b + 1)], start=False,
                                                    stop=(b == DB - 1 and G == 1 and n == PAGES - 1))
                last.then_inc(s_out, 1)

            def score(a):
                t, h = steps[a]
                if a >= 2:
                    pe.wait_ge(masked, a - 1)
                if h == 0:
                    pe.wait_ge(lo_done, t + 3)
                g, rr = h // 2, h % 2
                q = q_both[:, t % 2, 2 * (g // 2 * 2 + rr) + g % 2, :]
                for x in range(0, (t + 1) * P, 512):
                    n = min(512, (t + 1) * P - x)
                    out = big[:, a % 2 * 1024 + x:a % 2 * 1024 + x + n]
                    nc.tensor.matmul(out, q, k_hi[:, g, x:x + n], start=True, stop=False)
                    last = nc.tensor.matmul(out, q, k_lo[:, g, x:x + n], start=False, stop=True)
                last.then_inc(scored, 1)

            def turn_probs(a):
                t, h = steps[a]
                pe.wait_ge(exp_done, a + 1)
                for x in range(1 if t < 4 else 2):
                    if x == 0 and a:
                        pe.wait_ge(low_ready, a)
                    if x == 1 and high_before(a):
                        pe.wait_ge(high_ready, high_before(a))
                    for j in range(4 * x, min(4 * x + 4, t + 1)):
                        last = nc.tensor.transpose(turned[:, x, (j - 4 * x) * P:(j - 4 * x + 1) * P],
                                                   probs[:, a % 3, j * P:(j + 1) * P], ident[:, :])
                    last.then_inc((low_turned, high_turned)[x], 1)

            def mix(a):
                t, h = steps[a]
                if h == 0 and t:
                    pe.wait_ge(heads_done, 2 * t)
                pe.wait_ge(low_ready, a + 1)
                if t >= 4:
                    pe.wait_ge(high_ready, high_before(a + 1))
                for j in range(t + 1):
                    last = nc.tensor.matmul(out_ps[:, h * HD:(h + 1) * HD], probsT[:, a % 2, j, :],
                                            v[:, j, h // 2 * HD:(h // 2 + 1) * HD], start=(j == 0), stop=(j == t))
                last.then_inc(mixed, 1)

            def turn_out(t):
                pe.wait_ge(heads_done, 2 * t + 2)
                if t:
                    pe.wait_ge(out_kept, t)
                else:
                    pe.wait_ge(s_kept, 2)
                for n in range(4):
                    last = nc.tensor.transpose(back_ps[:, n * P:(n + 1) * P], heads[:, n * P:(n + 1) * P], ident[:, :])
                last.then_inc(out_turned, 1)

            pe.wait_ge(loaded["v"], 16)
            for a in range(len(steps) + 5):
                if a < len(steps):
                    score(a)
                if 2 <= a <= len(steps) + 1:
                    turn_probs(a - 2)
                if 3 <= a <= len(steps) + 2:
                    mix(a - 3)
                if FIRST <= a < FIRST + DB:
                    mix_pages(a - FIRST)
                if a >= 12 and (a - 4) % HEADS == 0:
                    turn_out((a - 4) // HEADS - 1)

        @block.scalar
        def _(act):
            act.wait_ge(spread_done, 1)
            for b in range(DB):
                for G in range(2):
                    act.wait_ge(page_turned, 4 * b + 2 * G + 2)
                    if b >= 2:
                        act.wait_ge(seq_scored, b - 1)
                    nc.scalar.activation(past[:, b % 2, G, 512:1024], turned[:, 1, :], ACT.Copy).then_inc(high_kept, 1)
            act.wait_ge(lo_done, 2)
            for G in range(2):
                act.wait_ge(s_bias, G + 1)
                nc.scalar.activation(probs[:, G, :], logits[:, G, :], ACT.Exp, bias=bias[:, G:G + 1], scale=SCALE,
                                     accum_out=mass[:, 0, G:G + 1]).then_inc(s_exp, 1)
            for G in range(2):
                act.wait_ge(page_turned, 4 * DB + 2 * G + 2)
                nc.scalar.activation(s_probsT[:, G, 4:8, :].rearrange("p a b -> p (a b)"), turned[:, 1, :], ACT.Copy
                                     ).then_inc(high_kept, 1)
            act.wait_ge(s_new, 2)
            for a in range(len(steps) + 5):
                if a < len(steps):
                    t, h = steps[a]
                    n = (t + 1) * P
                    act.wait_ge(bias_done, a + 1)
                    if a >= 3:
                        act.wait_ge(low_turned, a - 2)
                        if high_before(a - 2):
                            act.wait_ge(high_turned, high_before(a - 2))
                    if h == 0 and t >= 2:
                        act.wait_ge(share_done, t - 1)
                    nc.scalar.activation(probs[:, a % 3, 0:n], logits[:, a % 2, 0:n], ACT.Exp, bias=bias[:, a % 2:a % 2 + 1],
                                         scale=SCALE, accum_out=mass[:, t % 2, h:h + 1]).then_inc(exp_done, 1)
                if 2 <= a <= len(steps) + 1 and steps[a - 2][0] >= 4:
                    t, h = steps[a - 2]
                    act.wait_ge(high_turned, high_before(a - 1))
                    act.wait_ge(mixed, a - 3)
                    nc.scalar.activation(probsT[:, a % 2, 4:t + 1, :],
                                         turned[:, 1, 0:(t - 3) * P].rearrange("p (a b) -> p a b", b=P), ACT.Copy
                                         ).then_inc(high_ready, 1)
                if a == FIRST + DB:
                    act.wait_ge(s_out, DB)
                    for G in range(2):
                        nc.scalar.activation(new_out[:, 2 * G:2 * G + 2, :],
                                             s_out_ps[:, G, :].rearrange("p (r t) -> p r t", t=NS), ACT.Copy
                                             ).then_inc(s_kept, 1)
                if a >= 12 and (a - 4) % HEADS == 0:
                    t = (a - 4) // HEADS - 1
                    act.wait_ge(out_turned, t + 1)
                    if t >= 2:
                        act.wait_ge(stored[t % 2], 16 * (t // 2))
                    nc.scalar.activation(tile_out[:, t % 2, :, :], back_ps.rearrange("p (a b) -> p a b", b=P), ACT.Copy
                                         ).then_inc(out_kept, 1)

        @block.vector
        def _(dve):
            nc.vector.memset(wide[:, :], 0.0).then_inc(zeroed, 1)
            dve.wait_ge(zeroed, 1)
            dve.wait_ge(loaded["q_new"], 16)
            nc.vector.tensor_copy(spread(wide[:, :]), q_new[:, :, :].rearrange("p h (b j) -> p b h j", j=DT)
                                  ).then_inc(spread_done, 1)
            for b in range(DB):
                for G in range(2):
                    dve.wait_ge(page_turned, 4 * b + 2 * G + 1)
                    if b >= 2:
                        dve.wait_ge(seq_scored, b - 1)
                    nc.vector.tensor_copy(past[:, b % 2, G, 0:512], turned[:, 0, :]).then_inc(low_kept, 1)
            dve.wait_ge(seq_scored, DB)
            for G in range(2):
                nc.vector.tensor_tensor_reduce(logits[:, G, :], masks[:, SLABS - 1, :], big[:, 1536 * G:1536 * G + SW], 1.0,
                                               FLOOR, ALU.add, ALU.max, top[:, G:G + 1]).then_inc(s_logits, 1)
                dve.wait_ge(s_logits, G + 1)
                nc.vector.tensor_scalar(bias[:, G:G + 1], top[:, G:G + 1], -SCALE, None, ALU.mult).then_inc(s_bias, 1)
            dve.wait_ge(loaded["own"], 16)
            for G in range(2):
                dve.wait_ge(s_exp, G + 1)
                nc.vector.reciprocal(share[:, G:G + 1], mass[:, 0, G:G + 1]).then_inc(s_share, 1)
                dve.wait_ge(s_share, G + 1)
                nc.vector.tensor_scalar(probs[:, G, :], probs[:, G, :], share[:, G:G + 1], None, ALU.mult).then_inc(s_norm, 1)
                dve.wait_ge(s_norm, G + 1)
                nc.vector.tensor_tensor(new_probs[:, G, :, :], own_sb[:, :, :],
                                        probs[:, G, PAST:SW].unsqueeze(1).broadcast_to([P, DB, DT]), ALU.mult
                                        ).then_inc(s_new, 1)
            for G in range(2):
                dve.wait_ge(page_turned, 4 * DB + 2 * G + 1)
                nc.vector.tensor_copy(s_probsT[:, G, 0:4, :].rearrange("p a b -> p (a b)"), turned[:, 0, :]
                                      ).then_inc(low_kept, 1)
            dve.wait_ge(new_turned, 1)
            nc.vector.tensor_copy(new_probsT[:, :, :].rearrange("p a b -> p (a b)"), big[0:NS, 512:512 + 2 * P]
                                  ).then_inc(new_kept, 1)
            dve.wait_ge(loaded["causal"], 16)
            for a in range(len(steps) + 5):
                if a >= 11 and (a - 3) % HEADS == 0:
                    t = (a - 3) // HEADS - 1
                    if t:
                        dve.wait_ge(heads_done, 2 * t)
                    nc.vector.reciprocal(share[:, :], mass[:, t % 2, :]).then_inc(share_done, 1)
                    dve.wait_ge(share_done, t + 1)
                    dve.wait_ge(mixed, HEADS * (t + 1))
                    if t:
                        dve.wait_ge(out_turned, t)
                    half = HEADS * HD // 2
                    for G in range(2):
                        src = out_ps[:, G * half:(G + 1) * half].rearrange("p (g r d) -> p g r d", g=2, r=2)
                        dst = heads[:, G * half:(G + 1) * half].rearrange("p (r g d) -> p g r d", g=2, r=2)
                        w = share[:, 4 * G:4 * G + 4].rearrange("p (g r) -> p g r", g=2).unsqueeze(3)
                        nc.vector.tensor_tensor(dst, src, w.broadcast_to([P, 2, 2, HD]), ALU.mult).then_inc(heads_done, 1)
                if a < len(steps):
                    t, h = steps[a]
                    n = (t + 1) * P
                    dve.wait_ge(scored, a + 1)
                    if a < 2:
                        dve.wait_ge(s_exp, 2)
                    else:
                        dve.wait_ge(exp_done, a - 1)
                    m = masks[:, t - 2, 0:n] if t >= 2 else causal_sb[:, (1 - t) * P:2 * P]
                    nc.vector.tensor_tensor_reduce(logits[:, a % 2, 0:n], m, big[:, a % 2 * 1024:a % 2 * 1024 + n], 1.0,
                                                   FLOOR, ALU.add, ALU.max, top[:, a % 2:a % 2 + 1]).then_inc(masked, 1)
                    dve.wait_ge(masked, a + 1)
                    nc.vector.tensor_scalar(bias[:, a % 2:a % 2 + 1], top[:, a % 2:a % 2 + 1], -SCALE, None, ALU.mult
                                            ).then_inc(bias_done, 1)
                if 2 <= a <= len(steps) + 1:
                    t, h = steps[a - 2]
                    n = min(t + 1, 4)
                    dve.wait_ge(low_turned, a - 1)
                    if a >= 4:
                        dve.wait_ge(mixed, a - 3)
                    nc.vector.tensor_copy(probsT[:, a % 2, 0:n, :],
                                          turned[:, 0, 0:n * P].rearrange("p (a b) -> p a b", b=P)).then_inc(low_ready, 1)


HG = 4
LEVELS = [64, 32, 16, 8, 4, 2, 1]
NL = len(LEVELS) + 1
UW = SEQ // 2 + NS


def recurrence(nc, mixed_d, feat_d, hv_d, state_in, state_prompt, state_sample, bound, hg_gain, resets, level_masks, owner,
               ident, ones):
    with Scope(nc, "hg") as s:
        f = s.sb("f", [P, T])
        G = s.sb("G", [P, T])
        eG = s.sb("eG", [P, T])
        q_in = s.sb("q_in", [P, T])
        kd = s.sb("kd", [P, T])
        decay = s.sb("decay", [P, NL, UW])
        qL = s.sb("qL", [P, NL, T])
        kL = s.sb("kL", [P, NL, T])
        hv = s.sb("hv", [P, TT, P])
        st = s.sb("st", [P, DB, P])
        gate = s.sb("gate", [P, T])
        kept = s.sb("kept", [P, NL, P])
        attn = s.sb("attn", [P, 2, P])
        kdT = s.sb("kdT", [P, 2, P])
        S = s.sb("S", [P, 2, P])
        own_v = s.sb("own_v", [NS, DB, P])
        new_st = s.sb("new_st", [P, DB, P])
        oT = s.sb("oT", [P, T])
        rec = s.sb("rec", [P, T])
        sq = s.sb("sq", [P, UW])
        var = s.sb("var", [P, UW])
        root = s.sb("root", [P, UW])
        reset = s.sb("reset", [P, T])
        masks = s.sb("masks", [P, NL, P])
        own = s.sb("own", [NS, DB])
        lb_in = s.sb("lb_in", [P, 2, HG])
        lb = s.sb("lb", [P, HG])
        omlb = s.sb("omlb", [P, HG])
        lmax = s.sb("lmax", [P, HG])
        lexp = s.sb("lexp", [P, 2, HG])
        lsum = s.sb("lsum", [P, HG])
        gain = s.sb("gain", [P, 1])
        pairs = s.ps("pairs", [P, NL, P])
        o_ps = s.ps("o_ps", [P, 2, 512])
        kd_ps = s.ps("kd_ps", [P, 512])
        st_ps = s.ps("st_ps", [P, 512])
        sum_ps = s.ps("sum_ps", [P, 2, 512])
        tmp = sq

        def two(name):
            return [s.sem(f"{name}{u}") for u in range(2)]

        f_loaded, k_loaded, q_loaded, hv_loaded, gate_loaded = (two("f_loaded"), two("k_loaded"), two("q_loaded"),
                                                                two("hv_loaded"), two("gate_loaded"))
        st_loaded, consts = s.sem("st_loaded"), s.sem("consts")
        bound_step, bound_exp, bound_ready = s.sem("bound_step"), s.sem("bound_exp"), s.sem("bound_ready")
        f_ready, log_ready, G_ready, eG_ready = s.sem("f_ready"), s.sem("log_ready"), s.sem("G_ready"), s.sem("eG_ready")
        q_ready, k_ready, q_in_ready = s.sem("q_ready"), s.sem("k_ready"), s.sem("q_in_ready")
        dist_ready, decay_ready, qL_ready, kL_ready = (s.sem("dist_ready"), s.sem("decay_ready"), s.sem("qL_ready"),
                                                       s.sem("kL_ready"))
        pairs_done, kept_done, attn_done = s.sem("pairs_done"), s.sem("kept_done"), s.sem("attn_done")
        kd_turned, kdT_ready, o_done, o_kept = s.sem("kd_turned"), s.sem("kdT_ready"), s.sem("o_done"), s.sem("o_kept")
        st_done, S_ready = s.sem("st_done"), s.sem("S_ready")
        own_ready, new_done, new_scaled, new_ready, new_stored = (s.sem("own_ready"), s.sem("new_done"), s.sem("new_scaled"),
                                                                  s.sem("new_ready"), s.sem("new_stored"))
        S_stored, rec_stored = s.sem("S_stored"), two("rec_stored")
        squared, summed, var_ready, logged, rooted, multiplied, factor_ready, root_ready, normed, rec_ready = (
            s.sem("squared"), s.sem("summed"), s.sem("var_ready"), s.sem("logged"), s.sem("rooted"), s.sem("multiplied"),
            s.sem("factor_ready"), s.sem("root_ready"), s.sem("normed"), s.sem("rec_ready"))
        block = s.block()
        UNITS = 2 * HG
        CHUNKS_OF = (range(0, TILES // 2), range(TILES // 2, TT))
        COLS = (slice(0, SEQ // 2), slice(SEQ // 2, T))
        WIDTH = (SEQ // 2, T - SEQ // 2)

        def wait(engine, sem, value):
            if not isinstance(value, int) or value > 0:
                engine.wait_ge(sem, value)

        def chunks_through(h, u):
            return TT * h + CHUNKS_OF[u][-1] + 1

        def heads(engine, unit):
            def both(h, first=False, last=False):
                unit(h, 0, (h, 1), None if first else (h - 1, 1))
                unit(h, 1, None if last else (h + 1, 0), (h, 0))

            both(0, first=True)
            with engine.Fori(1, HG - 1) as h:
                both(h)
            both(HG - 1, last=True)

        def tile(n):
            return slice(n * P, (n + 1) * P) if n < TILES else slice(SEQ, T)

        @block.sync
        def _(sp):
            sp.dma_start(lb_in[:, :, :], bound).then_inc(consts, 16)

            def feat(b, h, u, dst, sem):
                sp.dma_start(dst[:, COLS[u]], feat_d[DynSlice(b + h, 1)][:, :, COLS[u]].rearrange("a p t -> (a p) t")
                             ).then_inc(sem[u], 16)

            def load_f(h, u):
                wait(sp, G_ready, 2 * h + u - 1)
                feat(8, h, u, f, f_loaded)

            def load(h, u):
                wait(sp, pairs_done, chunks_through(h - 1, u))
                feat(12, h, u, kL[:, NL - 1, :], k_loaded)
                feat(0, h, u, qL[:, NL - 1, :], q_loaded)
                wait(sp, o_done, chunks_through(h - 1, u))
                lo = u * TILES // 2
                sp.dma_start(hv[:, lo:lo + TILES // 2, :],
                             hv_d[lo * P:lo * P + SEQ // 2, DynSlice(P * h, P)].rearrange("(n p) v -> p n v", p=P)
                             ).then_inc(hv_loaded[u], 16)
                if u == 1:
                    sp.dma_start(hv[0:NS, TILES, :], hv_d[SEQ:T, DynSlice(P * h, P)]).then_inc(hv_loaded[u], 16)

            def load_gate(h, u):
                wait(sp, rec_ready, 2 * h + u - 1)
                feat(4, h, u, gate, gate_loaded)

            def load_state(h):
                wait(sp, o_done, TT * h)
                sp.dma_start(st[:, :, :], state_in[DynSlice(h, 1)].rearrange("a k b v -> (a k) b v")).then_inc(st_loaded, 16)

            def store(h, u, waited=False):
                if not waited:
                    sp.wait_ge(rec_ready, 2 * h + u + 1)
                sp.dma_start(mixed_d[DynSlice(h + 4, 1)][:, :, COLS[u]].rearrange("a p t -> (a p) t"), rec[:, COLS[u]]
                             ).then_inc(rec_stored[u], 16)

            load_f(0, 0)
            sp.dma_start(reset[:, :], resets).then_inc(consts, 16)
            load(0, 0)
            load_f(0, 1)
            sp.dma_start(masks[:, :, :], level_masks).then_inc(consts, 16)
            sp.dma_start(gain[:, :], hg_gain).then_inc(consts, 16)
            sp.dma_start(own[:, :], owner).then_inc(consts, 16)
            load_state(0)
            load_gate(0, 0)

            def unit(h, u, after, before):
                if after:
                    load(*after)
                if after:
                    load_gate(*after)
                if before:
                    store(*before, waited=after is not None)
                if not isinstance(h, int) or h + 1 < HG:
                    load_f(h + 1, u)
                if u == 1:
                    sp.wait_ge(S_ready, TILES * h + TILES)
                    sp.dma_start(state_prompt[DynSlice(h, 1)].rearrange("a k v -> (a k) v"), S[:, 1, :]
                                 ).then_inc(S_stored, 16)
                    sp.wait_ge(new_ready, h + 1)
                    sp.dma_start(state_sample[DynSlice(h, 1)].rearrange("a k b v -> (a k) b v"), new_st[:, :, :]
                                 ).then_inc(new_stored, 16)
                    if after:
                        load_state(h + 1)

            heads(sp, unit)
            store(HG - 1, 1)
            for u in range(2):
                sp.wait_ge(rec_stored[u], 16 * HG)
            sp.wait_ge(S_stored, 16 * HG)
            sp.wait_ge(new_stored, 16 * HG)

        @block.gpsimd
        def _(pool):
            def key_pass(h, u, n):
                U = 2 * h + u
                if n == 0:
                    pool.wait_ge(k_ready, U + 1)
                    wait(pool, kd_turned, chunks_through(h - 1, u))
                pool.wait_ge(decay_ready, NL * U + n + 1)
                w = WIDTH[u] if n == 0 or LEVELS[n - 1] <= 2 else SEQ // 2
                cols = slice(COLS[u].start, COLS[u].start + w)
                dst = kd[:, cols] if n == 0 else kL[:, n - 1, cols]
                nc.gpsimd.tensor_tensor(dst, kL[:, NL - 1, cols], decay[:, n, 0:w], ALU.mult).then_inc(kL_ready, 1)

            def newton(h, u):
                V, w = 2 * h + u, WIDTH[u]
                pool.wait_ge(rooted, V + 1)
                nc.gpsimd.tensor_tensor(tmp[:, 0:w], root[:, 0:w], root[:, 0:w], ALU.mult).then_inc(multiplied, 1)
                pool.wait_ge(multiplied, 2 * V + 1)
                nc.gpsimd.tensor_tensor(tmp[:, 0:w], tmp[:, 0:w], var[:, 0:w], ALU.mult).then_inc(multiplied, 1)

            def refine(h, u):
                V, w = 2 * h + u, WIDTH[u]
                pool.wait_ge(factor_ready, V + 1)
                nc.gpsimd.tensor_tensor(root[:, 0:w], root[:, 0:w], tmp[:, 0:w], ALU.mult).then_inc(root_ready, 1)

            def gated(h, u):
                V = 2 * h + u
                pool.wait_ge(normed, V + 1)
                pool.wait_ge(gate_loaded[u], 16 * h + 16)
                nc.gpsimd.tensor_tensor(rec[:, COLS[u]], rec[:, COLS[u]], gate[:, COLS[u]], ALU.mult).then_inc(rec_ready, 1)

            def unit(h, u, after, before):
                for n in range(NL):
                    if after:
                        key_pass(*after, n)
                    if before and n == 1:
                        newton(*before)
                    if before and n == 4:
                        refine(*before)
                if before:
                    gated(*before)

            for n in range(NL):
                key_pass(0, 0, n)
            heads(pool, unit)
            newton(HG - 1, 1)
            refine(HG - 1, 1)
            gated(HG - 1, 1)

        @block.scalar
        def _(act):
            act.wait_ge(bound_step, 3)
            for n in range(2):
                nc.scalar.activation(lexp[:, n, :], lb_in[:, n, :], ACT.Exp).then_inc(bound_exp, 1)

            def logs(h, u):
                U = 2 * h + u
                act.wait_ge(k_loaded[u], 16 * h + 16)
                nc.scalar.activation(kL[:, NL - 1, COLS[u]], kL[:, NL - 1, COLS[u]], ACT.Copy,
                                     scale=omlb[:, DynSlice(h, 1)]).then_inc(k_ready, 1)
                act.wait_ge(f_ready, U + 1)
                nc.scalar.activation(f[:, COLS[u]], f[:, COLS[u]], ACT.Ln).then_inc(log_ready, 1)

            def total_decay(h, u):
                U = 2 * h + u
                act.wait_ge(G_ready, U + 1)
                wait(act, S_ready, TILES * (h - 1) + TILES // 2 * (u + 1))
                wait(act, q_in_ready, U - 1)
                if u == 1:
                    wait(act, new_scaled, h)
                nc.scalar.activation(eG[:, COLS[u]], G[:, COLS[u]], ACT.Exp).then_inc(eG_ready, 1)

            def decays(h, u, passes):
                U = 2 * h + u
                for n in passes:
                    act.wait_ge(dist_ready, NL * U + n + 1)
                    if n == 0:
                        e = decay[:, 0, 0:WIDTH[u]]
                        nc.scalar.activation(e, e, ACT.Exp, scale=-1.0).then_inc(decay_ready, 1)
                    else:
                        b = LEVELS[n - 1]
                        w = WIDTH[u] if b <= 2 else SEQ // 2
                        e = decay[:, n, 0:w].rearrange("p (n b) -> p n b", b=2 * b)
                        nc.scalar.activation(e[:, :, b:2 * b], e[:, :, b:2 * b], ACT.Exp)
                        nc.scalar.activation(e[:, :, 0:b], e[:, :, 0:b], ACT.Exp, scale=-1.0).then_inc(decay_ready, 1)

            def square(h, u):
                V, w = 2 * h + u, WIDTH[u]
                act.wait_ge(o_kept, chunks_through(h, u))
                wait(act, root_ready, V)
                nc.scalar.activation(sq[:, 0:w], oT[:, COLS[u]], ACT.Square).then_inc(squared, 1)

            def inverse_root(h, u):
                V, w = 2 * h + u, WIDTH[u]
                act.wait_ge(var_ready, V + 1)
                wait(act, normed, V)
                nc.scalar.activation(root[:, 0:w], var[:, 0:w], ACT.Ln).then_inc(logged, 1)
                act.wait_ge(logged, V + 1)
                nc.scalar.activation(root[:, 0:w], root[:, 0:w], ACT.Exp, scale=-0.5).then_inc(rooted, 1)

            def keep_kd(h, n):
                w = P if n < TILES else NS
                act.wait_ge(kd_turned, TT * h + n + 1)
                if n >= 2:
                    act.wait_ge(st_done, TILES * h + n - 1)
                else:
                    wait(act, st_done, TILES * h)
                    wait(act, new_done, h)
                nc.scalar.activation(kdT[0:w, n % 2, :], kd_ps[0:w, 0:P], ACT.Copy).then_inc(kdT_ready, 1)

            def keep_o(h, n):
                w = P if n < TILES else NS
                act.wait_ge(o_done, TT * h + n + 1)
                nc.scalar.activation(oT[:, tile(n)], o_ps[:, n % 2, 0:w], ACT.Copy).then_inc(o_kept, 1)

            def unit(h, u, after, before):
                if before:
                    square(*before)
                keep_kd(h, CHUNKS_OF[u][0])
                for j, n in enumerate(CHUNKS_OF[u]):
                    if n != CHUNKS_OF[u][-1]:
                        keep_kd(h, n + 1)
                    if j == 0:
                        wait(act, normed, 2 * h + u - 1)
                    keep_o(h, n)
                    if after and j == 0:
                        logs(*after)
                    if after and j == 1:
                        decays(*after, (0,))
                        total_decay(*after)
                    if before and j == 1:
                        inverse_root(*before)
                    if after and 1 <= j <= 3:
                        decays(*after, {1: (1, 2), 2: (3, 4, 5), 3: (6, 7)}[j])

            act.wait_ge(bound_ready, 2)
            logs(0, 0)
            decays(0, 0, (0,))
            total_decay(0, 0)
            decays(0, 0, range(1, NL))
            heads(act, unit)
            square(HG - 1, 1)
            inverse_root(HG - 1, 1)

        @block.vector
        def _(dve):
            dve.wait_ge(consts, 80)
            nc.vector.tensor_tensor(lmax[:, :], lb_in[:, 0, :], lb_in[:, 1, :], ALU.max).then_inc(bound_step, 1)
            dve.wait_ge(bound_step, 1)
            nc.vector.tensor_tensor(lb_in[:, 0, :], lb_in[:, 0, :], lmax[:, :], ALU.subtract).then_inc(bound_step, 1)
            nc.vector.tensor_tensor(lb_in[:, 1, :], lb_in[:, 1, :], lmax[:, :], ALU.subtract).then_inc(bound_step, 1)
            dve.wait_ge(bound_exp, 2)
            nc.vector.tensor_tensor(lsum[:, :], lexp[:, 0, :], lexp[:, 1, :], ALU.add).then_inc(bound_step, 1)
            dve.wait_ge(bound_step, 4)
            nc.vector.reciprocal(lmax[:, :], lsum[:, :]).then_inc(bound_step, 1)
            dve.wait_ge(bound_step, 5)
            nc.vector.tensor_tensor(lb[:, :], lexp[:, 0, :], lmax[:, :], ALU.mult).then_inc(bound_ready, 1)
            dve.wait_ge(bound_ready, 1)
            nc.vector.tensor_scalar(omlb[:, :], lb[:, :], -1.0, 1.0, ALU.mult, ALU.add).then_inc(bound_ready, 1)
            dve.wait_ge(bound_ready, 2)

            def forget(h, u):
                dve.wait_ge(f_loaded[u], 16 * h + 16)
                nc.vector.tensor_scalar(f[:, COLS[u]], f[:, COLS[u]], omlb[:, DynSlice(h, 1)], lb[:, DynSlice(h, 1)],
                                        ALU.mult, ALU.add).then_inc(f_ready, 1)

            def scan(h, u):
                U = 2 * h + u
                dve.wait_ge(log_ready, U + 1)
                wait(dve, eG_ready, U - 1)
                wait(dve, decay_ready, NL * (U - 1))
                nc.vector.tensor_tensor_scan(G[:, COLS[u]], reset[:, COLS[u]], f[:, COLS[u]], 0.0, ALU.mult, ALU.add
                                             ).then_inc(G_ready, 1)
                dve.wait_ge(q_loaded[u], 16 * h + 16)
                q = qL[:, NL - 1, COLS[u]]
                nc.vector.tensor_scalar(q, q, float(P) ** -0.5, None, ALU.mult).then_inc(q_ready, 1)
                dve.wait_ge(G_ready, U + 1)

            def distances(h, u, passes):
                U = 2 * h + u
                lo = COLS[u].start
                for n in passes:
                    wait(dve, kL_ready, NL * (U - 1) + n + 1)
                    if n:
                        wait(dve, qL_ready, (NL - 1) * (U - 1) + n)
                    if n == 0:
                        parts = [(lo, lo + SEQ // 2, P, P - 1)]
                        if u == 1:
                            parts.append((SEQ, T, DT, DT - 1))
                    else:
                        b = LEVELS[n - 1]
                        parts = [(lo, COLS[u].stop if b <= 2 else lo + SEQ // 2, 2 * b, b - 1)]
                    for a, z, b, at in parts:
                        g = G[:, a:z].rearrange("p (n b) -> p n b", b=b)
                        d = decay[:, n, a - lo:z - lo].rearrange("p (n b) -> p n b", b=b)
                        last = nc.vector.tensor_tensor(d, g, g[:, :, at:at + 1].broadcast_to([P, (z - a) // b, b]),
                                                       ALU.subtract)
                    last.then_inc(dist_ready, 1)

            def carried_queries(h, u):
                U = 2 * h + u
                dve.wait_ge(eG_ready, U + 1)
                dve.wait_ge(q_ready, U + 1)
                wait(dve, o_done, chunks_through(h - 1, u))
                nc.vector.tensor_tensor(q_in[:, COLS[u]], qL[:, NL - 1, COLS[u]], eG[:, COLS[u]], ALU.mult
                                        ).then_inc(q_in_ready, 1)

            def queries(h, u, passes):
                U = 2 * h + u
                for n in passes:
                    w = WIDTH[u] if LEVELS[n - 1] <= 2 else SEQ // 2
                    cols = slice(COLS[u].start, COLS[u].start + w)
                    dve.wait_ge(decay_ready, NL * U + n + 1)
                    nc.vector.tensor_tensor(qL[:, n - 1, cols], qL[:, NL - 1, cols], decay[:, n, 0:w], ALU.mult
                                            ).then_inc(qL_ready, 1)

            def chunk(h, n):
                w = P if n < TILES else NS
                lv = 0 if n < TILES else NL - 3
                dve.wait_ge(pairs_done, TT * h + n + 1)
                wait(dve, attn_done, TT * h + n)
                nc.vector.tensor_tensor(kept[0:w, lv:NL, 0:w], pairs[0:w, lv:NL, 0:w], masks[0:w, lv:NL, 0:w], ALU.mult
                                        ).then_inc(kept_done, 1)
                dve.wait_ge(kept_done, TT * h + n + 1)
                wait(dve, o_done, TT * h + max(n - 1, 0))
                nc.vector.tensor_reduce(attn[0:w, n % 2, 0:w], kept[0:w, lv:NL, 0:w].rearrange("p l t -> p t l"), AX.X,
                                        ALU.add).then_inc(attn_done, 1)
                if n < TILES:
                    dve.wait_ge(st_done, TILES * h + n + 1)
                    wait(dve, S_ready, TILES * h + n)
                    wait(dve, o_done, TT * h + n)
                    if n == 1:
                        wait(dve, S_stored, 16 * h)
                    if n:
                        nc.vector.scalar_tensor_tensor(S[:, n % 2, :], S[:, (n + 1) % 2, :], eG[:, n * P + P - 1:n * P + P],
                                                       st_ps[:, 0:P], ALU.mult, ALU.add).then_inc(S_ready, 1)
                    else:
                        nc.vector.tensor_copy(S[:, 0, :], st_ps[:, 0:P]).then_inc(S_ready, 1)

            def own_values(h):
                dve.wait_ge(hv_loaded[1], 32 * h + 32)
                wait(dve, new_done, h)
                nc.vector.tensor_tensor(own_v[:, :, :], hv[0:NS, TILES:TT, :].broadcast_to([NS, DB, P]),
                                        own[:, :].unsqueeze(2).broadcast_to([NS, DB, P]), ALU.mult).then_inc(own_ready, 1)
                dve.wait_ge(st_loaded, 16 * h + 16)
                wait(dve, new_stored, 16 * h)
                wait(dve, new_ready, h)
                ends = eG[:, SEQ:T].rearrange("p (b j) -> p b j", j=DT)[:, :, DT - 1:DT]
                nc.vector.tensor_tensor(new_st[:, :, :], st[:, :, :], ends.broadcast_to([P, DB, P]), ALU.mult
                                        ).then_inc(new_scaled, 1)

            def new_states(h):
                dve.wait_ge(new_scaled, h + 1)
                dve.wait_ge(new_done, h + 1)
                nc.vector.tensor_tensor(new_st[:, :, :], new_st[:, :, :], pairs[:, :, :], ALU.add).then_inc(new_ready, 1)

            def variance(h, u):
                V, w = 2 * h + u, WIDTH[u]
                dve.wait_ge(summed, V + 1)
                wait(dve, multiplied, 2 * V)
                if u == 0:
                    v, total = var[:, 0:w], sum_ps[:, 0, 0:w]
                else:
                    v, total = var[:, 0:w].rearrange("p (c t) -> p c t", c=2), sum_ps[:, :, 0:w // 2]
                nc.vector.tensor_scalar(v, total, 1.0 / P, EPS, ALU.mult, ALU.add).then_inc(var_ready, 1)

            def factor(h, u):
                V, w = 2 * h + u, WIDTH[u]
                dve.wait_ge(multiplied, 2 * V + 2)
                nc.vector.tensor_scalar(tmp[:, 0:w], tmp[:, 0:w], -0.5, 1.5, ALU.mult, ALU.add).then_inc(factor_ready, 1)

            def norm(h, u):
                V, w = 2 * h + u, WIDTH[u]
                dve.wait_ge(root_ready, V + 1)
                wait(dve, rec_stored[u], 16 * h)
                nc.vector.scalar_tensor_tensor(rec[:, COLS[u]], oT[:, COLS[u]], gain[:, 0:1], root[:, 0:w], ALU.mult,
                                               ALU.mult).then_inc(normed, 1)

            def unit(h, u, after, before):
                for j, n in enumerate(CHUNKS_OF[u]):
                    chunk(h, n)
                    if before and j == 1:
                        variance(*before)
                    if after and j == 0:
                        forget(*after)
                    if after and j == 1:
                        scan(*after)
                        distances(*after, (0, 1, 2))
                    if after and j == 2:
                        distances(*after, (3, 4, 5))
                        carried_queries(*after)
                        queries(*after, (1, 2))
                    if before and j == 2:
                        factor(*before)
                    if after and j == 3:
                        distances(*after, (6, 7))
                        queries(*after, range(3, NL))
                    if before and j == 3:
                        norm(*before)
                    if u == 1 and j == 1:
                        own_values(h)
                if u == 1:
                    new_states(h)

            forget(0, 0)
            scan(0, 0)
            distances(0, 0, range(NL))
            carried_queries(0, 0)
            queries(0, 0, range(1, NL))
            heads(dve, unit)
            variance(HG - 1, 1)
            factor(HG - 1, 1)
            norm(HG - 1, 1)

        @block.tensor
        def _(pe):
            def pair_products(h, n):
                w = P if n < TILES else NS
                lv = 0 if n < TILES else NL - 3
                wait(pe, kept_done, TT * h + n)
                if n == 0:
                    wait(pe, new_ready, h)
                for x in range(lv, NL):
                    last = nc.tensor.matmul(pairs[0:w, x, 0:w], kL[:, x, tile(n)], qL[:, x, tile(n)], start=True,
                                            stop=True)
                last.then_inc(pairs_done, 1)

            def turn(h, n):
                w = P if n < TILES else NS
                wait(pe, kdT_ready, TT * h + n)
                nc.tensor.transpose(kd_ps[0:w, 0:P], kd[:, tile(n)], ident[:, :]).then_inc(kd_turned, 1)

            def states(h, n):
                pe.wait_ge(kdT_ready, TT * h + n + 1)
                if n < TILES:
                    wait(pe, S_ready, TILES * h + n)
                    nc.tensor.matmul(st_ps[:, 0:P], kdT[:, n % 2, :], hv[:, n, :], start=True, stop=True
                                     ).then_inc(st_done, 1)
                else:
                    pe.wait_ge(kept_done, TT * h + TT)
                    pe.wait_ge(own_ready, h + 1)
                    for x in range(2):
                        last = nc.tensor.matmul(pairs[:, 4 * x:4 * x + 4, :].rearrange("p a b -> p (a b)"),
                                                kdT[0:NS, n % 2, :],
                                                own_v[:, 4 * x:4 * x + 4, :].rearrange("p a b -> p (a b)"),
                                                start=True, stop=True)
                    last.then_inc(new_done, 1)

            def outputs(h, n):
                w = P if n < TILES else NS
                pe.wait_ge(attn_done, TT * h + n + 1)
                wait(pe, o_kept, TT * h + max(n - 1, 0))
                o = o_ps[:, n % 2, :]
                last = nc.tensor.matmul(o[:, 0:w], hv[0:w, n, :], attn[0:w, n % 2, 0:w], start=True, stop=(n == 0))
                if 0 < n < TILES:
                    pe.wait_ge(S_ready, TILES * h + n)
                    last = nc.tensor.matmul(o[:, 0:w], S[:, (n + 1) % 2, :], q_in[:, tile(n)], start=False, stop=True)
                if n == TILES:
                    pe.wait_ge(st_loaded, 16 * h + 16)
                    for b in range(DB):
                        last = nc.tensor.matmul(o[:, DT * b:DT * (b + 1)], st[:, b, :],
                                                q_in[:, SEQ + DT * b:SEQ + DT * (b + 1)], start=False, stop=(b == DB - 1))
                last.then_inc(o_done, 1)

            def sums(h, u):
                V, w = 2 * h + u, WIDTH[u]
                pe.wait_ge(squared, V + 1)
                wait(pe, var_ready, V)
                for x in range(u + 1):
                    c = w // (u + 1)
                    last = nc.tensor.matmul(sum_ps[:, x, 0:c], ones[:, :], sq[:, x * c:(x + 1) * c], start=True, stop=True)
                last.then_inc(summed, 1)

            def unit(h, u, after, before):
                U = 2 * h + u
                pe.wait_ge(qL_ready, (NL - 1) * (U + 1))
                pe.wait_ge(kL_ready, NL * (U + 1))
                pe.wait_ge(q_in_ready, U + 1)
                pe.wait_ge(hv_loaded[u], 16 * (u + 1) * (h + 1))
                first, end = CHUNKS_OF[u][0], CHUNKS_OF[u][-1]
                pair_products(h, first)
                turn(h, first)
                states(h, first)
                for n in CHUNKS_OF[u]:
                    if n < end:
                        pair_products(h, n + 1)
                        turn(h, n + 1)
                    outputs(h, n)
                    if n < end:
                        states(h, n + 1)
                    if before and n == first:
                        sums(*before)

            heads(pe, unit)
            sums(HG - 1, 1)



def merge(nc, xT, mixed_d, feat_d, w_attn, w_hgrn, w_out):
    with Scope(nc, "merge") as s:
        bhi = s.sb("bhi", [P, 8, T], F32R)
        blo = s.sb("blo", [P, 8, T], F32R)
        mhi = s.sb("mhi", [P, KD, T], F32R)
        mlo = s.sb("mlo", [P, KD, T], F32R)
        raw = s.sb("raw", [P, 2, UNIT])
        whi = s.sb("whi", [P, 2, UNIT], F32R)
        wlo = s.sb("wlo", [P, 2, UNIT], F32R)
        branch = s.sb("branch", [P, 2, CH])
        gates = s.sb("gates", [P, 2, 2, CH])
        both = s.sb("both", [P, 2, CH])
        ps = s.ps("ps", [P, 2, 2, 512])
        out_ps = s.ps("out_ps", [P, 4, 512])
        w_loaded = [s.sem(f"w_loaded{n}") for n in range(2)]
        branch_in = [s.sem(f"branch_in{n}") for n in range(2)]
        gates_in = [s.sem(f"gates_in{n}") for n in range(2)]
        b_hi_done, b_lo_done = s.sem("b_hi_done"), s.sem("b_lo_done")
        w_hi_done, w_lo_done = s.sem("w_hi_done"), s.sem("w_lo_done")
        mult_done = s.sem("mult_done")
        ps_done, gated, summed, m_hi_done, m_lo_done = (s.sem("ps_done"), s.sem("gated"), s.sem("summed"),
                                                        s.sem("m_hi_done"), s.sem("m_lo_done"))
        out_done, out_added = s.sem("out_done"), s.sem("out_added")
        block = s.block()
        parts = [(b, c) for c in range(NCH) for b in range(8)]
        wa = w_attn.rearrange("(G g r d) n -> g d G r n", G=2, g=2, r=2)
        wr = w_hgrn.rearrange("(k p) n -> p k n", p=P)
        wo = w_out.rearrange("(k p) n -> p k n", p=P)

        def pairs(engine, body):
            body(0, 0, 0, True)
            with engine.Fori(1, 4) as i:
                body(0, i, i, False)
            with engine.Fori(0, 4) as i:
                body(1, i, i + 4, False)

        @block.sync
        def _(sp):
            for n, (b, c) in enumerate(parts):
                if n >= 2:
                    sp.wait_ge(b_lo_done, n - 1)
                sp.dma_start(branch[:, n % 2, :], mixed_d[b][:, c * CH:(c + 1) * CH]).then_inc(branch_in[n % 2], 16)

            def body(kind, i, pair, first):
                for u in range(2):
                    if kind == 0:
                        for c in range(NCH):
                            y = 3 * u + c
                            if not (first and y < 2):
                                sp.wait_ge(gated, 12 * pair + 2 * y - 2)
                            for m in range(2):
                                sp.dma_start(gates[:, y % 2, m, :],
                                             feat_d[DynSlice(16 + 8 * m + 2 * i + u, 1)][:, :, c * CH:(c + 1) * CH
                                                                                         ].rearrange("a p t -> (a p) t")
                                             ).then_inc(gates_in[y % 2], 16)

            body(0, 0, 0, True)
            with sp.Fori(1, 4) as i:
                body(0, i, i, False)

        @block.gpsimd
        def _(pool):
            def body(kind, i, pair, first):
                for u in range(2):
                    if not first:
                        pool.wait_ge(w_lo_done, 2 * pair + u - 1)
                    col = (2 * i + u) * P
                    if kind == 0:
                        halves = raw[:, u, :].rearrange("p (m k f) -> p m k f", m=2, k=4)
                        for g in range(2):
                            for G in range(2):
                                pool.dma_start(halves[g * HD:(g + 1) * HD, 0, 2 * G:2 * G + 2, :],
                                               wa[g][:, G, :, DynSlice(col, P)]).then_inc(w_loaded[u], 16)
                        pool.dma_start(halves[:, 1, :, :], wr[:, :, DynSlice(col, P)]).then_inc(w_loaded[u], 16)
                    else:
                        pool.dma_start(raw[:, u, :].rearrange("p (k f) -> p k f", k=KD), wo[:, :, DynSlice(col, P)]
                                       ).then_inc(w_loaded[u], 16)

            pairs(pool, body)

        @block.scalar
        def _(act):
            def hi(u):
                nc.scalar.activation(whi[:, u, :], raw[:, u, :], ACT.Copy).then_inc(w_hi_done, 1)

            for n, (b, c) in enumerate(parts):
                act.wait_ge(branch_in[n % 2], 16 * (n // 2) + 16)
                nc.scalar.activation(bhi[:, b, c * CH:(c + 1) * CH], branch[:, n % 2, :], ACT.Copy).then_inc(b_hi_done, 1)
                if n == 3:
                    for u in range(2):
                        act.wait_ge(w_loaded[u], 80)
                        hi(u)
            with act.Fori(1, 4) as i:
                for u in range(2):
                    act.wait_ge(w_loaded[u], 80 * i + 80)
                    act.wait_ge(ps_done, 6 * i + 3 * u - 3)
                    hi(u)
            for u in range(2):
                act.wait_ge(w_loaded[u], 16 + 320)
                act.wait_ge(ps_done, 24 - 3 * (1 - u))
                hi(u)
            with act.Fori(1, 4) as i:
                for u in range(2):
                    act.wait_ge(w_loaded[u], 16 * i + 16 + 320)
                    act.wait_ge(out_done, 6 * i + 3 * u - 3)
                    hi(u)

        @block.vector
        def _(dve):
            def lo(u, pair):
                dve.wait_ge(w_hi_done, 2 * pair + u + 1)
                nc.vector.tensor_tensor(wlo[:, u, :], raw[:, u, :], whi[:, u, :], ALU.subtract).then_inc(w_lo_done, 1)

            def gate(i, u, c, first):
                y = 3 * u + c
                e = 6 * i + y
                dve.wait_ge(ps_done, e + 1)
                dve.wait_ge(gates_in[y % 2], 32 * (3 * i + y // 2) + 32)
                for m in range(2):
                    g = gates[:, y % 2, m, :]
                    nc.vector.tensor_tensor(g, g, ps[:, y % 2, m, 0:CH], ALU.mult).then_inc(mult_done, 1)
                dve.wait_ge(mult_done, 2 * e + 2)
                nc.vector.tensor_tensor(both[:, y % 2, :], gates[:, y % 2, 0, :], gates[:, y % 2, 1, :], ALU.add
                                        ).then_inc(gated, 2)
                dve.wait_ge(gated, 2 * e + 2)
                hi = mhi[:, DynSlice(2 * i + u, 1), c * CH:(c + 1) * CH].rearrange("p a t -> p (a t)")
                lo_ = mlo[:, DynSlice(2 * i + u, 1), c * CH:(c + 1) * CH].rearrange("p a t -> p (a t)")
                nc.vector.tensor_copy(hi, both[:, y % 2, :]).then_inc(m_hi_done, 1)
                dve.wait_ge(m_hi_done, e + 1)
                nc.vector.tensor_tensor(lo_, both[:, y % 2, :], hi, ALU.subtract).then_inc(m_lo_done, 1)

            def add(i, u, c):
                y = 3 * u + c
                dve.wait_ge(out_done, 6 * i + y + 1)
                x = xT[:, DynSlice(2 * i + u, 1), c * CH:(c + 1) * CH].rearrange("p a t -> p (a t)")
                nc.vector.tensor_tensor(x, x, out_ps[:, y % 3, 0:CH], ALU.add).then_inc(out_added, 1)

            for n, (b, c) in enumerate(parts):
                cols = slice(c * CH, (c + 1) * CH)
                dve.wait_ge(b_hi_done, n + 1)
                nc.vector.tensor_tensor(blo[:, b, cols], branch[:, n % 2, :], bhi[:, b, cols], ALU.subtract
                                        ).then_inc(b_lo_done, 1)
                if n == 4:
                    lo(0, 0)
                    lo(1, 0)

            def gates_of(i, u, first=False):
                for c in range(NCH):
                    gate(i, u, c, first)

            with dve.Fori(0, 3) as i:
                for u in range(2):
                    gates_of(i, u)
                    lo(u, i + 1)
            gates_of(3, 0)
            lo(0, 4)
            gates_of(3, 1)
            lo(1, 4)
            with dve.Fori(0, 3) as i:
                for u in range(2):
                    for c in range(NCH):
                        add(i, u, c)
                    lo(u, i + 5)
            for u in range(2):
                for c in range(NCH):
                    add(3, u, c)

        @block.tensor
        def _(pe):
            def body(kind, i, pair, first):
                for u in range(2):
                    pe.wait_ge(w_lo_done, 2 * pair + u + 1)
                    for c in range(NCH):
                        y = 3 * u + c
                        cols = slice(c * CH, (c + 1) * CH)
                        if kind == 0:
                            if first and u == 0:
                                pe.wait_ge(b_lo_done, 8 * c + 8)
                            if not (first and y < 2):
                                pe.wait_ge(gated, 12 * i + 2 * y - 2)
                            for m in range(2):
                                for k in range(4):
                                    w = slice((4 * m + k) * P, (4 * m + k + 1) * P)
                                    last = split_product(nc, ps[:, y % 2, m, 0:CH], whi[:, u, w], wlo[:, u, w],
                                                         bhi[:, 4 * m + k, cols], blo[:, 4 * m + k, cols], k == 0, k == 3)
                            last.then_inc(ps_done, 1)
                        else:
                            if first or (u == 0):
                                pe.wait_ge(m_lo_done, 18 + c + 4)
                            if not (first and y < 3):
                                pe.wait_ge(out_added, 6 * i + y - 2)
                            for k in range(KD):
                                w = slice(k * P, (k + 1) * P)
                                last = split_product(nc, out_ps[:, y % 3, 0:CH], whi[:, u, w], wlo[:, u, w],
                                                     mhi[:, k, cols], mlo[:, k, cols], k == 0, k == KD - 1)
                            last.then_inc(out_done, 1)

            body(0, 0, 0, True)
            with pe.Fori(1, 4) as i:
                body(0, i, i, False)
            body(1, 0, 4, True)
            with pe.Fori(1, 4) as i:
                body(1, i, i + 4, False)

OUTS = [("y_prompt", (1, SEQ, D)), ("y_sample", (DB, DT, D)), ("k_prompt", (1, 1, SEQ, KV, HD)), ("v_prompt", (1, 1, SEQ, KV, HD)),
        ("idx_k_prompt", (1, 1, SEQ, HD)), ("hgrn_prompt", (1, 1, HG, P, P)), ("k_sample", (1, DB, DT, KV, HD)),
        ("v_sample", (1, DB, DT, KV, HD)), ("idx_k_sample", (1, DB, DT, HD)), ("hgrn_sample", (1, DB, HG, P, P))]


def build(nc, a, o):
    scratch = {name: nc.dram_tensor(f"scratch_{name}", shape, F32).ap()
               for name, shape in (("qT", (4, P, T)), ("kT", (2, P, T)), ("qiT", (4, P, T)), ("kiT", (1, P, T)),
                                   ("wi", (T, HEADS)), ("hv", (T, HG * P)), ("feat", (FEATS, P, T)), ("mixed", (8, P, T)))}
    rows = {n: o[n].rearrange("a b t h d -> (a b t) (h d)") for n in ("k_prompt", "v_prompt", "k_sample", "v_sample")}
    rows |= {n: o[n].rearrange("a b t d -> (a b t) d") for n in ("idx_k_prompt", "idx_k_sample")}
    cache_k, cache_v = (a[n][0].rearrange("n s h d -> n s (h d)") for n in ("cache_k", "cache_v"))
    with Scope(nc, "core") as s:
        xT = s.sb("xT", [P, KD, T])
        ident = s.sb("ident", [P, P])
        ones = s.sb("ones", [P, P])
        ident_in, ones_set = s.sem("ident_in"), s.sem("ones_set")
        with nc.Block() as block:
            @block.sync
            def _(sp):
                sp.dma_start(ident[:, :], a["t_ident"]).then_inc(ident_in, 16)
                sp.wait_ge(ident_in, 16)

            @block.vector
            def _(dve):
                nc.vector.memset(ones[:, :], 1.0).then_inc(ones_set, 1)

        load_and_turn(nc, a["x_prompt"], a["x_sample"], xT, ident)

        def feed_forward(n):
            with Scope(nc, f"half{n}") as half:
                hhi = half.sb("hhi", [P, KD, T], F32R)
                hlo = half.sb("hlo", [P, KD, T], F32R)
                normalise(nc, f"norm{n}", xT, a[f"ffn{n}_norm"], hhi, hlo, ones)
                swiglu(nc, f"ff{n}", xT, hhi, hlo, a[f"ffn{n}_w_gate"], a[f"ffn{n}_w_up"], a[f"ffn{n}_w_down"])

        feed_forward(1)
        with Scope(nc, "mix") as mix:
            masks = mix.sb("masks", [P, SLABS, SW], mybir.dt.bfloat16)
            with Scope(nc, "proj") as proj:
                hhi = proj.sb("hhi", [P, KD, T], F32R)
                hlo = proj.sb("hlo", [P, KD, T], F32R)
                normalise(nc, "normm", xT, a["mix_norm"], hhi, hlo, ones)
                token_projections(nc, hhi, hlo, a["w_in"], a["q_norm"], a["k_norm"], a["t_cos"], a["t_sin"], ident,
                                  scratch["qT"], scratch["kT"], scratch["qiT"], scratch["kiT"], scratch["wi"],
                                  scratch["hv"], rows["k_prompt"], rows["k_sample"], rows["v_prompt"], rows["v_sample"],
                                  rows["idx_k_prompt"], rows["idx_k_sample"])
                scores = proj.sb("scores", [P, SLABS, SW])
                index_scores(nc, scores, scratch["qiT"], scratch["kiT"], scratch["wi"], a["cache_idx_k"], a["page_table"],
                             a["t_same_token"], a["t_new_floor"], ident)
                select_keys_and_project(nc, scores, masks, hhi, hlo, a["w_in"], scratch["feat"])
            attention(nc, scratch["mixed"], masks, scratch["qT"], scratch["kT"], rows["v_prompt"], rows["v_sample"],
                      cache_k, cache_v, a["page_table"], a["t_causal"], a["t_own"], ident)
        recurrence(nc, scratch["mixed"], scratch["feat"], scratch["hv"], a["state_hgrn"][0].rearrange("b h k v -> h k b v"),
                   o["hgrn_prompt"].rearrange("a b h k v -> (a b h) k v"),
                   o["hgrn_sample"].rearrange("a b h k v -> h k (a b) v"), a["hg_lower_bound"], a["hg_norm"],
                   a["t_resets"], a["t_levels"], a["t_owner"], ident, ones)
        merge(nc, xT, scratch["mixed"], scratch["feat"], a["w_branch_attn"][0], a["w_branch_hgrn"][0], a["w_out"][0])
        feed_forward(2)
        turn_and_store(nc, xT, o["y_prompt"], o["y_sample"], ident)


GAINS = ('ffn1_norm', 'mix_norm', 'ffn2_norm')


def shape_tables():
    half = HD // 2
    inv = (10000.0 ** (-np.arange(half) * 2.0 / HD)).astype(np.float32)
    pos = np.concatenate([np.arange(SEQ), np.zeros(P - NS), SEQ + np.tile(np.arange(DT), DB)]).astype(np.float32)
    ang = pos[:, None] * inv[None, :]
    c, s = np.cos(ang), np.sin(ang)
    cos = np.concatenate([c, c], 1).reshape(TT, P, HD).transpose(1, 0, 2)
    sin = np.concatenate([-s, s], 1).reshape(TT, P, HD).transpose(1, 0, 2)
    row = np.arange(P)
    same = row[:, None] % NS == row[None, :] % NS
    causal = np.concatenate([np.zeros((P, P)), np.where(row[None, :] <= row[:, None], 0.0, MASKED)], 1)
    own = np.repeat(row[:, None, None] % NS // DT == np.arange(DB)[None, :, None], DT, 2)
    t = np.arange(T)
    start = np.where(t < SEQ, t % P == 0, (t - SEQ) % DT == 0)
    resets = np.broadcast_to(np.where(start, 0.0, 1.0)[None, :], (P, T))
    s_, t_ = row[:, None], row[None, :]
    levels = np.stack([(s_ // (2 * b) == t_ // (2 * b)) & (s_ % (2 * b) < b) & (t_ % (2 * b) >= b) for b in LEVELS]
                      + [s_ == t_], 1)
    return {"t_cos": cos, "t_sin": sin, "t_ident": np.eye(P),
            "t_causal": causal, "t_own": own,
            "t_resets": resets, "t_levels": levels, "t_owner": row[0:NS, None] // DT == np.arange(DB)[None, :],
            "t_same_token": same, "t_new_floor": np.where(np.arange(DT)[None] <= np.arange(P)[:, None] % DT, 0.0, FLOOR)}


def kernel(**inputs):
    import concourse.bacc as bacc
    from concourse.bass_utils import run_bass_kernel_spmd
    nc = bacc.Bacc("TRN2", target_bir_lowering=False, num_devices=1)
    arrays, a = {}, {}
    for name, v in inputs.items():
        v = np.ascontiguousarray(v)
        if name in GAINS:
            v = v.reshape(KD, P).T
        elif name == 'hg_lower_bound':
            v = v.reshape(2, HG, P).transpose(2, 0, 1)
        elif name == 'hg_norm':
            v = v.reshape(P, 1)
        v = np.ascontiguousarray(v)
        arrays[f"in_{name}"] = v
    for name, v in shape_tables().items():
        arrays[f"in_{name}"] = np.ascontiguousarray(v, dtype=np.float32)
    for name, v in arrays.items():
        a[name[3:]] = nc.dram_tensor(name, v.shape, mybir.dt.from_np(v.dtype), kind="ExternalInput").ap()
    o = {}
    for name, shape in OUTS:
        o[name] = nc.dram_tensor(f"out_{name}", shape, F32, kind="ExternalOutput").ap()
    build(nc, a, o)
    r = run_bass_kernel_spmd(nc, [arrays], core_ids=[0])
    return tuple(r.results[0][f"out_{name}"] for name, _ in OUTS)
```
